# Optimizing a Trainium2 kernel written in Bass

```python
import math
import jax, jax.numpy as jnp
from jax import lax
import numpy as np

D_MODEL = 1024
BATCH = 1
SEQ = 1024
DEPTH = 1

MEM_LEN = 256
EPS = 1e-6
NEG = -1e30
MAX_POS_OFFSET = 4096

MLA_HEADS = 4
MLA_NOPE = 64
MLA_ROPE = 32
MLA_V = 64
MLA_Q_RANK = 192
MLA_KV_RANK = 128
MLA_OUT = MLA_HEADS * MLA_V
ROPE_THETA = 10000.0

LRU_WIDTH = 512
LRU_BLOCKS = 8
LRU_BLOCK = LRU_WIDTH // LRU_BLOCKS
CONV_W = 4
LRU_C = 8.0

DIFF_HEADS = 4
DIFF_DK = 32
DIFF_DV = 2 * DIFF_DK
DIFF_QK = DIFF_HEADS * 2 * DIFF_DK
DIFF_OUT = DIFF_HEADS * DIFF_DV

MIX_WIDTH = MLA_OUT + LRU_WIDTH + DIFF_OUT

IN_SPLITS = (
    MLA_Q_RANK,
    MLA_Q_RANK + MLA_KV_RANK,
    MLA_Q_RANK + MLA_KV_RANK + MLA_ROPE,
    MLA_Q_RANK + MLA_KV_RANK + MLA_ROPE + LRU_WIDTH,
    MLA_Q_RANK + MLA_KV_RANK + MLA_ROPE + 2 * LRU_WIDTH,
    MLA_Q_RANK + MLA_KV_RANK + MLA_ROPE + 2 * LRU_WIDTH + DIFF_QK,
    MLA_Q_RANK + MLA_KV_RANK + MLA_ROPE + 2 * LRU_WIDTH + 2 * DIFF_QK,
)
IN_WIDTH = MLA_Q_RANK + MLA_KV_RANK + MLA_ROPE + 2 * LRU_WIDTH + 2 * DIFF_QK + DIFF_OUT

N_BUCKETS = 32
MAX_DIST = 128

CROSS_HEADS = 4
CROSS_DH = D_MODEL // CROSS_HEADS

PEER_HEADS = 8
PEER_NKEYS = 128
PEER_EXPERTS = PEER_NKEYS * PEER_NKEYS
PEER_TOPK = 16
PEER_DQ = 128

Q_BLOCK = 128
TOKEN_BLOCK = 128

kernel_name = 'hybrid_mla_rglru_diffattn_peer'

def rmsnorm(x, g):
    x32 = x.astype(jnp.float32)
    y = x32 * lax.rsqrt(jnp.mean(x32 * x32, axis=-1, keepdims=True) + EPS)
    return (y * g.astype(jnp.float32)).astype(x.dtype)

def rope(x, pos):
    r = x.shape[-1]
    inv = ROPE_THETA ** (-jnp.arange(0, r, 2, dtype=jnp.float32) / r)
    ang = pos.astype(jnp.float32)[..., None] * inv
    if x.ndim == 4:
        ang = ang[:, :, None, :]
    cos, sin = jnp.cos(ang), jnp.sin(ang)
    x32 = x.astype(jnp.float32)
    x1, x2 = x32[..., : r // 2], x32[..., r // 2:]
    return jnp.concatenate([x1 * cos - x2 * sin, x1 * sin + x2 * cos], axis=-1).astype(x.dtype)

def t5_bucket(rel):
    n = jnp.maximum(-rel, 0)
    max_exact = N_BUCKETS // 2
    large = max_exact + (jnp.log(jnp.maximum(n, 1).astype(jnp.float32) / max_exact)
                         / math.log(MAX_DIST / max_exact) * (N_BUCKETS - max_exact)).astype(jnp.int32)
    large = jnp.minimum(large, N_BUCKETS - 1)
    return jnp.where(n < max_exact, n, large)

def causal_depthwise_conv(x, w, b):
    s = x.shape[1]
    xp = jnp.pad(x, ((0, 0), (CONV_W - 1, 0), (0, 0)))
    y = b
    for k in range(CONV_W):
        y = y + xp[:, k:k + s] * w[k]
    return y

def _linear_combine(c1, c2):
    a1, b1 = c1
    a2, b2 = c2
    return a1 * a2, a2 * b1 + b2

def rg_lru_branch(x_in, gate_in, conv_w, conv_b, w_a, b_a, w_x, b_x, lam):
    b, s, _ = x_in.shape
    xc = causal_depthwise_conv(x_in, conv_w, conv_b)
    xb = xc.reshape(b, s, LRU_BLOCKS, LRU_BLOCK)
    r = jax.nn.sigmoid(jnp.einsum('bsgi,gij->bsgj', xb, w_a) + b_a).reshape(b, s, LRU_WIDTH)
    i = jax.nn.sigmoid(jnp.einsum('bsgi,gij->bsgj', xb, w_x) + b_x).reshape(b, s, LRU_WIDTH)
    log_a = -LRU_C * r.astype(jnp.float32) * jax.nn.softplus(-lam.astype(jnp.float32))
    a = jnp.exp(log_a)
    u = jnp.sqrt(-jnp.expm1(2.0 * log_a)) * (i * xc).astype(jnp.float32)
    _, h = lax.associative_scan(_linear_combine, (a, u), axis=1)
    return h.astype(x_in.dtype) * jax.nn.gelu(gate_in, approximate=False)

def causal_block_attention(q_nope, q_rope, k_nope, k_rope, v_mla, q_d, k_d, v_d, positions, rel_bias, lam):
    b, s = positions.shape
    n_blocks = s // Q_BLOCK
    k_idx = jnp.arange(s)
    mla_scale = 1.0 / math.sqrt(MLA_NOPE + MLA_ROPE)
    diff_scale = 1.0 / math.sqrt(DIFF_DK)

    def one_block(blk):
        start = blk * Q_BLOCK
        sl = lambda t: lax.dynamic_slice_in_dim(t, start, Q_BLOCK, axis=1)
        q_idx = start + jnp.arange(Q_BLOCK)
        mask = k_idx[None, :] <= q_idx[:, None]
        s1 = (jnp.einsum('bqhd,bkhd->bhqk', sl(q_nope), k_nope)
              + jnp.einsum('bqhr,bkr->bhqk', sl(q_rope), k_rope)).astype(jnp.float32) * mla_scale
        p1 = jax.nn.softmax(jnp.where(mask, s1, NEG), axis=-1).astype(v_mla.dtype)
        o_mla = jnp.einsum('bhqk,bkhd->bqhd', p1, v_mla)
        rel = positions[:, None, :] - sl(positions)[:, :, None]
        bias = jnp.moveaxis(rel_bias[t5_bucket(rel)], -1, 1).astype(jnp.float32)
        s2 = jnp.einsum('bqhcd,bkhcd->bhcqk', sl(q_d), k_d).astype(jnp.float32) * diff_scale + bias[:, :, None]
        p2 = jax.nn.softmax(jnp.where(mask, s2, NEG), axis=-1)
        w = (p2[:, :, 0] - lam * p2[:, :, 1]).astype(v_d.dtype)
        o_diff = jnp.einsum('bhqk,bkhd->bqhd', w, v_d)
        return o_mla, o_diff

    o_mla, o_diff = lax.map(one_block, jnp.arange(n_blocks))
    o_mla = jnp.moveaxis(o_mla, 0, 1).reshape(b, s, MLA_HEADS, MLA_V)
    o_diff = jnp.moveaxis(o_diff, 0, 1).reshape(b, s, DIFF_HEADS, DIFF_DV)
    return o_mla, o_diff

def hybrid_mixer(h, positions, rel_bias, layer_idx, w_in, q_norm, w_uq, kv_norm, w_ukv,
                 conv_w, conv_b, w_a, b_a, w_x, b_x, lru_lambda, diff_lambda, diff_norm,
                 out_norm_mla, out_norm_lru, w_out):
    b, s, _ = h.shape
    c_q, c_kv, k_r, x_lru, g_lru, q_d, k_d, v_d = jnp.split(h @ w_in, IN_SPLITS, axis=-1)
    q = (rmsnorm(c_q, q_norm) @ w_uq).reshape(b, s, MLA_HEADS, MLA_NOPE + MLA_ROPE)
    q_nope, q_rope = q[..., :MLA_NOPE], rope(q[..., MLA_NOPE:], positions)
    kv = (rmsnorm(c_kv, kv_norm) @ w_ukv).reshape(b, s, MLA_HEADS, MLA_NOPE + MLA_V)
    k_nope, v_mla = kv[..., :MLA_NOPE], kv[..., MLA_NOPE:]
    k_rope = rope(k_r, positions)
    q_d = q_d.reshape(b, s, DIFF_HEADS, 2, DIFF_DK)
    k_d = k_d.reshape(b, s, DIFF_HEADS, 2, DIFF_DK)
    v_d = v_d.reshape(b, s, DIFF_HEADS, DIFF_DV)
    lam_init = 0.8 - 0.6 * math.exp(-0.3 * layer_idx)
    dl = diff_lambda.astype(jnp.float32)
    lam = jnp.exp(jnp.sum(dl[0] * dl[1])) - jnp.exp(jnp.sum(dl[2] * dl[3])) + lam_init
    o_mla, o_diff = causal_block_attention(q_nope, q_rope, k_nope, k_rope, v_mla,
                                           q_d, k_d, v_d, positions, rel_bias, lam)
    o_diff = (rmsnorm(o_diff, diff_norm) * (1.0 - lam_init)).reshape(b, s, DIFF_OUT)
    o_mla = rmsnorm(o_mla.reshape(b, s, MLA_OUT), out_norm_mla)
    o_lru = rmsnorm(rg_lru_branch(x_lru, g_lru, conv_w, conv_b, w_a, b_a, w_x, b_x, lru_lambda), out_norm_lru)
    y = jnp.concatenate([o_mla, o_lru, o_diff], axis=-1)
    return y @ w_out

def memory_cross_attention(h, mem_n, w_cq, w_ckv, w_co):
    b, s, d = h.shape
    m = mem_n.shape[1]
    q = (h @ w_cq).reshape(b, s, CROSS_HEADS, CROSS_DH)
    k, v = jnp.split(mem_n @ w_ckv, 2, axis=-1)
    k = k.reshape(b, m, CROSS_HEADS, CROSS_DH)
    v = v.reshape(b, m, CROSS_HEADS, CROSS_DH)
    sc = jnp.einsum('bshd,bmhd->bhsm', q, k).astype(jnp.float32) * (1.0 / math.sqrt(CROSS_DH))
    p = jax.nn.softmax(sc, axis=-1).astype(v.dtype)
    o = jnp.einsum('bhsm,bmhd->bshd', p, v).reshape(b, s, d)
    return o @ w_co

def peer_ffn(h, w_q, keys, u, v):
    b, s, d = h.shape
    q = (h @ w_q).reshape(b, s, PEER_HEADS, 2, PEER_DQ // 2)
    sc = jnp.einsum('bshcd,cnd->bshcn', q, keys).astype(jnp.float32)
    top_s, top_i = lax.top_k(sc, PEER_TOPK)
    cand = top_s[..., 0, :, None] + top_s[..., 1, None, :]
    best_s, best_c = lax.top_k(cand.reshape(b, s, PEER_HEADS, PEER_TOPK * PEER_TOPK), PEER_TOPK)
    ia = best_c // PEER_TOPK
    ib = best_c % PEER_TOPK
    experts = (jnp.take_along_axis(top_i[..., 0, :], ia, axis=-1) * PEER_NKEYS
               + jnp.take_along_axis(top_i[..., 1, :], ib, axis=-1))
    g = jax.nn.softmax(best_s, axis=-1).astype(h.dtype)
    n_blk = (b * s) // TOKEN_BLOCK
    hb = h.reshape(n_blk, TOKEN_BLOCK, d)
    eb = experts.reshape(n_blk, TOKEN_BLOCK, PEER_HEADS, PEER_TOPK)
    gb = g.reshape(n_blk, TOKEN_BLOCK, PEER_HEADS, PEER_TOPK)

    def block(args):
        xt, et, gt = args
        act = jax.nn.gelu(jnp.einsum('td,thkd->thk', xt, u[et]), approximate=False)
        return jnp.einsum('thk,thkd->td', gt * act, v[et])

    y = lax.map(block, (hb, eb, gb))
    return y.reshape(b, s, d)

def setup_inputs(seed: int = 0) -> dict:
    key = jax.random.key(seed)
    ks = jax.random.split(key, 40)
    f32 = jnp.float32
    L, D = DEPTH, D_MODEL

    def nrm(i, shape, scale):
        return jax.random.normal(ks[i], shape, f32) * scale

    def gain(i, shape):
        return 1.0 + 0.02 * jax.random.normal(ks[i], shape, f32)

    x = nrm(0, (BATCH, SEQ, D), 1.0)
    mem = nrm(1, (BATCH, MEM_LEN, D), 1.0)
    offset = jax.random.randint(ks[2], (BATCH, 1), 0, MAX_POS_OFFSET, dtype=jnp.int32)
    positions = offset + jnp.arange(SEQ, dtype=jnp.int32)[None, :]
    rel_bias = nrm(3, (N_BUCKETS, DIFF_HEADS), 0.2)
    norm_mix = gain(4, (L, D))
    w_in = nrm(5, (L, D, IN_WIDTH), D ** -0.5)
    mla_q_norm = gain(6, (L, MLA_Q_RANK))
    mla_w_uq = nrm(7, (L, MLA_Q_RANK, MLA_HEADS * (MLA_NOPE + MLA_ROPE)), MLA_Q_RANK ** -0.5)
    mla_kv_norm = gain(8, (L, MLA_KV_RANK))
    mla_w_ukv = nrm(9, (L, MLA_KV_RANK, MLA_HEADS * (MLA_NOPE + MLA_V)), MLA_KV_RANK ** -0.5)
    lru_conv_w = nrm(10, (L, CONV_W, LRU_WIDTH), CONV_W ** -0.5)
    lru_conv_b = nrm(11, (L, LRU_WIDTH), 0.01)
    lru_w_a = nrm(12, (L, LRU_BLOCKS, LRU_BLOCK, LRU_BLOCK), LRU_BLOCK ** -0.5)
    lru_b_a = nrm(13, (L, LRU_BLOCKS, LRU_BLOCK), 0.01)
    lru_w_x = nrm(14, (L, LRU_BLOCKS, LRU_BLOCK, LRU_BLOCK), LRU_BLOCK ** -0.5)
    lru_b_x = nrm(15, (L, LRU_BLOCKS, LRU_BLOCK), 0.01)
    a_pow = jax.random.uniform(ks[16], (L, LRU_WIDTH), f32, 0.9, 0.999)
    a0 = a_pow ** (1.0 / LRU_C)
    lru_lambda = jnp.log(a0) - jnp.log1p(-a0)
    diff_lambda = nrm(17, (L, 4, DIFF_DK), 0.1)
    diff_norm = gain(18, (L, DIFF_DV))
    out_norm_mla = gain(19, (L, MLA_OUT))
    out_norm_lru = gain(20, (L, LRU_WIDTH))
    w_out = nrm(21, (L, MIX_WIDTH, D), MIX_WIDTH ** -0.5)
    norm_cross = gain(22, (L, D))
    norm_mem = gain(23, (L, D))
    w_cq = nrm(24, (L, D, D), D ** -0.5)
    w_ckv = nrm(25, (L, D, 2 * D), D ** -0.5)
    w_co = nrm(26, (L, D, D), D ** -0.5)
    norm_ffn = gain(27, (L, D))
    peer_w_q = nrm(28, (L, D, PEER_HEADS * PEER_DQ), D ** -0.5)
    peer_keys = nrm(29, (L, 2, PEER_NKEYS, PEER_DQ // 2), (PEER_DQ // 2) ** -0.5)
    peer_u = nrm(30, (L, PEER_EXPERTS, D), D ** -0.5)
    peer_v = nrm(31, (L, PEER_EXPERTS, D), PEER_HEADS ** -0.5)
    norm_final = gain(32, (D,))
    return {'x': x, 'mem': mem, 'positions': positions, 'rel_bias': rel_bias,
            'norm_mix': norm_mix, 'w_in': w_in,
            'mla_q_norm': mla_q_norm, 'mla_w_uq': mla_w_uq, 'mla_kv_norm': mla_kv_norm, 'mla_w_ukv': mla_w_ukv,
            'lru_conv_w': lru_conv_w, 'lru_conv_b': lru_conv_b, 'lru_w_a': lru_w_a, 'lru_b_a': lru_b_a,
            'lru_w_x': lru_w_x, 'lru_b_x': lru_b_x, 'lru_lambda': lru_lambda,
            'diff_lambda': diff_lambda, 'diff_norm': diff_norm,
            'out_norm_mla': out_norm_mla, 'out_norm_lru': out_norm_lru, 'w_out': w_out,
            'norm_cross': norm_cross, 'norm_mem': norm_mem, 'w_cq': w_cq, 'w_ckv': w_ckv, 'w_co': w_co,
            'norm_ffn': norm_ffn, 'peer_w_q': peer_w_q, 'peer_keys': peer_keys,
            'peer_u': peer_u, 'peer_v': peer_v, 'norm_final': norm_final}

def reference(x, mem, positions, rel_bias, norm_mix, w_in, mla_q_norm, mla_w_uq, mla_kv_norm, mla_w_ukv,
              lru_conv_w, lru_conv_b, lru_w_a, lru_b_a, lru_w_x, lru_b_x, lru_lambda,
              diff_lambda, diff_norm, out_norm_mla, out_norm_lru, w_out,
              norm_cross, norm_mem, w_cq, w_ckv, w_co,
              norm_ffn, peer_w_q, peer_keys, peer_u, peer_v, norm_final):
    for l in range(DEPTH):
        h = rmsnorm(x, norm_mix[l])
        x = x + hybrid_mixer(h, positions, rel_bias, l, w_in[l], mla_q_norm[l], mla_w_uq[l],
                             mla_kv_norm[l], mla_w_ukv[l], lru_conv_w[l], lru_conv_b[l],
                             lru_w_a[l], lru_b_a[l], lru_w_x[l], lru_b_x[l], lru_lambda[l],
                             diff_lambda[l], diff_norm[l], out_norm_mla[l], out_norm_lru[l], w_out[l])
        h = rmsnorm(x, norm_cross[l])
        x = x + memory_cross_attention(h, rmsnorm(mem, norm_mem[l]), w_cq[l], w_ckv[l], w_co[l])
        h = rmsnorm(x, norm_ffn[l])
        x = x + peer_ffn(h, peer_w_q[l], peer_keys[l], peer_u[l], peer_v[l])
    return rmsnorm(x, norm_final)


_drawn_inputs = setup_inputs


def setup_inputs(seed=0):
    import zlib

    import numpy as np

    out = dict(_drawn_inputs(seed))
    spreads = {}
    factors = {'mla_q_norm': 4.084,
     'mla_kv_norm': 2.921,
     'lru_b_a': 8.0,
     'lru_b_x': 8.0,
     'diff_lambda': 8.0,
     'diff_norm': 4.633,
     'out_norm_mla': 4.093,
     'out_norm_lru': 3.354,
     'norm_cross': 8.0,
     'norm_mem': 7.977,
     'norm_ffn': 24.568,
     'norm_final': 7.491}
    for name, (base, spread) in spreads.items():
        noise = np.random.default_rng([zlib.crc32(name.encode()), seed]).standard_normal(out[name].shape)
        drawn = base * np.exp(spread * noise) if base else spread * noise
        out[name] = __import__('jax').numpy.asarray(drawn.astype(out[name].dtype))
    for name, factor in factors.items():
        out[name] = (out[name] * factor).astype(out[name].dtype)
    return out
```

```python
import math
from contextlib import ExitStack

import concourse.bass as bass
import numpy as np
from concourse import mybir

F32 = mybir.dt.float32
I32 = mybir.dt.int32
U32 = mybir.dt.uint32
ALU = mybir.AluOpType
ACT = mybir.ActivationFunctionType
AX_X = mybir.AxisListType.X

P = 128
D = 1024
KT = D // P
SEQ = 1024
NB = SEQ // P
MEM = 256
MT = MEM // P
EPS = 1e-6
NEG = -1e30

MLA_H, NOPE, ROPE, MLA_V = 4, 64, 32, 64
Q_RANK, KV_RANK = 192, 128
MLA_SCALE = 1.0 / math.sqrt(NOPE + ROPE)
ROPE_THETA = 10000.0
LRU_W, LRU_G, CONV_W = 512, 64, 4
LT = LRU_W // P
DIFF_H, DK, DV = 4, 32, 64
DIFF_SCALE = 1.0 / math.sqrt(DK)
LAM_INIT = 0.8 - 0.6 * math.exp(-0.3 * 0)
CROSS_H = 4
CROSS_SCALE = 1.0 / math.sqrt(D // CROSS_H)
BUCKETS, MAX_DIST = 32, 128
HEADS, NKEYS, TOPK = 8, 128, 16
EXPERTS = HEADS * TOPK

HALF = 512
W_RING = 7
G_RING = 8
STEP = 8
STEPS = EXPERTS // STEP
IN_TILES = 17
MEM_SLICES = 4 * KT
BLOCK_SLICES = 2 * (IN_TILES + 4 * KT)
W_SHIFT = (-MEM_SLICES) % W_RING
BAND = 2 * SEQ - P

_COLS = [("mix", KT), ("cross", KT), ("mem", KT), ("ffn", KT), ("qn", 2), ("kvn", 1), ("yn", KT), ("conv_w", CONV_W * LT),
         ("conv_b", LT), ("gate_b", 2 * LT), ("lam", LT), ("freq", 1), ("sign", 1)]
COL, N_COLS = {}, 0
for _name, _n in _COLS:
    COL[_name] = N_COLS
    N_COLS += _n


def bucket_starts():
    exact = BUCKETS // 2
    out = [float(j) for j in range(1, exact + 1)]
    for j in range(1, BUCKETS - exact):
        out.append(float(math.ceil(exact * (MAX_DIST / exact) ** (j / (BUCKETS - exact)))))
    return out


TWO_PI_A = 6.28125
TWO_PI_B = float(np.float32(np.round((2 * math.pi - TWO_PI_A) * 2 ** 21) / 2 ** 21))
TWO_PI_C = 2 * math.pi - TWO_PI_A - TWO_PI_B
ROUND = 1.5 * 2.0 ** 23

PIECES = [
    ["norm_mix", "project_0", "project_1"],
    ["project_2", "project_3", "latents"],
    ["project_4", "mla_up", "conv"],
    ["gates", "recur"],
    ["mla_0", "mla_1"],
    ["mla_2", "mla_3"],
    ["diff_0"],
    ["diff_1"],
    ["diff_2"],
    ["diff_3", "join"],
    ["mix_out"],
    ["norm_cross", "cross_q", "cross_scores"],
    ["cross_mix", "cross_out"],
    ["norm_ffn", "peer_q", "peer_scores"],
    ["top_0", "top_1"],
    ["choose"],
]


def program(nc, x, wstream, columns, w_uq, w_ukv, w_gates, keys_t, ffn_gain, final_gain, mem, positions, pos_cols,
            rel_bias, diff_lambda, peer_u, peer_v, out):
    with ExitStack() as ctx:
        def sb(name, shape, dt=F32):
            return ctx.enter_context(nc.sbuf_tensor(name, shape, dt))

        def pb(name, cols):
            return ctx.enter_context(nc.psum_tensor(name, [P, cols], F32))

        def sem(name):
            return ctx.enter_context(nc.semaphore(name))

        rows = sb("rows", [P, 2 * G_RING, D])
        u_rows, v_rows = rows[:, 0:G_RING, :], rows[:, G_RING:2 * G_RING, :]
        w_ring = sb("w_ring", [P, W_RING, HALF])
        ident = sb("ident", [P, P])
        ones = sb("ones", [P, P])
        cols = sb("cols", [P, N_COLS])
        ffn_row = sb("ffn_row", [P, D])
        final_row = sb("final_row", [P, D])
        wuq = sb("wuq", [P, 2, MLA_H * P])
        wukv = sb("wukv", [P, 2, MLA_H * NOPE])
        wgate = sb("wgate", [P, 2, LT, P])
        keys = sb("keys", [P, 2 * NKEYS])
        mem_k = sb("mem_k", [P, KT, MEM])
        mem_v = sb("mem_v", [P, MT, D])
        k_mla = sb("k_mla", [NOPE + ROPE, MLA_H, SEQ])
        v_mla = sb("v_mla", [P, NB, MLA_H * MLA_V])
        k_diff = sb("k_diff", [P, 2, SEQ])
        v_diff = sb("v_diff", [P, NB, DIFF_H * DV])
        x_next = sb("x_next", [P, D])
        x_cur = sb("x_cur", [P, D])
        h_cur = sb("h_cur", [P, D])
        xs = sb("xs", [P, D])
        hT = sb("hT", [P, KT, P])
        e0 = sb("e0", [P, D])
        e1 = sb("e1", [P, D])
        pT = sb("pT", [P, KT, P])
        bias_t = sb("bias_t", [P, SEQ])
        feat_a = sb("feat_a", [P, KT * P])
        feat_b = sb("feat_b", [P, KT * P])
        conv_in = sb("conv_in", [P, LT, P + CONV_W - 1])
        rope_t = sb("rope_t", [NOPE + ROPE, 2, P])
        k_swap = sb("k_swap", [NOPE + ROPE, P])
        h_last = sb("h_last", [P, LT])
        small = sb("small", [P, 128])
        gates_c = sb("gates_c", [P, 3 * LT])
        lru_c = sb("lru_c", [P, 2 * LT])
        lam_t = sb("lam_t", [P, 8])
        pos_i = sb("pos_i", [P, NB], I32)
        pos_q = sb("pos_q", [P, NB])
        flag = sb("flag", [P, 1], I32)
        iota_i = sb("iota_i", [P, TOPK], I32)
        iota_f = sb("iota_f", [P, TOPK])
        ids_cur = sb("ids_cur", [P, EXPERTS], U32)
        g_cur = sb("g_cur", [P, EXPERTS])
        dots = sb("dots", [P, EXPERTS])
        acts = sb("acts", [P, EXPERTS])
        coef = sb("coef", [P, EXPERTS])
        diag = sb("diag", [P, 4, P])
        out_stat = sb("out_stat", [P, 8])

        latent = feat_a[:, 0:3 * P].rearrange("p (a t) -> p a t", a=3)
        latent_n = feat_a[:, 3 * P:6 * P].rearrange("p (a t) -> p a t", a=3)
        q_diff = feat_a[:, 6 * P:8 * P].rearrange("p (a t) -> p a t", a=2)
        q_mla = feat_b[:, 0:4 * P].rearrange("p (a t) -> p a t", a=4)
        gelu_g = feat_b[:, 4 * P:8 * P].rearrange("p (a t) -> p a t", a=4)
        feat_q = feat_a[:, :].rearrange("p (a t) -> p a t", a=KT)
        cross_oT = feat_b[:, :].rearrange("p (a t) -> p a t", a=KT)
        lru_x = e0[:, 0:512].rearrange("p (a t) -> p a t", a=LT)
        lru_a = e0[:, 512:1024].rearrange("p (a t) -> p a t", a=LT)
        lru_t = e1[:, 0:512].rearrange("p (a t) -> p a t", a=LT)
        lru_i = e1[:, 512:1024].rearrange("p (a t) -> p a t", a=LT)
        table = bias_t[:, 0:BUCKETS * DIFF_H]
        steps_t = bias_t[:, BUCKETS * DIFF_H:(2 * BUCKETS - 1) * DIFF_H]
        top_v = feat_b[:, 0:256].rearrange("p (a k) -> p a k", k=TOPK)
        top_i = feat_b[:, 256:512].bitcast(U32).rearrange("p (a k) -> p a k", k=TOPK)
        top_f = feat_b[:, 512:768].rearrange("p (a k) -> p a k", k=TOPK)
        best_v = feat_b[:, 768:896].rearrange("p (a k) -> p a k", k=TOPK)
        best_i = feat_b[:, 896:1024].bitcast(U32).rearrange("p (a k) -> p a k", k=TOPK)
        pick = pT[:, 0:4, :]
        pick_i = pT[:, 4:6, :].bitcast(U32)
        ids_next, g_next = pT[:, 6, :].bitcast(U32), pT[:, 7, :]
        mem_t = rows[:, 14:16, :].rearrange("p a (k m) -> p (a k) m", m=MEM)

        ps_sum = pb("ps_sum", D)
        ps_p = [pb("ps_p0", 512), pb("ps_p1", 512)]
        ps_s = pb("ps_s", D)
        ps_t = [pb("ps_t0", 512), pb("ps_t1", 512)]

        bias_d = nc.dram_tensor("bias_rows", (DIFF_H + 1, SEQ, SEQ), F32, kind="Internal").ap()
        rope_d = nc.dram_tensor("rope_rows", (2, ROPE, SEQ), F32, kind="Internal").ap()

        cols_in, rows_in, pos_in, mem_in = sem("cols_in"), sem("rows_in"), sem("pos_in"), sem("mem_in")
        consts_in = sem("consts_in")
        w_landed = [sem(f"w_landed{i}") for i in range(W_RING)]
        w_used = sem("w_used")
        consts_made = sem("consts_made")
        ones_made = sem("ones_made")
        dve_step, act_step, pool_step = sem("dve_step"), sem("act_step"), sem("pool_step")
        band_step, any_step, top_step = sem("band_step"), sem("any_step"), sem("top_step")
        pre = {n: sem("pre_" + n) for n in
               ("square", "xs", "turned", "memT", "k_out", "v_out", "abs", "exp", "lamsum",
                "lamexp", "rope_arg", "rope_done", "rope_stored", "band", "stored", "flag")}
        x_landed, rope_landed, x_stored = sem("x_landed"), sem("rope_landed"), sem("x_stored")
        bias_landed, bias_used = sem("bias_landed"), sem("bias_used")
        handed = sem("handed")
        squared, scaled, turned, hT_made = sem("squared"), sem("scaled"), sem("turned"), sem("hT_made")
        proj_out = [sem(f"proj_out{g}") for g in range(5)]
        lat_sq, lat_sum, lat_n = sem("lat_sq"), sem("lat_sum"), sem("lat_n")
        up_q, up_k, up_v, q_swap, q_nope, q_rope, k_rope, kv_out = (sem(n) for n in (
            "up_q", "up_k", "up_v", "q_swap", "q_nope", "q_rope", "k_rope", "kv_out"))
        conv_done, gate_ps, gate_out, decay_out, root_in, root_out = (sem(n) for n in (
            "conv_done", "gate_ps", "gate_out", "decay_out", "root_in", "root_out"))
        lru_sq, lru_sum, lru_done = sem("lru_sq"), sem("lru_sum"), sem("lru_done")
        s_ps, s_max, s_exp, w_done = sem("s_ps"), sem("s_max"), sem("s_exp"), sem("w_done")
        p_turned, pT_made, pv_ps, pv_out = sem("p_turned"), sem("pT_made"), sem("pv_ps"), sem("pv_out")
        y_made, y_turned, yT_made = sem("y_made"), sem("y_turned"), sem("yT_made")
        out_added = sem("out_added")
        q_out = sem("q_out")
        c_ps, c_max, c_exp, c_norm, c_turned, c_pT, co_ps, co_out = (sem(n) for n in (
            "c_ps", "c_max", "c_exp", "c_norm", "c_turned", "c_pT", "co_ps", "co_out"))
        k_ps, k_out = sem("key_ps"), sem("key_out")
        g_arg, g_exp, chosen = sem("g_arg"), sem("g_exp"), sem("chosen")
        x_handed, ids_handed = sem("x_handed"), sem("ids_handed")
        u_landed = [sem(f"u_landed{i}") for i in range(G_RING)]
        v_landed = [sem(f"v_landed{i}") for i in range(G_RING)]
        u_used, v_used = sem("u_used"), sem("v_used")
        acts_made, coef_made, diag_made = sem("acts_made"), sem("coef_made"), sem("diag_made")
        fin_sum, fin_sq, fin_made, fin_stored = sem("fin_sum"), sem("fin_sq"), sem("fin_made"), sem("fin_stored")

        class Steps:

            def __init__(self, semaphore):
                self.sem, self.origin, self.n = semaphore, 0, 0

            def start(self, origin):
                self.origin, self.n = origin, 0

            def note(self, ins):
                ins.then_inc(self.sem, 1)
                self.n += 1

            def settle(self, eng):
                eng.wait_ge(self.sem, self.origin + self.n)

            def run(self, eng, ins):
                self.note(ins)
                self.settle(eng)

        def ge(eng, semaphore, value):
            if isinstance(value, int) and value <= 0:
                return
            eng.wait_ge(semaphore, value)

        def bc(ap, shape):
            return ap.broadcast_to(shape)

        def col(name, i=0, n=1):
            return cols[:, COL[name] + i:COL[name] + i + n]

        def products(b, i):
            return b * BLOCK_SLICES + (MEM_SLICES + i)

        def run_pieces(front, b, pieces):
            for name in pieces:
                if name in front:
                    front[name](b)

        def counter(eng, name):
            reg = eng.alloc_register(name)
            eng.reg_mov(reg, 0)
            return reg

        def wait_more(eng, semaphore, waited, n):
            eng.wait_ge(semaphore, eng.snap(waited) + n)
            eng.reg_add(waited, waited, n)

        block = ctx.enter_context(nc.Block())

        @block.sync
        def _(sp):
            def load_w(i, n):
                slot = (i + W_SHIFT) % W_RING if isinstance(n, int) and n < MEM_SLICES else (i - MEM_SLICES) % W_RING
                ge(sp, w_used, n - W_RING + 1)
                sp.dma_start(w_ring[:, slot, :], wstream[i]).then_inc(w_landed[slot], 16)

            sp.dma_start(cols[:, :], columns).then_inc(cols_in, 16)
            for t in range(MT):
                sp.dma_start((e0, e1)[t][:, :], mem[t * P:(t + 1) * P, :]).then_inc(mem_in, 16)
            for i in range(W_RING):
                load_w(i, i)
            sp.dma_start(rows[:, 11, :].bitcast(I32), positions.partition_broadcast(P)).then_inc(pos_in, 16)
            sp.dma_start(pos_i[:, :], pos_cols).then_inc(pos_in, 16)
            sp.dma_start(table[:, :], rel_bias.partition_broadcast(P)).then_inc(rows_in, 16)
            sp.dma_start(rows[:, 10, 0:4 * DK], diff_lambda.partition_broadcast(P)).then_inc(rows_in, 16)
            sp.dma_start(wuq[:, :, :], w_uq).then_inc(consts_in, 16)
            sp.dma_start(wukv[:, :, :], w_ukv).then_inc(consts_in, 16)
            sp.dma_start(wgate[:, :, :, :], w_gates).then_inc(consts_in, 16)
            sp.dma_start(keys[:, :], keys_t).then_inc(consts_in, 16)
            sp.dma_start(ffn_row[:, :], ffn_gain.partition_broadcast(P)).then_inc(consts_in, 16)
            sp.dma_start(final_row[:, :], final_gain.partition_broadcast(P)).then_inc(consts_in, 16)
            for i in range(W_RING, MEM_SLICES):
                load_w(i, i)
            for c in range(2):
                sp.wait_ge(pre["rope_done"], c + 1)
                sp.dma_start(rope_d[c], (xs, hT[:, :, :].rearrange("p a b -> p (a b)"))[c][NOPE:NOPE + ROPE, :]).then_inc(pre["rope_stored"], 16)
            sp.wait_ge(pre["rope_stored"], 32)
            sp.wait_ge(pre["flag"], 1)
            jumps = sp.alloc_register("jumps_sp")
            sp.reg_load(jumps, flag[0:1, 0:1])
            with sp.If_eq(jumps, 0):
                for h in range(DIFF_H + 1):
                    sp.wait_ge(pre["band"], h + 1)
                    for b in range(NB):
                        at = SEQ - P - b * P
                        sp.dma_start(bias_d[h, b * P:(b + 1) * P, :],
                                     rows[:, 2 * h:2 * h + 2, :].rearrange("p a c -> p (a c)")[:, at:at + SEQ]).then_inc(pre["stored"], 16)
                sp.wait_ge(pre["stored"], 16 * NB * (DIFF_H + 1))
            with sp.Else():
                with sp.Fori(0, NB) as b:
                    for h in range(DIFF_H + 1):
                        sp.wait_ge(ones_made, 1)
                        ge(sp, pre["band"], b * (DIFF_H + 1) + h + 1)
                        sp.dma_start(bias_d[h, bass.ds(b * P, P), :], rows[:, h, :]).then_inc(pre["stored"], 16)
                sp.wait_ge(pre["stored"], 16 * NB * (DIFF_H + 1))
            sp.nop()

            def front_loads(b, c0, c1):
                for i in range(c0, c1):
                    load_w(MEM_SLICES + i, MEM_SLICES + b * BLOCK_SLICES + i)

            def load_bias(b, h):
                order = b * (DIFF_H + 1) + (h + 1) % (DIFF_H + 1)
                sp.wait_ge(ones_made, 1)
                ge(sp, bias_used, order)
                at = b * P
                sp.dma_start(bias_t[:, :], bias_d[h, bass.ds(at, P), :]).then_inc(bias_landed, 16)

            def load_x(b):
                sp.wait_ge(ones_made, 1)
                ge(sp, x_handed, b)
                sp.dma_start(x_next[:, :], x[bass.ds(b * P, P), :]).then_inc(x_landed, 16)
                sp.wait_ge(ones_made, 1)
                ge(sp, q_rope, b)
                ge(sp, k_rope, b)
                sp.dma_start(rope_t[NOPE:NOPE + ROPE, :, :],
                             rope_d[:, :, bass.ds(b * P, P)].rearrange("c r t -> r c t")).then_inc(rope_landed, 16)

            tile = 2
            w_at = {"project_0": (0, 3), "project_1": (3, 7), "project_2": (7, 11), "project_3": (11, 15),
                    "project_4": (15, 17), "mix_out": (17, 25), "cross_q": (25, 33), "cross_out": (33, 41),
                    "peer_q": (41, 49)}
            front = {n: (lambda b, r=r: front_loads(b, tile * r[0], tile * r[1])) for n, r in w_at.items()}
            front["norm_mix"] = load_x
            mask_first = front["project_3"]

            def project_3(b):
                mask_first(b)
                load_bias(b, DIFF_H)
            front["project_3"] = project_3
            for h in range(DIFF_H):
                front[f"diff_{h}"] = lambda b, h=h: load_bias(b, h)

            def store(b):
                sp.wait_ge(ones_made, 1)
                ge(sp, fin_made, b + 1)
                sp.dma_start(out[bass.ds(b * P, P), :], x_cur[:, :]).then_inc(fin_stored, 16)

            for pieces in PIECES:
                run_pieces(front, 0, pieces)
            with sp.Fori(1, NB) as b:
                for pieces in PIECES:
                    run_pieces(front, b, pieces)
                store(b - 1)
            store(NB - 1)
            sp.wait_ge(fin_stored, 16 * NB)

        @block.gpsimd
        def _(pool):
            pool.memset(ident[:, :], 0.0).then_inc(pool_step, 1)
            pool.iota(iota_i[:, :], [[1, TOPK]], base=0, channel_multiplier=0).then_inc(consts_made, 1)
            pool.iota(rows[:, 13, :].bitcast(I32), [[1, SEQ]], base=0, channel_multiplier=-1).then_inc(consts_made, 1)
            pool.wait_ge(pool_step, 1)
            pool.affine_select(out=ident[:, :], in_=ident[:, :], compare_op=ALU.not_equal, fill=1.0, base=0,
                               pattern=[[-1, P]], channel_multiplier=1).then_inc(consts_made, 1)
            for t in (k_mla, v_mla, k_diff, v_diff, conv_in, h_last):
                pool.memset(t[tuple(slice(None) for _ in t.shape)], 0.0).then_inc(consts_made, 1)

            u_waited, v_waited = counter(pool, "u_waited"), counter(pool, "v_waited")

            def gather_u(bp, j):
                wait_more(pool, u_used, u_waited, 1)
                pool.indirect_dma_start(u_rows[:, j % G_RING, :], None, peer_u,
                                        bass.IndirectOffsetOnAxis(ap=ids_cur[:, j:j + 1], axis=0)).then_inc(u_landed[j % G_RING], 16)

            def gather_v(bp, j):
                wait_more(pool, v_used, v_waited, 1)
                pool.indirect_dma_start(v_rows[:, j % G_RING, :], None, peer_v,
                                        bass.IndirectOffsetOnAxis(ap=ids_cur[:, j:j + 1], axis=0)).then_inc(v_landed[j % G_RING], 16)

            def retrieve(bp):
                pool.wait_ge(ids_handed, bp + 1)
                for s in range(STEPS + 1):
                    for k in range(STEP):
                        if s < STEPS:
                            gather_u(bp, s * STEP + k)
                        if s > 0:
                            gather_v(bp, (s - 1) * STEP + k)

            pool.wait_ge(pre["stored"], 16 * NB * (DIFF_H + 1))
            pool.wait_ge(pre["v_out"], 4)
            with pool.Fori(0, NB) as bp:
                retrieve(bp)

        @block.tensor
        def _(pe):
            def slice_in(i, uses):
                pe.wait_ge(w_landed[i], 16 * uses)

            def mem_slice(i):
                slot = (i + W_SHIFT) % W_RING
                before = sum(1 for j in range(i) if (j + W_SHIFT) % W_RING == slot)
                pe.wait_ge(w_landed[slot], 16 * (before + 1))
                return w_ring[:, slot, :]

            uses0 = [sum(1 for j in range(MEM_SLICES) if (j + W_SHIFT) % W_RING == s) for s in range(W_RING)]

            def block_slice(b, i):
                slot = i % W_RING
                pe.wait_ge(w_landed[slot], 16 * (BLOCK_SLICES // W_RING) * b + 16 * (uses0[slot] + i // W_RING + 1))
                return w_ring[:, slot, :]

            pe.wait_ge(consts_made, 3)
            for t in range(MT):
                pe.wait_ge(pre["xs"], t + 1)
                for g in range(2):
                    if t:
                        pe.wait_ge(pre["memT"], 2 * (t - 1) + g + 1)
                    for k in range(4):
                        ins = pe.transpose(ps_t[g][:, k * P:(k + 1) * P], (e0, e1)[t][:, (4 * g + k) * P:(4 * g + k + 1) * P], ident[:, :])
                    ins.then_inc(pre["turned"], 1)
            pe.wait_ge(pre["memT"], 2 * MT)
            for f in range(KT):
                if f >= 4 and f % 2 == 0:
                    pe.wait_ge(pre["k_out"], f // 2 - 1)
                for half in range(2):
                    w = mem_slice(2 * f + half).rearrange("p (k c) -> p k c", k=4)
                    for k in range(4):
                        kt = 4 * half + k
                        ins = pe.matmul(ps_p[(f // 2) % 2][:, (f % 2) * MEM:(f % 2 + 1) * MEM], w[:, k, :], mem_t[:, kt, :],
                                        start=(kt == 0), stop=(kt == KT - 1))
                    ins.then_inc(w_used, 1)
            for n in range(2):
                if n:
                    pe.wait_ge(pre["v_out"], 2)
                for kt in range(KT):
                    w = mem_slice(2 * KT + n * KT + kt)
                    for t in range(MT):
                        ins = pe.matmul(ps_s[:, t * 512:(t + 1) * 512], mem_t[:, kt, t * P:(t + 1) * P], w,
                                        start=(kt == 0), stop=(kt == KT - 1), skip_group_check=True)
                    ins.then_inc(w_used, 1)

            def turn_x(b, n):
                pe.wait_ge(scaled, 3 * b + n + 1)
                for g in range(2):
                    for k in range(4):
                        ins = pe.transpose(ps_t[g][:, k * P:(k + 1) * P], xs[:, (4 * g + k) * P:(4 * g + k + 1) * P], ident[:, :])
                    ins.then_inc(turned, 1)

            def col_tile(b, i, dst):
                for half in range(2):
                    w = block_slice(b, 2 * i + half).rearrange("p (k c) -> p k c", k=4)
                    for k in range(4):
                        kt = 4 * half + k
                        ins = pe.matmul(dst, w[:, k, :], hT[:, kt, :], start=(kt == 0), stop=(kt == KT - 1))
                    ins.then_inc(w_used, 1)

            def project(b, g, first, n):
                if g == 0:
                    pe.wait_ge(hT_made, 6 * b + 2)
                if g >= 2:
                    pe.wait_ge(proj_out[g - 2], b + 1)
                for i in range(n):
                    dst = ps_p[g % 2][:, i * P:(i + 1) * P]
                    if g < 4:
                        col_tile(b, first + i, dst)
                    else:
                        for half in range(2):
                            w = block_slice(b, 2 * (first + i) + half).rearrange("p (k c) -> p k c", k=4)
                            for k in range(4):
                                kt = 4 * half + k
                                ins = pe.matmul(dst, hT[:, kt, :], w[:, k, :], start=(kt == 0), stop=(kt == KT - 1))
                            ins.then_inc(w_used, 1)

            def latents(b):
                pe.wait_ge(lat_sq, b + 1)
                sq = pT
                pe.matmul(ps_t[0][:, 0:P], ones[:, :], sq[:, 0, :], start=True, stop=False)
                pe.matmul(ps_t[0][:, 0:P], ones[0:64, :], sq[0:64, 1, :], start=False, stop=True)
                pe.matmul(ps_t[0][:, P:2 * P], ones[:, :], sq[:, 2, :], start=True, stop=True).then_inc(lat_sum, 1)

            def mla_up(b):
                pe.wait_ge(lat_n, b + 1)
                pe.wait_ge(proj_out[3], b + 1)
                for h in range(MLA_H):
                    dst = ps_p[1][:, h * P:(h + 1) * P]
                    pe.matmul(dst, wuq[:, 0, h * P:(h + 1) * P], latent_n[:, 0, :], start=True, stop=False)
                    ins = pe.matmul(dst, wuq[0:64, 1, h * P:(h + 1) * P], latent_n[0:64, 1, :], start=False, stop=True)
                ins.then_inc(up_q, 1)
                pe.wait_ge(proj_out[4], b + 1)
                for h in range(MLA_H):
                    ins = pe.matmul(ps_p[0][0:NOPE, h * P:(h + 1) * P], wukv[:, 0, h * NOPE:(h + 1) * NOPE], latent_n[:, 2, :],
                                    start=True, stop=True)
                ins.then_inc(up_k, 1)
                pe.matmul(ps_t[1][:, 0:MLA_H * MLA_V], latent_n[:, 2, :], wukv[:, 1, :], start=True, stop=True).then_inc(up_v, 1)

            def gates(b):
                pe.wait_ge(conv_done, b + 1)
                pe.wait_ge(kv_out, 2 * b + 2)
                for a in range(2):
                    for i in range(LT):
                        ins = pe.matmul(ps_t[a][:, i * P:(i + 1) * P], wgate[:, a, i, :], lru_x[:, i, :], start=True, stop=True)
                    ins.then_inc(gate_ps, 1)

            def recur(b):
                pe.wait_ge(lru_sq, b + 1)
                for i in range(LT):
                    ins = pe.matmul(ps_t[0][:, 0:P], ones[:, :], lru_t[:, i, :], start=(i == 0), stop=(i == LT - 1))
                ins.then_inc(lru_sum, 1)

            def turn_p(src):
                for g in range(2):
                    for k in range(4):
                        ins = pe.transpose(ps_t[g][:, k * P:(k + 1) * P], src[:, (4 * g + k) * P:(4 * g + k + 1) * P], ident[:, :])
                    ins.then_inc(p_turned, 1)

            def mla(b, h):
                if h == 0:
                    pe.wait_ge(q_nope, b + 1)
                    pe.wait_ge(q_rope, b + 1)
                    pe.wait_ge(k_rope, b + 1)
                    pe.wait_ge(kv_out, 2 * b + 2)
                if h == 1:
                    pe.wait_ge(lru_done, b + 1)
                n = 12 * b + h
                ge(pe, s_max, n)
                for g in range(2):
                    ins = pe.matmul(ps_s[:, g * 512:(g + 1) * 512], q_mla[0:NOPE + ROPE, h, :], k_mla[:, h, g * 512:(g + 1) * 512],
                                    start=True, stop=True)
                ins.then_inc(s_ps, 1)
                pe.wait_ge(s_exp, n + 1)
                turn_p((e0, e1)[h % 2])
                m = 8 * b + h
                pe.wait_ge(pT_made, 2 * m + 2)
                for t in range(NB):
                    ins = pe.matmul(ps_p[0][:, h * MLA_V:(h + 1) * MLA_V], pT[:, t, :], v_mla[:, t, h * MLA_V:(h + 1) * MLA_V],
                                    start=(t == 0), stop=(t == NB - 1))
                ins.then_inc(pv_ps, 1)

            def diff(b, h):
                for c in range(2):
                    n = 12 * b + 4 + 2 * h + c
                    ge(pe, s_max, n)
                    r = 32 * ((2 * h + c) % 4)
                    for g in range(2):
                        ins = pe.matmul(ps_s[:, g * 512:(g + 1) * 512], q_diff[r:r + DK, (2 * h + c) // 4, :],
                                        k_diff[r:r + DK, (2 * h + c) // 4, g * 512:(g + 1) * 512], start=True, stop=True)
                    ins.then_inc(s_ps, 1)
                pe.wait_ge(w_done, 4 * b + h + 1)
                turn_p(e0)
                m = 8 * b + 4 + h
                pe.wait_ge(pT_made, 2 * m + 2)
                for t in range(NB):
                    ins = pe.matmul(ps_p[1][:, h * DV:(h + 1) * DV], pT[:, t, :], v_diff[:, t, h * DV:(h + 1) * DV],
                                    start=(t == 0), stop=(t == NB - 1))
                ins.then_inc(pv_ps, 1)

            def join(b):
                pe.wait_ge(y_made, b + 1)
                for k in range(2):
                    pe.transpose(ps_t[0][:, k * P:(k + 1) * P], xs[:, k * P:(k + 1) * P], ident[:, :])
                for k in range(2):
                    ins = pe.transpose(ps_t[0][:, (2 + k) * P:(3 + k) * P], xs[:, 512 + k * P:512 + (k + 1) * P], ident[:, :])
                ins.then_inc(y_turned, 1)

            def row_product(b, first, lhs):
                for n in range(2):
                    for kt in range(KT):
                        w = block_slice(b, first + n * KT + kt)
                        pe.matmul(ps_s[:, n * 512:(n + 1) * 512], lhs[:, kt, :], w, start=(kt == 0), stop=(kt == KT - 1)).then_inc(w_used, 1)

            def mix_out(b):
                pe.wait_ge(yT_made, b + 1)
                row_product(b, 34, hT)

            def queries(b, n, first):
                pe.wait_ge(hT_made, 6 * b + 4 + 2 * n)
                for f in range(KT):
                    col_tile(b, first + f, ps_p[f // 4][:, (f % 4) * P:(f % 4 + 1) * P])

            def cross_scores(b):
                pe.wait_ge(q_out, 4 * b + 2)
                pe.wait_ge(out_added, 4 * b + 2)
                for h in range(CROSS_H):
                    for j in range(2):
                        ins = pe.matmul(ps_s[:, h * MEM:(h + 1) * MEM], feat_q[:, 2 * h + j, :], mem_k[:, 2 * h + j, :],
                                        start=(j == 0), stop=(j == 1))
                ins.then_inc(c_ps, 1)

            def cross_mix(b):
                pe.wait_ge(c_norm, b + 1)
                for g in range(2):
                    for k in range(4):
                        ins = pe.transpose(ps_t[g][:, k * P:(k + 1) * P], e0[:, (4 * g + k) * P:(4 * g + k + 1) * P], ident[:, :])
                    ins.then_inc(c_turned, 1)
                pe.wait_ge(c_pT, 2 * b + 2)
                for f in range(KT):
                    for m in range(MT):
                        ins = pe.matmul(ps_p[f // 4][:, (f % 4) * P:(f % 4 + 1) * P], mem_v[:, m, f * P:(f + 1) * P],
                                        pT[:, 2 * (f // 2) + m, :], start=(m == 0), stop=(m == MT - 1))
                    if f % 4 == 3:
                        ins.then_inc(co_ps, 1)

            def cross_out(b):
                pe.wait_ge(co_out, 2 * b + 2)
                row_product(b, 66, cross_oT)

            def peer_scores(b):
                pe.wait_ge(q_out, 4 * b + 4)
                for g in range(2):
                    pe.wait_ge(out_added, 4 * b + 4)
                    if g:
                        pe.wait_ge(k_out, 2 * b + 1)
                    for h in range(4):
                        ins = pe.matmul(ps_s[:, h * 2 * NKEYS:(h + 1) * 2 * NKEYS], feat_q[:, 4 * g + h, :], keys[:, :],
                                        start=True, stop=True)
                    ins.then_inc(k_ps, 1)

            front = {
                "norm_mix": lambda b: turn_x(b, 0), "latents": latents, "mla_up": mla_up, "gates": gates, "recur": recur,
                "join": join, "mix_out": mix_out, "norm_cross": lambda b: turn_x(b, 1),
                "cross_q": lambda b: queries(b, 0, 25), "cross_scores": cross_scores, "cross_mix": cross_mix,
                "cross_out": cross_out, "norm_ffn": lambda b: turn_x(b, 2), "peer_q": lambda b: queries(b, 1, 41),
                "peer_scores": peer_scores,
            }
            for g, (first, n) in enumerate([(0, 3), (3, 4), (7, 4), (11, 4), (15, 2)]):
                front[f"project_{g}"] = lambda b, g=g, first=first, n=n: project(b, g, first, n)
            for h in range(4):
                front[f"mla_{h}"] = lambda b, h=h: mla(b, h)
                front[f"diff_{h}"] = lambda b, h=h: diff(b, h)

            def add_rows(bp, s):
                for k in range(STEP):
                    j = s * STEP + k
                    pe.wait_ge(diag_made, bp * EXPERTS + j + 1)
                    pe.wait_ge(v_landed[j % G_RING], bp * (16 * EXPERTS // G_RING) + 16 * (j // G_RING + 1))
                    if j == 0:
                        ge(pe, fin_sum, bp)
                    for n in range(2):
                        ins = pe.matmul(ps_sum[:, n * 512:(n + 1) * 512], diag[:, j % 4, :], v_rows[:, j % G_RING, n * 512:(n + 1) * 512],
                                        start=(j == 0), stop=(j == EXPERTS - 1), skip_group_check=True)
                    ins.then_inc(v_used, 1)

            pe.nop().then_inc(v_used, G_RING)
            pe.wait_ge(consts_in, 96)
            pe.wait_ge(ones_made, 1)
            for pieces in PIECES:
                run_pieces(front, 0, pieces)
            with pe.Fori(1, NB) as b:
                for s in range(STEPS + 1):
                    if s:
                        add_rows(b - 1, s - 1)
                    if s < STEPS:
                        run_pieces(front, b, PIECES[s])
            for s in range(STEPS):
                add_rows(NB - 1, s)

        @block.scalar
        def _(act):
            def copy(dst, src, scale=1.0):
                return act.activation(dst, src, ACT.Copy, scale=scale)

            for t in range(MT):
                act.wait_ge(mem_in, 16 * MT)
                act.activation(pT[:, :, :].rearrange("p a b -> p (a b)"), (e0, e1)[t][:, :], ACT.Square,
                               accum_out=small[:, t:t + 1]).then_inc(pre["square"], 1)
                act.wait_ge(pre["square"], t + 1)
            act.wait_ge(pre["abs"], 1)
            act.activation(small[:, 12:12 + LT], small[:, 8:8 + LT], ACT.Exp, scale=-1.0).then_inc(pre["exp"], 1)
            act.wait_ge(pre["lamsum"], 1)
            act.activation(lam_t[:, 2:4], lam_t[:, 0:2], ACT.Exp).then_inc(pre["lamexp"], 1)
            for c in range(2):
                act.wait_ge(pre["rope_arg"], c + 1)
                t = (xs[:, :], hT[:, :, :].rearrange("p a b -> p (a b)"))[c][NOPE:NOPE + ROPE, :]
                act.activation(t, t, ACT.Sin).then_inc(act_step, 1)
                act.wait_ge(act_step, c + 1)
                if c == 0:
                    act.nop().then_inc(pre["rope_done"], 1)
                else:
                    act.activation(t, t, ACT.Copy, scale=cols[NOPE:NOPE + ROPE, COL["sign"]:COL["sign"] + 1]).then_inc(pre["rope_done"], 1)
            for f in range(4):
                act.wait_ge(w_used, 4 * (f + 1))
                copy(mem_k[:, 2 * f:2 * f + 2, :].rearrange("p a b -> p (a b)"), ps_p[f % 2][:, :]).then_inc(pre["k_out"], 1)
            for n in range(2):
                act.wait_ge(w_used, 2 * KT + KT * (n + 1))
                for t in range(MT):
                    copy(mem_v[:, t, n * 512:(n + 1) * 512], ps_s[:, t * 512:(t + 1) * 512]).then_inc(pre["v_out"], 1)

            def square_x(b, n):
                if n == 0:
                    act.wait_ge(x_landed, 16 * b + 16)
                    ge(act, handed, b)
                else:
                    act.wait_ge(out_added, 4 * b + 2 * n)
                act.activation(xs[:, :], x_next[:, :], ACT.Square, accum_out=small[:, n:n + 1]).then_inc(squared, 1)

            def project_0(b):
                act.wait_ge(w_used, products(b, 6))
                copy(latent.rearrange("p a t -> p (a t)"), ps_p[0][:, 0:3 * P])
                copy(k_swap[NOPE:NOPE + ROPE, :], ps_p[0][96:128, P:2 * P]).then_inc(proj_out[0], 1)

            def project_1(b):
                act.wait_ge(w_used, products(b, 14))
                copy(q_diff.rearrange("p a t -> p (a t)"), ps_p[1][:, 0:2 * P], DIFF_SCALE)
                copy(k_diff[:, :, bass.ds(b * P, P)], ps_p[1][:, 2 * P:4 * P].rearrange("p (a t) -> p a t", a=2)).then_inc(proj_out[1], 1)

            def project_2(b):
                act.wait_ge(w_used, products(b, 22))
                copy(conv_in[:, :, CONV_W - 1:], ps_p[0][:, :].rearrange("p (a t) -> p a t", a=LT)).then_inc(proj_out[2], 1)

            def project_3(b):
                act.wait_ge(w_used, products(b, 30))
                act.activation(gelu_g.rearrange("p a t -> p (a t)"), ps_p[1][:, :], ACT.Gelu).then_inc(proj_out[3], 1)

            def project_4(b):
                act.wait_ge(w_used, products(b, 34))
                copy(v_diff[:, bass.ds(b, 1), :].rearrange("p a c -> p (a c)"), ps_p[0][:, 0:2 * P]).then_inc(proj_out[4], 1)

            def mla_up(b):
                act.wait_ge(up_q, b + 1)
                copy(e1[NOPE:NOPE + ROPE, 0:512], ps_p[1][96:128, :]).then_inc(q_swap, 1)
                copy(q_mla[0:NOPE, :, :].rearrange("p a t -> p (a t)"), ps_p[1][0:NOPE, :], MLA_SCALE).then_inc(q_nope, 1)
                act.wait_ge(up_k, b + 1)
                copy(k_mla[0:NOPE, :, bass.ds(b * P, P)], ps_p[0][0:NOPE, :].rearrange("p (a t) -> p a t", a=MLA_H)).then_inc(kv_out, 1)
                act.wait_ge(up_v, b + 1)
                copy(v_mla[:, bass.ds(b, 1), :].rearrange("p a c -> p (a c)"), ps_t[1][:, 0:MLA_H * MLA_V]).then_inc(kv_out, 1)

            def gates(b):
                act.wait_ge(q_rope, b + 1)
                for a, dst in ((0, lru_t), (1, lru_i)):
                    act.wait_ge(gate_ps, 2 * b + a + 1)
                    for i in range(LT):
                        ins = act.activation(dst[:, i, :], ps_t[a][:, i * P:(i + 1) * P], ACT.Tanh,
                                             bias=gates_c[:, a * LT + i:a * LT + i + 1], scale=0.5)
                    ins.then_inc(gate_out, 1)
                act.wait_ge(gate_out, 2 * b + 2)
                for i in range(LT):
                    act.activation(lru_a[:, i, :], lru_t[:, i, :], ACT.Exp, bias=lru_c[:, i:i + 1], scale=lru_c[:, i:i + 1])
                for i in range(LT):
                    ins = act.activation(lru_t[:, i, :], lru_t[:, i, :], ACT.Tanh, bias=lru_c[:, LT + i:LT + i + 1],
                                         scale=lru_c[:, LT + i:LT + i + 1])
                ins.then_inc(decay_out, 1)
                act.wait_ge(root_in, b + 1)
                act.activation(lru_t.rearrange("p a t -> p (a t)"), lru_t.rearrange("p a t -> p (a t)"), ACT.Sqrt).then_inc(root_out, 1)

            def exp_scores(b, n, buf):
                act.wait_ge(s_max, 12 * b + n + 1)
                act.activation(buf[:, :], buf[:, :], ACT.Exp, bias=small[:, 32 + n:33 + n],
                               accum_out=small[:, 48 + n:49 + n]).then_inc(s_exp, 1)

            def out_pT(b, m):
                act.wait_ge(p_turned, 16 * b + 2 * m + 1)
                copy(pT[:, 0:4, :].rearrange("p a t -> p (a t)"), ps_t[0][:, :]).then_inc(pT_made, 1)
                act.wait_ge(p_turned, 16 * b + 2 * m + 2)
                copy(pT[:, 4:8, :].rearrange("p a t -> p (a t)"), ps_t[1][:, :]).then_inc(pT_made, 1)

            def mla(b, h):
                exp_scores(b, h, (e0, e1)[h % 2])
                out_pT(b, h)

            def diff(b, h):
                exp_scores(b, 4 + 2 * h, e0)
                exp_scores(b, 5 + 2 * h, e1)
                out_pT(b, 4 + h)

            def queries(b, n):
                for g in range(2):
                    act.wait_ge(w_used, products(b, (50, 82)[n] + 8 * (g + 1)))
                    copy(feat_a[:, g * 512:(g + 1) * 512], ps_p[g][:, :], CROSS_SCALE if n == 0 else 1.0).then_inc(q_out, 1)

            def cross_scores(b):
                act.wait_ge(c_max, b + 1)
                for h in range(CROSS_H):
                    ins = act.activation(e0[:, h * MEM:(h + 1) * MEM], ps_s[:, h * MEM:(h + 1) * MEM], ACT.Exp,
                                         bias=small[:, 64 + h:65 + h], accum_out=small[:, 68 + h:69 + h])
                ins.then_inc(c_exp, 1)

            def cross_mix(b):
                for g in range(2):
                    act.wait_ge(c_turned, 2 * b + g + 1)
                    copy(pT[:, 4 * g:4 * g + 4, :].rearrange("p a t -> p (a t)"), ps_t[g][:, :]).then_inc(c_pT, 1)
                for g in range(2):
                    act.wait_ge(co_ps, 2 * b + g + 1)
                    copy(feat_b[:, g * 512:(g + 1) * 512], ps_p[g][:, :]).then_inc(co_out, 1)

            def peer_scores(b):
                for g in range(2):
                    act.wait_ge(k_ps, 2 * b + g + 1)
                    copy((e0, e1)[g][:, :], ps_s[:, :]).then_inc(k_out, 1)

            def choose(b):
                act.wait_ge(g_arg, b + 1)
                act.activation(g_next[:, :], g_next[:, :], ACT.Exp).then_inc(g_exp, 1)

            front = {
                "norm_mix": lambda b: square_x(b, 0), "project_0": project_0, "project_1": project_1, "project_2": project_2,
                "project_3": project_3, "project_4": project_4, "mla_up": mla_up, "gates": gates,
                "norm_cross": lambda b: square_x(b, 1), "cross_q": lambda b: queries(b, 0), "cross_scores": cross_scores,
                "cross_mix": cross_mix, "norm_ffn": lambda b: square_x(b, 2), "peer_q": lambda b: queries(b, 1),
                "peer_scores": peer_scores, "choose": choose,
            }
            for h in range(4):
                front[f"mla_{h}"] = lambda b, h=h: mla(b, h)
                front[f"diff_{h}"] = lambda b, h=h: diff(b, h)

            def activate(bp, s):
                act.wait_ge(u_used, bp * EXPERTS + (G_RING + (s + 1) * STEP))
                act.activation(acts[:, s * STEP:(s + 1) * STEP], dots[:, s * STEP:(s + 1) * STEP], ACT.Gelu).then_inc(acts_made, 1)

            def spread(bp, s):
                act.wait_ge(coef_made, bp * STEPS + s + 1)
                for k in range(STEP):
                    j = s * STEP + k
                    act.wait_ge(v_used, bp * EXPERTS + (j + G_RING - 3))
                    act.activation(diag[:, j % 4, :], ident[:, :], ACT.Copy, scale=coef[:, j:j + 1]).then_inc(diag_made, 1)

            def finish(bp):
                act.wait_ge(fin_sum, bp + 1)
                act.activation(h_cur[:, :], x_cur[:, :], ACT.Square, accum_out=out_stat[:, 0:1]).then_inc(fin_sq, 1)

            act.wait_ge(pre["rope_stored"], 32)
            for pieces in PIECES:
                run_pieces(front, 0, pieces)
            with act.Fori(1, NB) as b:
                for s in range(STEPS + 1):
                    if s > 0:
                        spread(b - 1, s - 1)
                    if s < STEPS:
                        run_pieces(front, b, PIECES[s])
                        activate(b - 1, s)
                finish(b - 1)
            for s in range(STEPS + 1):
                if s > 0:
                    spread(NB - 1, s - 1)
                if s < STEPS:
                    activate(NB - 1, s)
            finish(NB - 1)

        @block.vector
        def _(dve):
            steps = Steps(dve_step)
            scores_waited, keys_waited, top_waited = (counter(dve, n) for n in ("scores_waited", "keys_waited", "top_waited"))

            def run(ins):
                steps.run(dve, ins)

            def rsqrt(y, v, t):
                run(dve.tensor_scalar(t.bitcast(I32), v.bitcast(I32), 1, None, ALU.logical_shift_right))
                run(dve.tensor_scalar(y.bitcast(I32), t.bitcast(I32), -1.0, float(0x5F3759DF), ALU.mult, ALU.add))
                for _ in range(3):
                    run(dve.scalar_tensor_tensor(t, y, -0.5, y, ALU.mult, ALU.mult))
                    run(dve.tensor_tensor(t, t, v, ALU.mult))
                    run(dve.scalar_tensor_tensor(y, t, 1.5, y, ALU.add, ALU.mult))

            dve.memset(ones[:, :], 1.0).then_inc(ones_made, 1)
            dve.wait_ge(cols_in, 16)
            for t in range(MT):
                dve.wait_ge(pre["square"], t + 1)
                run(dve.tensor_scalar(small[:, 2:3], small[:, t:t + 1], 1.0 / D, EPS, ALU.mult, ALU.add))
                rsqrt(small[:, 3:4], small[:, 2:3], small[:, 4:5])
                dve.tensor_scalar((e0, e1)[t][:, :], (e0, e1)[t][:, :], small[:, 3:4], None, ALU.mult).then_inc(pre["xs"], 1)
                for g in range(2):
                    dve.wait_ge(pre["turned"], 2 * t + g + 1)
                    dve.tensor_tensor(mem_t[:, 4 * g:4 * g + 4, t * P:(t + 1) * P], ps_t[g][:, :].rearrange("p (a t) -> p a t", a=4),
                                      bc(col("mem", 4 * g, 4).unsqueeze(2), [P, 4, P]), ALU.mult).then_inc(pre["memT"], 1)
            run(dve.tensor_scalar(gates_c[:, 0:2 * LT], col("gate_b", 0, 2 * LT), 0.5, None, ALU.mult))
            lam4, neg4, e4, s4, q4, r4 = (small[:, 8 + LT * i:8 + LT * (i + 1)] for i in (0, 2, 1, 3, 4, 5))
            run(dve.tensor_scalar(neg4, col("lam", 0, LT), -1.0, None, ALU.mult))
            dve.tensor_tensor(lam4, col("lam", 0, LT), neg4, ALU.max).then_inc(pre["abs"], 1)
            dve.wait_ge(pre["exp"], 1)
            run(dve.tensor_scalar(s4, e4, 2.0, None, ALU.add))
            run(dve.reciprocal(q4, s4))
            run(dve.tensor_tensor(s4, e4, q4, ALU.mult))
            run(dve.tensor_tensor(q4, s4, s4, ALU.mult))
            run(dve.tensor_scalar(r4, q4, 1.0 / 17, 1.0 / 15, ALU.mult, ALU.add))
            for n in (13, 11, 9, 7, 5, 3, 1):
                run(dve.tensor_tensor(r4, r4, q4, ALU.mult))
                run(dve.tensor_scalar(r4, r4, 1.0 / n, None, ALU.add))
            run(dve.scalar_tensor_tensor(r4, r4, 2.0, s4, ALU.mult, ALU.mult))
            run(dve.scalar_tensor_tensor(r4, neg4, 0.0, r4, ALU.max, ALU.add))
            run(dve.tensor_scalar(lru_c[:, 0:LT], r4, -4.0, None, ALU.mult))
            run(dve.tensor_scalar(lru_c[:, LT:2 * LT], r4, 4.0, None, ALU.mult))
            dve.wait_ge(rows_in, 32)
            dl = rows[:, 10, 0:4 * DK]
            for i in range(2):
                ins = dve.tensor_tensor_reduce(rows[:, 10, 128 + 32 * i:160 + 32 * i], dl[:, 2 * i * DK:(2 * i + 1) * DK],
                                               dl[:, (2 * i + 1) * DK:(2 * i + 2) * DK], 1.0, 0.0, ALU.mult, ALU.add, lam_t[:, i:i + 1])
            ins.then_inc(pre["lamsum"], 1)
            dve.wait_ge(pre["lamexp"], 1)
            run(dve.tensor_tensor(lam_t[:, 4:5], lam_t[:, 3:4], lam_t[:, 2:3], ALU.subtract))
            run(dve.tensor_scalar(lam_t[:, 5:6], lam_t[:, 4:5], LAM_INIT, None, ALU.subtract))
            run(dve.tensor_tensor(steps_t[:, :], table[:, DIFF_H:], table[:, 0:(BUCKETS - 1) * DIFF_H], ALU.subtract))
            dve.wait_ge(pos_in, 32)
            pos_k = rows[:, 11, :]
            run(dve.tensor_copy(pos_q[:, :], pos_i[:, :]))
            run(dve.tensor_copy(rows[:, 12, :], pos_k.bitcast(I32)))
            pos_k = rows[:, 12, :]
            run(dve.tensor_tensor(rows[:, 11, 0:SEQ - 1], pos_k[:, 1:], pos_k[:, 0:SEQ - 1], ALU.subtract))
            run(dve.tensor_scalar(rows[:, 11, 0:SEQ - 1], rows[:, 11, 0:SEQ - 1], 1.0, None, ALU.not_equal))
            run(dve.tensor_reduce(small[:, 5:6], rows[:, 11, 0:SEQ - 1], AX_X, ALU.max))
            run(dve.tensor_copy(flag[:, :], small[:, 5:6]))
            dve.nop().then_inc(pre["flag"], 1)
            r = slice(NOPE, NOPE + ROPE)
            angle, turns = rows[r, 11, :], rows[r, 10, :]
            run(dve.tensor_scalar(angle, pos_k[r, :], cols[r, COL["freq"]:COL["freq"] + 1], None, ALU.mult))
            for c, t in enumerate((xs[r, :], hT[r, :, :].rearrange("p a b -> p (a b)"))):
                run(dve.tensor_scalar(turns, angle, 1.0 / (2 * math.pi), 0.25 if c == 0 else 0.0, ALU.mult, ALU.add))
                run(dve.tensor_scalar(turns, turns, ROUND, None, ALU.add))
                run(dve.tensor_scalar(turns, turns, ROUND, None, ALU.subtract))
                run(dve.scalar_tensor_tensor(t, turns, -TWO_PI_A, angle, ALU.mult, ALU.add))
                run(dve.scalar_tensor_tensor(t, turns, -TWO_PI_B, t, ALU.mult, ALU.add))
                run(dve.scalar_tensor_tensor(t, turns, -TWO_PI_C, t, ALU.mult, ALU.add))
                if c == 0:
                    run(dve.tensor_scalar(t, t, math.pi / 2, None, ALU.add))
                pi = float(np.nextafter(np.float32(math.pi), np.float32(0)))
                run(dve.tensor_scalar(t, t, pi, -pi, ALU.min, ALU.max))
                dve.nop().then_inc(pre["rope_arg"], 1)

            def bias_of(own, dist, mask, dst):
                for h in range(DIFF_H):
                    own.note(dve.tensor_scalar(dst[h], dist, 0.0, table[:, h:h + 1], ALU.mult, ALU.add))
                own.settle(dve)
                for j, start in enumerate(bucket_starts()):
                    own.run(dve, dve.tensor_scalar(mask, dist, start, None, ALU.is_ge))
                    for h in range(DIFF_H):
                        own.note(dve.scalar_tensor_tensor(dst[h], mask, steps_t[:, j * DIFF_H + h:j * DIFF_H + h + 1], dst[h],
                                                          ALU.mult, ALU.add))
                    own.settle(dve)

            jumps = dve.alloc_register("jumps_dve")
            dve.reg_load(jumps, flag[0:1, 0:1])
            dve.wait_ge(consts_made, 3)
            run(dve.tensor_copy(iota_f[:, :], iota_i[:, :]))
            ahead = rows[:, 15, :]
            dve.wait_ge(w_used, MEM_SLICES)
            run(dve.tensor_copy(ahead, rows[:, 13, :].bitcast(I32)))
            with dve.If_eq(jumps, 0):
                band_steps = Steps(band_step)
                band = [rows[:, 2 * h:2 * h + 2, :].rearrange("p a c -> p (a c)") for h in range(DIFF_H + 1)]
                near = SEQ - 2 * P
                dist, gap, mask = rows[:, 13, 0:256], rows[:, 13, 256:512], rows[:, 13, 512:768]
                band_steps.run(dve, dve.tensor_scalar(gap, ahead[:, 0:256], -1.0, float(P), ALU.mult, ALU.add))
                band_steps.run(dve, dve.tensor_scalar(dist, gap, 0.0, None, ALU.max))
                for h in range(DIFF_H + 1):
                    band_steps.run(dve, dve.memset(band[h][:, 0:BAND], NEG if h < DIFF_H else 0.0))
                    if h < DIFF_H:
                        last = (BUCKETS - 1) * DIFF_H + h
                        band_steps.run(dve, dve.tensor_scalar(band[h][:, 0:near], band[h][:, 0:near], 0.0, table[:, last:last + 1],
                                                              ALU.mult, ALU.add))
                band_steps.run(dve, dve.memset(band[DIFF_H][:, SEQ:BAND], NEG))
                bias_of(band_steps, dist, mask, [band[h][:, near:SEQ] for h in range(DIFF_H)])
                band_steps.run(dve, dve.tensor_scalar(mask, gap, 0.0, NEG, ALU.is_lt, ALU.mult))
                for h in range(DIFF_H + 1):
                    dve.tensor_tensor(band[h][:, near:SEQ], band[h][:, near:SEQ], mask, ALU.add).then_inc(pre["band"], 1)
            with dve.Else():
                dist, mask = rows[:, 5, :], rows[:, 6, :]
                tiles = [rows[:, h, :] for h in range(DIFF_H + 1)]
                first_ahead = small[:, 7:8]
                dve.memset(first_ahead, 0.0).then_inc(any_step, 1)
                dve.wait_ge(any_step, 1)
                per_row_block = 4 + DIFF_H + 5 * (BUCKETS - 1) + 2
                with dve.Fori(0, NB) as b:
                    any_steps = Steps(any_step)
                    any_steps.start(b * per_row_block + 1)
                    dve.wait_ge(pre["stored"], b * (16 * (DIFF_H + 1)))
                    any_steps.run(dve, dve.tensor_copy(small[:, 6:7], pos_q[:, bass.ds(b, 1)]))
                    any_steps.run(dve, dve.tensor_scalar(dist, pos_k, small[:, 6:7], -1.0, ALU.subtract, ALU.mult))
                    any_steps.run(dve, dve.tensor_scalar(dist, dist, 0.0, None, ALU.max))
                    any_steps.run(dve, dve.memset(tiles[DIFF_H], 0.0))
                    bias_of(any_steps, dist, mask, tiles[0:DIFF_H])
                    any_steps.run(dve, dve.tensor_scalar(mask, ahead, first_ahead, NEG, ALU.is_gt, ALU.mult))
                    any_steps.run(dve, dve.tensor_scalar(first_ahead, first_ahead, float(P), None, ALU.add))
                    for h in range(DIFF_H + 1):
                        dve.tensor_tensor(tiles[h], tiles[h], mask, ALU.add).then_inc(pre["band"], 1)
                    assert any_steps.n == per_row_block
            dve.nop()

            def norm(b, n, gain):
                dve.wait_ge(squared, 3 * b + n + 1)
                run(dve.tensor_scalar(small[:, 4:5], small[:, n:n + 1], 1.0 / D, EPS, ALU.mult, ALU.add))
                rsqrt(small[:, 5:6], small[:, 4:5], small[:, 6:7])
                dve.tensor_scalar(xs[:, :], x_next[:, :], small[:, 5:6], None, ALU.mult).then_inc(scaled, 1)
                for g in range(2):
                    dve.wait_ge(turned, 6 * b + 2 * n + g + 1)
                    dve.tensor_tensor(hT[:, 4 * g:4 * g + 4, :], ps_t[g][:, :].rearrange("p (a t) -> p a t", a=4),
                                      bc(col(gain, 4 * g, 4).unsqueeze(2), [P, 4, P]), ALU.mult).then_inc(hT_made, 1)

            def latents(b):
                dve.wait_ge(proj_out[0], b + 1)
                dve.tensor_tensor(pT[:, 0:3, :], latent, latent, ALU.mult).then_inc(lat_sq, 1)
                dve.wait_ge(lat_sum, b + 1)
                steps.note(dve.tensor_scalar(pT[:, 3, :], ps_t[0][:, 0:P], 1.0 / Q_RANK, EPS, ALU.mult, ALU.add))
                run(dve.tensor_scalar(pT[:, 4, :], ps_t[0][:, P:2 * P], 1.0 / KV_RANK, EPS, ALU.mult, ALU.add))
                flat = pT[:, :, :].rearrange("p a t -> p (a t)")
                rsqrt(flat[:, 5 * P:7 * P], flat[:, 3 * P:5 * P], flat[:, 0:2 * P])
                dve.scalar_tensor_tensor(latent_n[:, 0, :], latent[:, 0, :], col("qn", 0), pT[:, 5, :], ALU.mult, ALU.mult)
                dve.scalar_tensor_tensor(latent_n[0:64, 1, :], latent[0:64, 1, :], col("qn", 1)[0:64, :], pT[0:64, 5, :],
                                         ALU.mult, ALU.mult)
                dve.scalar_tensor_tensor(latent_n[:, 2, :], latent[:, 2, :], col("kvn"), pT[:, 6, :], ALU.mult, ALU.mult)\
                   .then_inc(lat_n, 1)

            def mla_up(b):
                rr = slice(NOPE, NOPE + ROPE)
                dve.wait_ge(rope_landed, 16 * b + 16)
                steps.note(dve.tensor_tensor(pT[rr, 3, :], latent[rr, 1, :], rope_t[rr, 0, :], ALU.mult))
                run(dve.tensor_tensor(pT[rr, 4, :], k_swap[rr, :], rope_t[rr, 1, :], ALU.mult))
                dve.tensor_tensor(k_mla[rr, :, bass.ds(b * P, P)], bc(pT[rr, 3:4, :], [ROPE, MLA_H, P]),
                                  bc(pT[rr, 4:5, :], [ROPE, MLA_H, P]), ALU.add).then_inc(k_rope, 1)
                cos, sin = (bc(rope_t[rr, c:c + 1, :], [ROPE, MLA_H, P]) for c in range(2))
                straight = e1[rr, 512:1024].rearrange("p (a t) -> p a t", a=MLA_H)
                swapped = e1[rr, 0:512].rearrange("p (a t) -> p a t", a=MLA_H)
                dve.wait_ge(up_q, b + 1)
                steps.note(dve.scalar_tensor_tensor(straight, ps_p[1][rr, :].rearrange("p (a t) -> p a t", a=MLA_H), MLA_SCALE, cos,
                                                    ALU.mult, ALU.mult))
                dve.wait_ge(q_swap, b + 1)
                run(dve.scalar_tensor_tensor(swapped, swapped, MLA_SCALE, sin, ALU.mult, ALU.mult))
                dve.tensor_tensor(q_mla[rr, :, :], straight, swapped, ALU.add).then_inc(q_rope, 1)

            def conv(b):
                dve.wait_ge(proj_out[2], b + 1)
                for i in range(LT):
                    steps.note(dve.tensor_scalar(lru_x[:, i, :], conv_in[:, i, 0:P], col("conv_w", i), col("conv_b", i),
                                                 ALU.mult, ALU.add))
                for k in range(1, CONV_W):
                    steps.settle(dve)
                    for i in range(LT):
                        steps.note(dve.scalar_tensor_tensor(lru_x[:, i, :], conv_in[:, i, k:k + P], col("conv_w", k * LT + i),
                                                            lru_x[:, i, :], ALU.mult, ALU.add))
                dve.tensor_copy(conv_in[:, :, 0:CONV_W - 1], conv_in[:, :, P:P + CONV_W - 1]).then_inc(conv_done, 1)

            def gates(b):
                dve.wait_ge(gate_out, 2 * b + 2)
                run(dve.scalar_tensor_tensor(lru_i, lru_i, 1.0, lru_x, ALU.add, ALU.mult))
                dve.wait_ge(decay_out, b + 1)
                run(dve.tensor_tensor(lru_x, lru_a, lru_a, ALU.mult))
                dve.scalar_tensor_tensor(lru_t, lru_x, 1.0, lru_t, ALU.add, ALU.mult).then_inc(root_in, 1)
                dve.wait_ge(root_out, b + 1)
                run(dve.scalar_tensor_tensor(lru_i, lru_i, 0.5, lru_t, ALU.mult, ALU.mult))
                for i in range(LT):
                    steps.note(dve.tensor_tensor_scan(lru_x[:, i, :], lru_a[:, i, :], lru_i[:, i, :], h_last[:, i:i + 1],
                                                      ALU.mult, ALU.add))
                steps.settle(dve)
                steps.note(dve.tensor_copy(h_last[:, :], lru_x[:, :, P - 1]))
                dve.wait_ge(proj_out[3], b + 1)
                run(dve.tensor_tensor(lru_i, lru_x, gelu_g, ALU.mult))
                dve.tensor_tensor(lru_t, lru_i, lru_i, ALU.mult).then_inc(lru_sq, 1)

            def recur(b):
                dve.wait_ge(lru_sum, b + 1)
                run(dve.tensor_scalar(lru_a[:, 0, :], ps_t[0][:, 0:P], 1.0 / LRU_W, EPS, ALU.mult, ALU.add))
                rsqrt(lru_a[:, 1, :], lru_a[:, 0, :], lru_a[:, 2, :])
                for i in range(LT):
                    ins = dve.scalar_tensor_tensor(hT[:, 2 + i, :], lru_i[:, i, :], col("yn", 2 + i), lru_a[:, 1, :], ALU.mult, ALU.mult)
                ins.then_inc(lru_done, 1)
                dve.wait_ge(lru_done, b + 1)

            def masked_max(b, n, buf):
                wait_more(dve, s_ps, scores_waited, 1)
                run(dve.tensor_tensor_reduce(buf[:, :], ps_s[:, :], bias_t[:, :], 1.0, -3.0e38, ALU.add, ALU.max,
                                             small[:, 16 + n:17 + n]))
                dve.tensor_scalar(small[:, 32 + n:33 + n], small[:, 16 + n:17 + n], -1.0, None, ALU.mult).then_inc(s_max, 1)

            def mla(b, h):
                if h == 0:
                    dve.wait_ge(bias_landed, 80 * b + 16)
                if h >= 2:
                    dve.wait_ge(p_turned, 16 * b + 2 * (h - 1))
                masked_max(b, h, (e0, e1)[h % 2])
                if h == MLA_H - 1:
                    dve.nop().then_inc(bias_used, 1)

            def diff(b, h):
                dve.wait_ge(bias_landed, 80 * b + 16 * (h + 2))
                dve.wait_ge(p_turned, 16 * b + 2 * (4 + h))
                masked_max(b, 4 + 2 * h, e0)
                masked_max(b, 5 + 2 * h, e1)
                dve.nop().then_inc(bias_used, 1)
                dve.wait_ge(s_exp, 12 * b + 6 + 2 * h)
                run(dve.reciprocal(small[:, 72:74], small[:, 52 + 2 * h:54 + 2 * h]))
                run(dve.tensor_scalar(small[:, 74:75], small[:, 73:74], lam_t[:, 5:6], None, ALU.mult))
                run(dve.tensor_scalar(e1[:, :], e1[:, :], small[:, 74:75], None, ALU.mult))
                dve.scalar_tensor_tensor(e0[:, :], e0[:, :], small[:, 72:73], e1[:, :], ALU.mult, ALU.add).then_inc(w_done, 1)

            def join(b):
                dve.wait_ge(pv_ps, 8 * b + 8)
                run(dve.reciprocal(small[:, 76:80], small[:, 48:52]))
                for h in range(MLA_H):
                    steps.note(dve.tensor_scalar(xs[:, h * MLA_V:(h + 1) * MLA_V], ps_p[0][:, h * MLA_V:(h + 1) * MLA_V],
                                                 small[:, 76 + h:77 + h], None, ALU.mult))
                run(dve.tensor_copy(xs[:, 512:768], ps_p[1][:, 0:256]))
                steps.note(dve.tensor_tensor_reduce(xs[:, 256:512], xs[:, 0:256], xs[:, 0:256], 1.0, 0.0, ALU.mult, ALU.add,
                                                    small[:, 84:85]))
                run(dve.tensor_tensor(xs[:, 768:1024], xs[:, 512:768], xs[:, 512:768], ALU.mult))
                run(dve.tensor_reduce(small[:, 85:89], xs[:, 768:1024].rearrange("p (h c) -> p h c", h=DIFF_H), AX_X, ALU.add))
                steps.note(dve.tensor_scalar(small[:, 90:91], small[:, 84:85], 1.0 / (MLA_H * MLA_V), EPS, ALU.mult, ALU.add))
                run(dve.tensor_scalar(small[:, 91:95], small[:, 85:89], 1.0 / DV, EPS, ALU.mult, ALU.add))
                rsqrt(small[:, 95:100], small[:, 90:95], small[:, 100:105])
                dve.tensor_scalar(xs[:, 0:256], xs[:, 0:256], small[:, 95:96], None, ALU.mult)
                o = xs[:, 512:768].rearrange("p (h c) -> p h c", h=DIFF_H)
                dve.tensor_tensor(o, o, bc(small[:, 96:100].unsqueeze(2), [P, DIFF_H, DV]), ALU.mult).then_inc(y_made, 1)
                dve.wait_ge(y_turned, b + 1)
                t = ps_t[0][:, :].rearrange("p (a t) -> p a t", a=4)
                dve.tensor_tensor(hT[:, 0:2, :], t[:, 0:2, :], bc(col("yn", 0, 2).unsqueeze(2), [P, 2, P]), ALU.mult)
                dve.scalar_tensor_tensor(hT[:, 6:8, :], t[:, 2:4, :], 1.0 - LAM_INIT, bc(col("yn", 6, 2).unsqueeze(2), [P, 2, P]),
                                         ALU.mult, ALU.mult).then_inc(yT_made, 1)

            def add_out(b, first):
                for n in range(2):
                    dve.wait_ge(w_used, products(b, first + KT * (n + 1)))
                    dve.tensor_tensor(x_next[:, n * 512:(n + 1) * 512], x_next[:, n * 512:(n + 1) * 512],
                                      ps_s[:, n * 512:(n + 1) * 512], ALU.add).then_inc(out_added, 1)

            def cross_scores(b):
                dve.wait_ge(c_ps, b + 1)
                run(dve.tensor_reduce(small[:, 60:64], ps_s[:, :].rearrange("p (h m) -> p h m", h=CROSS_H), AX_X, ALU.max))
                dve.tensor_scalar(small[:, 64:68], small[:, 60:64], -1.0, None, ALU.mult).then_inc(c_max, 1)

            def cross_mix(b):
                dve.wait_ge(c_exp, b + 1)
                run(dve.reciprocal(small[:, 80:84], small[:, 68:72]))
                for h in range(CROSS_H):
                    ins = dve.tensor_scalar(e0[:, h * MEM:(h + 1) * MEM], e0[:, h * MEM:(h + 1) * MEM], small[:, 80 + h:81 + h], None,
                                            ALU.mult)
                ins.then_inc(c_norm, 1)

            def top16(values, indices, sources):
                n = len(sources)
                for first in (0, 8):
                    for v, s in zip(values, sources):
                        dve.max(v[:, first:first + 8], s).then_inc(top_step, 1)
                    wait_more(dve, top_step, top_waited, n)
                    for v, i, s in zip(values, indices, sources):
                        dve.max_index(i[:, first:first + 8], v[:, first:first + 8], s).then_inc(top_step, 1)
                        if first == 0:
                            dve.match_replace(s, v[:, 0:8], s, -3.0e38).then_inc(top_step, 1)
                    wait_more(dve, top_step, top_waited, 2 * n if first == 0 else n)

            def top(b, g):
                wait_more(dve, k_out, keys_waited, 1)
                at = range(8 * g, 8 * g + 8)
                top16([top_v[:, a, :] for a in at], [top_i[:, a, :] for a in at],
                      [(e0, e1)[g][:, k * NKEYS:(k + 1) * NKEYS] for k in range(8)])

            def choose(b):
                halves = [e[:, :].rearrange("p (h i j) -> p h i j", h=4, i=TOPK) for e in (e0, e1)]
                wide = [P, 4, TOPK, TOPK]
                tv = top_v[:, :, :].rearrange("p (h c) k -> p h c k", c=2)
                run(dve.tensor_copy(top_f[:, :, :], top_i[:, :, :]))
                tf = top_f[:, :, :].rearrange("p (h c) k -> p h c k", c=2)
                for g in range(2):
                    hs = slice(4 * g, 4 * g + 4)
                    dve.tensor_tensor(halves[g], bc(tv[:, hs, 0, :].unsqueeze(3), wide), bc(tv[:, hs, 1, :].unsqueeze(2), wide),
                                      ALU.add).then_inc(top_step, 1)
                wait_more(dve, top_step, top_waited, 2)
                top16([best_v[:, h, :] for h in range(HEADS)], [best_i[:, h, :] for h in range(HEADS)],
                      [(e0, e1)[h // 4][:, (h % 4) * 256:(h % 4 + 1) * 256] for h in range(HEADS)])
                g3 = g_next[:, :].rearrange("p (h k) -> p h k", h=HEADS)
                dve.tensor_tensor(g3, best_v[:, :, :], bc(best_v[:, :, 0:1], [P, HEADS, TOPK]), ALU.subtract).then_inc(g_arg, 1)
                flat_i = best_i[:, :, :].rearrange("p h k -> p (h k)")
                steps.note(dve.tensor_scalar(pick_i[:, 0, :], flat_i, 4, None, ALU.logical_shift_right))
                run(dve.tensor_scalar(pick_i[:, 1, :], flat_i, TOPK - 1, None, ALU.bitwise_and))
                run(dve.tensor_copy(pick[:, 0:2, :], pick_i[:, :, :]))
                for c in range(2):
                    place = pick[:, c, :].rearrange("p (h k) -> p h k", h=HEADS)
                    found = pick[:, 2 + c, :].rearrange("p (h k) -> p h k", h=HEADS)
                    for g in range(2):
                        hs = slice(4 * g, 4 * g + 4)
                        steps.note(dve.tensor_tensor(halves[g], bc(place[:, hs, :].unsqueeze(3), wide),
                                                     bc(iota_f[:, :].unsqueeze(1).unsqueeze(1), wide), ALU.is_equal))
                    steps.settle(dve)
                    for g in range(2):
                        hs = slice(4 * g, 4 * g + 4)
                        steps.note(dve.tensor_tensor(halves[g], halves[g], bc(tf[:, hs, c, :].unsqueeze(2), wide), ALU.mult))
                    steps.settle(dve)
                    for g in range(2):
                        hs = slice(4 * g, 4 * g + 4)
                        steps.note(dve.tensor_reduce(found[:, hs, :], halves[g], AX_X, ALU.add))
                    steps.settle(dve)
                run(dve.scalar_tensor_tensor(ids_next[:, :], pick[:, 2, :], float(NKEYS), pick[:, 3, :], ALU.mult, ALU.add))
                dve.wait_ge(g_exp, b + 1)
                run(dve.tensor_reduce(small[:, 106:106 + HEADS], g3, AX_X, ALU.add))
                run(dve.reciprocal(small[:, 114:114 + HEADS], small[:, 106:106 + HEADS]))
                run(dve.tensor_tensor(g3, g3, bc(small[:, 114:114 + HEADS].unsqueeze(2), [P, HEADS, TOPK]), ALU.mult))

            def hand_over(b):
                dve.wait_ge(u_used, b * EXPERTS + G_RING)
                dve.wait_ge(v_used, b * EXPERTS + G_RING)
                dve.tensor_copy(ids_cur[:, :], ids_next[:, :]).then_inc(ids_handed, 1)
                steps.note(dve.tensor_copy(g_cur[:, :], g_next[:, :]))
                ge(dve, fin_sq, b)
                dve.tensor_tensor(h_cur[:, :], xs[:, :], ffn_row[:, :], ALU.mult).then_inc(handed, 1)
                ge(dve, fin_stored, 16 * b)
                dve.tensor_copy(x_cur[:, :], x_next[:, :]).then_inc(x_handed, 1)
                dve.wait_ge(x_handed, b + 1)
                dve.wait_ge(handed, b + 1)
                steps.settle(dve)

            front = {
                "norm_mix": lambda b: norm(b, 0, "mix"), "latents": latents, "mla_up": mla_up, "conv": conv, "gates": gates,
                "recur": recur, "join": join, "mix_out": lambda b: add_out(b, 34), "norm_cross": lambda b: norm(b, 1, "cross"),
                "cross_scores": cross_scores, "cross_mix": cross_mix, "cross_out": lambda b: add_out(b, 66),
                "norm_ffn": lambda b: norm(b, 2, "ffn"), "top_0": lambda b: top(b, 0), "top_1": lambda b: top(b, 1),
                "choose": choose,
            }
            for h in range(4):
                front[f"mla_{h}"] = lambda b, h=h: mla(b, h)
                front[f"diff_{h}"] = lambda b, h=h: diff(b, h)

            def multiply_rows(bp, s, k0, k1):
                for k in range(k0, k1):
                    j = s * STEP + k
                    dve.wait_ge(u_landed[j % G_RING], bp * (16 * EXPERTS // G_RING) + 16 * (j // G_RING + 1))
                    row = u_rows[:, j % G_RING, :]
                    dve.tensor_tensor_reduce(row, row, h_cur[:, :], 1.0, 0.0, ALU.mult, ALU.add, dots[:, j:j + 1]).then_inc(u_used, 1)

            def weigh(bp, s):
                dve.wait_ge(acts_made, bp * STEPS + s + 1)
                a = slice(s * STEP, (s + 1) * STEP)
                dve.tensor_tensor(coef[:, a], g_cur[:, a], acts[:, a], ALU.mult).then_inc(coef_made, 1)

            def retrieval_step(bp, s):
                if s < STEPS:
                    multiply_rows(bp, s, 0, 2)
                if s > 0:
                    weigh(bp, s - 1)
                if s < STEPS:
                    multiply_rows(bp, s, 2, STEP)

            def finish(bp):
                dve.wait_ge(v_used, bp * EXPERTS + (EXPERTS + G_RING))
                dve.tensor_tensor(x_cur[:, :], x_cur[:, :], ps_sum[:, :], ALU.add).then_inc(fin_sum, 1)
                dve.wait_ge(fin_sq, bp + 1)
                run(dve.tensor_scalar(out_stat[:, 1:2], out_stat[:, 0:1], 1.0 / D, EPS, ALU.mult, ALU.add))
                rsqrt(out_stat[:, 2:3], out_stat[:, 1:2], out_stat[:, 3:4])
                dve.scalar_tensor_tensor(x_cur[:, :], x_cur[:, :], out_stat[:, 2:3], final_row[:, :], ALU.mult, ALU.mult)\
                   .then_inc(fin_made, 1)

            dve.wait_ge(pre["rope_stored"], 32)
            dve.wait_ge(consts_in, 96)
            dve.wait_ge(consts_made, 9)
            dve.nop().then_inc(u_used, G_RING)
            prologue_steps = steps.n
            for pieces in PIECES:
                run_pieces(front, 0, pieces)
            hand_over(0)
            first_steps = steps.n - prologue_steps
            finish_steps = 12
            with dve.Fori(1, NB) as b:
                steps.start(b * (first_steps + finish_steps) + (prologue_steps - finish_steps))
                for s in range(STEPS + 1):
                    retrieval_step(b - 1, s)
                    if s < STEPS:
                        run_pieces(front, b, PIECES[s])
                finish(b - 1)
                hand_over(b)
                assert steps.n == first_steps + finish_steps, (steps.n, first_steps)
            steps.start(prologue_steps + NB * first_steps + (NB - 1) * finish_steps)
            for s in range(STEPS + 1):
                retrieval_step(NB - 1, s)
            finish(NB - 1)


def kernel(x, mem, positions, rel_bias, norm_mix, w_in, mla_q_norm, mla_w_uq, mla_kv_norm, mla_w_ukv, lru_conv_w, lru_conv_b,
           lru_w_a, lru_b_a, lru_w_x, lru_b_x, lru_lambda, diff_lambda, diff_norm, out_norm_mla, out_norm_lru, w_out,
           norm_cross, norm_mem, w_cq, w_ckv, w_co, norm_ffn, peer_w_q, peer_keys, peer_u, peer_v, norm_final):
    import concourse.bacc as bacc
    from concourse.bass_utils import run_bass_kernel_spmd

    A = np.asarray

    def column_slices(w):
        n = w.shape[1] // P
        return w.reshape(2, 4, P, n, P).transpose(3, 0, 2, 1, 4).reshape(2 * n, P, HALF)

    def row_slices(w):
        return w.reshape(KT, P, 2, HALF).transpose(2, 0, 1, 3).reshape(2 * KT, P, HALF)

    def swapped(w):
        return np.concatenate([w[..., ROPE // 2:], w[..., :ROPE // 2]], axis=-1)

    w = A(w_in)[0]
    at = np.cumsum([0, Q_RANK, KV_RANK, ROPE, LRU_W, LRU_W, 256, 256, 256])
    c_q, c_kv, k_r, x_l, g_l, q_d, k_d, v_d = (w[:, at[i]:at[i + 1]] for i in range(8))
    w_in_own = np.concatenate([c_q, k_r, swapped(k_r), c_kv, q_d, k_d, x_l, g_l, v_d], axis=1)
    ckv = A(w_ckv)[0]
    wstream = np.concatenate([column_slices(ckv[:, :D]), row_slices(ckv[:, D:]), column_slices(w_in_own), row_slices(A(w_out)[0]),
                              column_slices(A(w_cq)[0]), row_slices(A(w_co)[0]), column_slices(A(peer_w_q)[0])])

    columns = np.zeros((P, N_COLS), np.float32)

    def put(name, a, rows=P):
        a = A(a).reshape(-1, rows).T
        columns[0:rows, COL[name]:COL[name] + a.shape[1]] = a

    for name, a in (("mix", norm_mix), ("cross", norm_cross), ("mem", norm_mem), ("ffn", norm_ffn), ("kvn", mla_kv_norm),
                    ("conv_w", lru_conv_w), ("conv_b", lru_conv_b), ("lam", lru_lambda)):
        put(name, a)
    columns[:, COL["qn"]] = A(mla_q_norm)[0, 0:P]
    columns[0:Q_RANK - P, COL["qn"] + 1] = A(mla_q_norm)[0, P:]
    dn = A(diff_norm)[0]
    put("yn", np.concatenate([A(out_norm_mla)[0], A(out_norm_lru)[0], dn, dn, dn, dn]))
    put("gate_b", np.concatenate([A(lru_b_a).reshape(-1), A(lru_b_x).reshape(-1)]))
    freq = np.float32(ROPE_THETA) ** (-np.arange(0, ROPE, 2, dtype=np.float32) / np.float32(ROPE))
    columns[NOPE:NOPE + ROPE, COL["freq"]] = np.concatenate([freq, freq])
    columns[NOPE:NOPE + ROPE, COL["sign"]] = np.repeat(np.float32([-1, 1]), ROPE // 2)

    uq = A(mla_w_uq)[0].reshape(Q_RANK, MLA_H, NOPE + ROPE)
    uq = np.concatenate([uq, swapped(uq[:, :, NOPE:])], axis=2).reshape(Q_RANK, MLA_H * P)
    w_uq = np.zeros((P, 2, MLA_H * P), np.float32)
    w_uq[:, 0] = uq[0:P]
    w_uq[0:Q_RANK - P, 1] = uq[P:]
    ukv = A(mla_w_ukv)[0].reshape(KV_RANK, MLA_H, 2, NOPE)
    w_ukv = ukv.transpose(0, 2, 1, 3).reshape(KV_RANK, 2, MLA_H * NOPE)
    w_gates = np.zeros((P, 2, LT, P), np.float32)
    for a, g in enumerate((A(lru_w_a)[0], A(lru_w_x)[0])):
        for i in range(LRU_W // LRU_G):
            r = (i % 2) * LRU_G
            w_gates[r:r + LRU_G, a, i // 2, r:r + LRU_G] = g[i]
    pk = A(peer_keys)[0]
    keys_t = np.zeros((P, 2 * NKEYS), np.float32)
    keys_t[0:64, 0:NKEYS] = pk[0].T
    keys_t[64:128, NKEYS:] = pk[1].T

    ins = {
        "x": A(x)[0], "wstream": wstream, "columns": columns, "w_uq": w_uq, "w_ukv": w_ukv, "w_gates": w_gates, "keys_t": keys_t,
        "ffn_gain": A(norm_ffn)[0], "final_gain": A(norm_final), "mem": A(mem)[0], "positions": A(positions)[0],
        "pos_cols": A(positions)[0].reshape(NB, P).T,
        "rel_bias": A(rel_bias).reshape(-1), "diff_lambda": A(diff_lambda)[0].reshape(-1), "peer_u": A(peer_u)[0],
        "peer_v": A(peer_v)[0],
    }
    ins = {k: np.ascontiguousarray(v) for k, v in ins.items()}
    nc = bacc.Bacc("TRN2", target_bir_lowering=False, num_devices=1)
    aps = {k: nc.dram_tensor("in_" + k, v.shape, mybir.dt.from_np(v.dtype), kind="ExternalInput").ap() for k, v in ins.items()}
    out = nc.dram_tensor("out", (SEQ, D), F32, kind="ExternalOutput").ap()
    program(nc, *aps.values(), out)
    r = run_bass_kernel_spmd(nc, [{"in_" + k: v for k, v in ins.items()}], core_ids=[0])
    return r.results[0]["out"].reshape(1, SEQ, D)
```

```python
import math
from contextlib import ExitStack

import concourse.bass as bass
import numpy as np
from concourse import mybir

F32 = mybir.dt.float32
I32 = mybir.dt.int32
U32 = mybir.dt.uint32
ALU = mybir.AluOpType
ACT = mybir.ActivationFunctionType
AX_X = mybir.AxisListType.X

P = 128
D = 1024
KT = D // P
SEQ = 1024
NB = SEQ // P
MEM = 256
MT = MEM // P
EPS = 1e-6
NEG = -1e30

MLA_H, NOPE, ROPE, MLA_V = 4, 64, 32, 64
Q_RANK, KV_RANK = 192, 128
MLA_SCALE = 1.0 / math.sqrt(NOPE + ROPE)
ROPE_THETA = 10000.0
LRU_W, LRU_G, CONV_W = 512, 64, 4
LT = LRU_W // P
DIFF_H, DK, DV = 4, 32, 64
DIFF_SCALE = 1.0 / math.sqrt(DK)
LAM_INIT = 0.8 - 0.6 * math.exp(-0.3 * 0)
CROSS_H = 4
CROSS_SCALE = 1.0 / math.sqrt(D // CROSS_H)
BUCKETS, MAX_DIST = 32, 128
HEADS, NKEYS, TOPK = 8, 128, 16
EXPERTS = HEADS * TOPK

HALF = 512
VECTOR_HEADS = 2
W_RING = 7
G_RING = 8
STEP = 8
STEPS = EXPERTS // STEP
IN_TILES = 17
MEM_SLICES = 4 * KT
BLOCK_SLICES = 2 * (IN_TILES + 4 * KT)
W_SHIFT = (-MEM_SLICES) % W_RING
BAND = 2 * SEQ - P

_COLS = [("mix", KT), ("cross", KT), ("mem", KT), ("ffn", KT), ("qn", 2), ("kvn", 1), ("yn", KT), ("conv_w", CONV_W * LT),
         ("conv_b", LT), ("gate_b", 2 * LT), ("lam", LT), ("freq", 1), ("sign", 1)]
COL, N_COLS = {}, 0
for _name, _n in _COLS:
    COL[_name] = N_COLS
    N_COLS += _n


def bucket_starts():
    exact = BUCKETS // 2
    out = [float(j) for j in range(1, exact + 1)]
    for j in range(1, BUCKETS - exact):
        out.append(float(math.ceil(exact * (MAX_DIST / exact) ** (j / (BUCKETS - exact)))))
    return out


TWO_PI_A = 6.28125
TWO_PI_B = float(np.float32(np.round((2 * math.pi - TWO_PI_A) * 2 ** 21) / 2 ** 21))
TWO_PI_C = 2 * math.pi - TWO_PI_A - TWO_PI_B
ROUND = 1.5 * 2.0 ** 23

PIECES = [("norm_mix", 2), ("project_0", 5), ("project_1", 5), ("project_2", 5), ("latents", 1), ("project_3", 5),
          ("project_4", 3), ("mla_up", 2), ("conv", 1), ("gates", 3), ("recur", 1)] \
    + [(f"mla_{h}", 3) for h in range(MLA_H)] + [(f"diff_{h}", 5) for h in range(DIFF_H)] \
    + [("join", 1), ("mix_out", 11), ("norm_cross", 2), ("cross_q", 11), ("cross_scores", 1), ("cross_mix", 2),
       ("cross_out", 11), ("norm_ffn", 2), ("peer_q", 11), ("peer_scores", 2), ("top_0", 5), ("top_1", 5), ("choose", 14)]


def spans():
    total, done, out = sum(n for _, n in PIECES), 0, []
    for name, n in PIECES:
        out.append((name, EXPERTS * done / total, EXPERTS * (done + n) / total))
        done += n
    return out


GATE_LAG = 1
DIAG_LAG = STEP + 2
SUM_LAG = STEP + 3
GATHER_LAG = STEP + 4
EARLY = G_RING
END = EXPERTS + SUM_LAG


def program(nc, x, wstream, columns, w_uq, w_ukv, w_gates, keys_t, ffn_gain, final_gain, mem, positions, pos_cols,
            rel_bias, diff_lambda, peer_u, peer_v, out):
    with ExitStack() as ctx:
        def sb(name, shape, dt=F32):
            return ctx.enter_context(nc.sbuf_tensor(name, shape, dt))

        def pb(name, cols):
            return ctx.enter_context(nc.psum_tensor(name, [P, cols], F32))

        def sem(name):
            return ctx.enter_context(nc.semaphore(name))

        rows = sb("rows", [P, 2 * G_RING, D])
        u_rows, v_rows = rows[:, 0:G_RING, :], rows[:, G_RING:2 * G_RING, :]
        w_ring = sb("w_ring", [P, W_RING, HALF])
        ident = sb("ident", [P, P])
        ones = sb("ones", [P, P])
        cols = sb("cols", [P, N_COLS])
        ffn_row = sb("ffn_row", [P, D])
        final_row = sb("final_row", [P, D])
        wuq = sb("wuq", [P, 2, MLA_H * P])
        wukv = sb("wukv", [P, 2, MLA_H * NOPE])
        wgate = sb("wgate", [P, 2, LT, P])
        keys = sb("keys", [P, 2 * NKEYS])
        mem_k = sb("mem_k", [P, KT, MEM])
        mem_v = sb("mem_v", [P, MT, D])
        k_mla = sb("k_mla", [NOPE + ROPE, MLA_H, SEQ])
        v_mla = sb("v_mla", [P, NB, MLA_H * MLA_V])
        k_diff = sb("k_diff", [P, 2, SEQ])
        v_diff = sb("v_diff", [P, NB, DIFF_H * DV])
        x_next = sb("x_next", [P, D])
        x_cur = sb("x_cur", [P, D])
        h_cur = sb("h_cur", [P, D])
        xs = sb("xs", [P, D])
        hT = sb("hT", [P, KT, P])
        e0 = sb("e0", [P, D])
        e1 = sb("e1", [P, D])
        pT = sb("pT", [P, KT, P])
        bias_t = sb("bias_t", [P, SEQ])
        feat_a = sb("feat_a", [P, KT * P])
        feat_b = sb("feat_b", [P, KT * P])
        conv_in = sb("conv_in", [P, LT, P + CONV_W - 1])
        rope_t = sb("rope_t", [NOPE + ROPE, 2, P])
        k_swap = sb("k_swap", [NOPE + ROPE, P])
        h_last = sb("h_last", [P, LT])
        small = sb("small", [P, 128])
        gates_c = sb("gates_c", [P, 3 * LT])
        lru_c = sb("lru_c", [P, 2 * LT])
        lam_t = sb("lam_t", [P, 8])
        pos_i = sb("pos_i", [P, NB], I32)
        pos_q = sb("pos_q", [P, NB])
        flag = sb("flag", [P, 1], I32)
        iota_i = sb("iota_i", [P, TOPK], I32)
        iota_f = sb("iota_f", [P, TOPK])
        ids_u = sb("ids_u", [P, EXPERTS], U32)
        ids_v = sb("ids_v", [P, EXPERTS], U32)
        g_cur = sb("g_cur", [P, EXPERTS])
        dots = sb("dots", [P, EXPERTS])
        acts = sb("acts", [P, EXPERTS])
        coef = acts
        diag = sb("diag", [P, 4, P])
        out_stat = sb("out_stat", [P, 8])

        latent = feat_a[:, 0:3 * P].rearrange("p (a t) -> p a t", a=3)
        latent_n = feat_a[:, 3 * P:6 * P].rearrange("p (a t) -> p a t", a=3)
        q_diff = feat_a[:, 6 * P:8 * P].rearrange("p (a t) -> p a t", a=2)
        q_mla = feat_b[:, 0:4 * P].rearrange("p (a t) -> p a t", a=4)
        gelu_g = feat_b[:, 4 * P:8 * P].rearrange("p (a t) -> p a t", a=4)
        feat_q = feat_a[:, :].rearrange("p (a t) -> p a t", a=KT)
        cross_oT = feat_b[:, :].rearrange("p (a t) -> p a t", a=KT)
        lru_x = e0[:, 0:512].rearrange("p (a t) -> p a t", a=LT)
        lru_a = e0[:, 512:1024].rearrange("p (a t) -> p a t", a=LT)
        lru_t = e1[:, 0:512].rearrange("p (a t) -> p a t", a=LT)
        lru_i = e1[:, 512:1024].rearrange("p (a t) -> p a t", a=LT)
        table = dots[:, 0:BUCKETS * DIFF_H]
        steps_t = acts[:, 0:(BUCKETS - 1) * DIFF_H]
        top_v = feat_b[:, 0:256].rearrange("p (a k) -> p a k", k=TOPK)
        top_i = feat_b[:, 256:512].bitcast(U32).rearrange("p (a k) -> p a k", k=TOPK)
        top_f = feat_b[:, 512:768].rearrange("p (a k) -> p a k", k=TOPK)
        best_v = feat_b[:, 768:896].rearrange("p (a k) -> p a k", k=TOPK)
        best_i = feat_b[:, 896:1024].bitcast(U32).rearrange("p (a k) -> p a k", k=TOPK)
        pick = pT[:, 0:4, :]
        pick_i = pT[:, 4:6, :].bitcast(U32)
        ids_next, g_next = pT[:, 6, :].bitcast(U32), pT[:, 7, :]
        mem_t = rows[:, 14:16, :].rearrange("p a (k m) -> p (a k) m", m=MEM)

        near = SEQ - 2 * P
        band = [rows[:, 2 * h:2 * h + 2, :].rearrange("p a c -> p (a c)") for h in range(DIFF_H + 1)]
        ahead = rows[:, 13, :]
        gap, dist, hidden = ahead[:, 0:256], ahead[:, 256:512], ahead[:, 512:768]

        ps_sum = pb("ps_sum", D)
        ps_p = [pb("ps_p0", 512), pb("ps_p1", 512)]
        ps_s = pb("ps_s", D)
        ps_t = [pb("ps_t0", 512), pb("ps_t1", 512)]

        bias_d = nc.dram_tensor("bias_rows", (DIFF_H + 1, SEQ, BAND), F32, kind="Internal").ap()
        rope_d = nc.dram_tensor("rope_rows", (2, ROPE, SEQ), F32, kind="Internal").ap()

        cols_in, rows_in, pos_in, mem_in = sem("cols_in"), sem("rows_in"), sem("pos_in"), sem("mem_in")
        consts_in = sem("consts_in")
        w_landed = [sem(f"w_landed{i}") for i in range(W_RING)]
        w_used = sem("w_used")
        consts_made = sem("consts_made")
        ones_made = sem("ones_made")
        ahead_made = sem("ahead_made")
        dve_step, act_step, pool_step = sem("dve_step"), sem("act_step"), sem("pool_step")
        band_step, near_step, any_step, top_step = (sem(n) for n in ("band_step", "near_step", "any_step", "top_step"))
        pre = {n: sem("pre_" + n) for n in
               ("square", "xs", "turned", "memT", "k_out", "v_out", "abs", "exp", "lamsum",
                "lamexp", "rope_arg", "rope_done", "rope_stored", "band", "stored", "flag", "steps", "gaps", "near")}
        x_landed, rope_landed, x_stored = sem("x_landed"), sem("rope_landed"), sem("x_stored")
        bias_landed, bias_used = sem("bias_landed"), sem("bias_used")
        handed = sem("handed")
        squared, scaled, turned, hT_made = sem("squared"), sem("scaled"), sem("turned"), sem("hT_made")
        proj_out = [sem(f"proj_out{g}") for g in range(5)]
        lat_sq, lat_sum, lat_n = sem("lat_sq"), sem("lat_sum"), sem("lat_n")
        up_q, up_k, up_v, q_swap, q_nope, q_rope, k_rope, kv_out = (sem(n) for n in (
            "up_q", "up_k", "up_v", "q_swap", "q_nope", "q_rope", "k_rope", "kv_out"))
        conv_done, gate_ps, gate_out, decay_out, root_in, root_out = (sem(n) for n in (
            "conv_done", "gate_ps", "gate_out", "decay_out", "root_in", "root_out"))
        lru_sq, lru_sum, lru_done = sem("lru_sq"), sem("lru_sum"), sem("lru_done")
        s_ps, s_max, s_exp, w_done = sem("s_ps"), sem("s_max"), sem("s_exp"), sem("w_done")
        p_turned, pT_made, pv_ps, pv_out = sem("p_turned"), sem("pT_made"), sem("pv_ps"), sem("pv_out")
        y_made, y_turned, yT_made = sem("y_made"), sem("y_turned"), sem("yT_made")
        out_added = sem("out_added")
        q_out = sem("q_out")
        c_ps, c_max, c_exp, c_norm, c_turned, c_pT, co_ps, co_out = (sem(n) for n in (
            "c_ps", "c_max", "c_exp", "c_norm", "c_turned", "c_pT", "co_ps", "co_out"))
        k_ps, k_out = sem("key_ps"), sem("key_out")
        g_arg, g_exp, chosen = sem("g_arg"), sem("g_exp"), sem("chosen")
        x_handed, ids_handed, v_ids_handed = sem("x_handed"), sem("ids_handed"), sem("v_ids_handed")
        u_landed = [sem(f"u_landed{i}") for i in range(G_RING)]
        v_landed = [sem(f"v_landed{i}") for i in range(G_RING)]
        u_used, v_used = sem("u_used"), sem("v_used")
        acts_made, coef_made, diag_made = sem("acts_made"), sem("coef_made"), sem("diag_made")
        fin_sum, fin_sq, fin_made, fin_stored = sem("fin_sum"), sem("fin_sq"), sem("fin_made"), sem("fin_stored")

        class Steps:

            def __init__(self, semaphore):
                self.sem, self.origin, self.n = semaphore, 0, 0

            def start(self, origin):
                self.origin, self.n = origin, 0

            def note(self, ins):
                ins.then_inc(self.sem, 1)
                self.n += 1

            def settle(self, eng):
                eng.wait_ge(self.sem, self.origin + self.n)

            def run(self, eng, ins):
                self.note(ins)
                self.settle(eng)

        def ge(eng, semaphore, value):
            if isinstance(value, int) and value <= 0:
                return
            eng.wait_ge(semaphore, value)

        def bc(ap, shape):
            return ap.broadcast_to(shape)

        def col(name, i=0, n=1):
            return cols[:, COL[name] + i:COL[name] + i + n]

        def products(b, i):
            return b * BLOCK_SLICES + (MEM_SLICES + i)

        class Pace:

            def __init__(self, position):
                self.position, self.at, self.bp = position, 0, None

            def start(self, bp):
                self.at, self.bp = 0, bp

            def to(self, r):
                if self.bp is not None:
                    for p in range(self.at, r):
                        self.position(self.bp, p)
                    self.at = max(self.at, r)

            def part(self, share):
                self.to(int(self.first + share * (self.last - self.first)))

            def run(self, front, b):
                for name, self.first, self.last in spans():
                    if name in front:
                        self.part(0)
                        front[name](b)
                self.to(EXPERTS)

        def counter(eng, name):
            reg = eng.alloc_register(name)
            eng.reg_mov(reg, 0)
            return reg

        def key_tiles(b):
            return 2 if isinstance(b, int) else NB

        def wait_more(eng, semaphore, waited, n):
            eng.wait_ge(semaphore, eng.snap(waited) + n)
            eng.reg_add(waited, waited, n)

        block = ctx.enter_context(nc.Block())

        @block.sync
        def _(sp):
            def load_w(i, n):
                slot = (i + W_SHIFT) % W_RING if isinstance(n, int) and n < MEM_SLICES else (i - MEM_SLICES) % W_RING
                ge(sp, w_used, n - W_RING + 1)
                sp.dma_start(w_ring[:, slot, :], wstream[i]).then_inc(w_landed[slot], 16)

            sp.dma_start(cols[:, :], columns).then_inc(cols_in, 16)
            for t in range(MT):
                sp.dma_start((e0, e1)[t][:, :], mem[t * P:(t + 1) * P, :]).then_inc(mem_in, 16)
            for i in range(W_RING):
                load_w(i, i)
            sp.dma_start(rows[:, 11, :].bitcast(I32), positions.partition_broadcast(P)).then_inc(pos_in, 16)
            sp.dma_start(pos_i[:, :], pos_cols).then_inc(pos_in, 16)
            sp.dma_start(table[:, :], rel_bias.partition_broadcast(P)).then_inc(rows_in, 16)
            sp.dma_start(g_cur[:, 0:4 * DK], diff_lambda.partition_broadcast(P)).then_inc(rows_in, 16)
            sp.dma_start(wuq[:, :, :], w_uq).then_inc(consts_in, 16)
            sp.dma_start(wukv[:, :, :], w_ukv).then_inc(consts_in, 16)
            sp.dma_start(wgate[:, :, :, :], w_gates).then_inc(consts_in, 16)
            sp.dma_start(keys[:, :], keys_t).then_inc(consts_in, 16)
            sp.dma_start(ffn_row[:, :], ffn_gain.partition_broadcast(P)).then_inc(consts_in, 16)
            sp.dma_start(final_row[:, :], final_gain.partition_broadcast(P)).then_inc(consts_in, 16)
            for i in range(W_RING, MEM_SLICES):
                load_w(i, i)
            jumps = sp.alloc_register("jumps_sp")
            row_at, col_at, row_step, col_step = (sp.alloc_register(n) for n in ("row_at", "col_at", "row_step", "col_step"))

            def store_rope():
                for c in range(2):
                    sp.wait_ge(pre["rope_done"], c + 1)
                    sp.dma_start(rope_d[c], (x_cur, h_cur)[c][NOPE:NOPE + ROPE, :]).then_inc(pre["rope_stored"], 16)
                sp.wait_ge(pre["rope_stored"], 32)

            def store_mask():
                sp.wait_ge(pre["flag"], 1)
                sp.reg_load(jumps, flag[0:1, 0:1])
                with sp.If_eq(jumps, 0):
                    for reg, value in ((row_at, 0), (col_at, SEQ - P), (row_step, 0), (col_step, P)):
                        sp.reg_mov(reg, value)
                    sp.wait_ge(pre["band"], 1)
                    store_band(DIFF_H, 1)
                with sp.Else():
                    for reg, value in ((row_at, 0), (col_at, 0), (row_step, P), (col_step, 0)):
                        sp.reg_mov(reg, value)
                    with sp.Fori(0, NB) as b:
                        for h in range(DIFF_H + 1):
                            sp.wait_ge(ones_made, 1)
                            sp.wait_ge(pre["band"], b * (DIFF_H + 1) + (h + 1))
                            sp.dma_start(bias_d[h, bass.ds(b * P, P), 0:SEQ], rows[:, h, :]).then_inc(pre["stored"], 16)
                    sp.wait_ge(pre["stored"], 16 * NB * (DIFF_H + 1))
                sp.nop()

            def store_band(h, n):
                sp.dma_start(bias_d[h, 0:P, :], rows[:, 2 * h:2 * h + 2, :].rearrange("p a c -> p (a c)")[:, 0:BAND])\
                  .then_inc(pre["stored"], 16)
                sp.wait_ge(pre["stored"], 16 * n)

            def store_biases():
                with sp.If_eq(jumps, 0):
                    sp.wait_ge(pre["near"], VECTOR_HEADS)
                    sp.wait_ge(pre["band"], 1 + (DIFF_H - VECTOR_HEADS))
                    for h in range(DIFF_H):
                        store_band(h, 2 + h)
                with sp.Else():
                    sp.nop()
                sp.nop()

            def front_loads(b, c0, c1):
                for i in range(c0, c1):
                    load_w(MEM_SLICES + i, MEM_SLICES + b * BLOCK_SLICES + i)

            def load_bias(b, h):
                order = b * (DIFF_H + 1) + (h + 1) % (DIFF_H + 1)
                at, left = sp.snap(row_at, min_val=0, max_val=SEQ - P), sp.snap(col_at, min_val=0, max_val=SEQ - P)
                sp.wait_ge(ones_made, 1)
                ge(sp, bias_used, order)
                sp.dma_start(bias_t[:, :], bias_d[h, bass.ds(at, P), bass.ds(left, SEQ)]).then_inc(bias_landed, 16)
                if h == DIFF_H - 1:
                    sp.reg_add(row_at, row_at, row_step)
                    sp.reg_sub(col_at, col_at, col_step)

            def load_x(b):
                sp.wait_ge(ones_made, 1)
                ge(sp, x_handed, b)
                sp.dma_start(x_next[:, :], x[bass.ds(b * P, P), :]).then_inc(x_landed, 16)

            def load_rope(b):
                sp.wait_ge(ones_made, 1)
                ge(sp, q_rope, b)
                ge(sp, k_rope, b)
                sp.dma_start(rope_t[NOPE:NOPE + ROPE, :, :],
                             rope_d[:, :, bass.ds(b * P, P)].rearrange("c r t -> r c t")).then_inc(rope_landed, 16)

            tile = 2
            w_at = {"project_0": (0, 3), "project_1": (3, 7), "project_2": (7, 11), "project_3": (11, 15),
                    "project_4": (15, 17), "mix_out": (17, 25), "cross_q": (25, 33), "cross_out": (33, 41),
                    "peer_q": (41, 49)}
            front = {n: (lambda b, r=r: front_loads(b, tile * r[0], tile * r[1])) for n, r in w_at.items()}
            front["norm_mix"] = load_x

            def project_3(b):
                front_loads(b, tile * 11, tile * 15)
                if isinstance(b, int):
                    store_rope()
                load_rope(b)

            def project_4(b):
                front_loads(b, tile * 15, tile * 17)
                if isinstance(b, int):
                    store_mask()
                load_bias(b, DIFF_H)

            def diff_0(b):
                if isinstance(b, int):
                    store_biases()
                load_bias(b, 0)

            front["project_3"], front["project_4"], front["diff_0"] = project_3, project_4, diff_0
            for h in range(1, DIFF_H):
                front[f"diff_{h}"] = lambda b, h=h: load_bias(b, h)

            def store(b):
                sp.wait_ge(ones_made, 1)
                ge(sp, fin_made, b + 1)
                sp.dma_start(out[bass.ds(b * P, P), :], x_cur[:, :]).then_inc(fin_stored, 16)

            pace = Pace(None)
            pace.run(front, 0)
            with sp.Fori(1, NB) as b:
                pace.run(front, b)
                store(b - 1)
            store(NB - 1)
            sp.wait_ge(fin_stored, 16 * NB)

        @block.gpsimd
        def _(pool):
            pool.memset(ident[:, :], 0.0).then_inc(pool_step, 1)
            pool.iota(iota_i[:, :], [[1, TOPK]], base=0, channel_multiplier=0).then_inc(consts_made, 1)
            pool.iota(rows[:, 13, :].bitcast(I32), [[1, SEQ]], base=0, channel_multiplier=-1).then_inc(consts_made, 1)
            pool.wait_ge(pool_step, 1)
            pool.affine_select(out=ident[:, :], in_=ident[:, :], compare_op=ALU.not_equal, fill=1.0, base=0,
                               pattern=[[-1, P]], channel_multiplier=1).then_inc(consts_made, 1)
            for t in (k_mla, v_mla, k_diff, v_diff, conv_in, h_last):
                pool.memset(t[tuple(slice(None) for _ in t.shape)], 0.0).then_inc(consts_made, 1)

            u_waited, v_waited, ids_waited, v_ids_waited = (counter(pool, n) for n in (
                "u_waited", "v_waited", "ids_waited", "v_ids_waited"))

            def gather_u(j):
                wait_more(pool, u_used, u_waited, 1)
                pool.indirect_dma_start(u_rows[:, j % G_RING, :], None, peer_u,
                                        bass.IndirectOffsetOnAxis(ap=ids_u[:, j:j + 1], axis=0)).then_inc(u_landed[j % G_RING], 16)

            def gather_v(j):
                wait_more(pool, v_used, v_waited, 1)
                pool.indirect_dma_start(v_rows[:, j % G_RING, :], None, peer_v,
                                        bass.IndirectOffsetOnAxis(ap=ids_v[:, j:j + 1], axis=0)).then_inc(v_landed[j % G_RING], 16)

            def retrieve(more):
                for i in range(G_RING, EXPERTS):
                    gather_u(i)
                    if i == GATHER_LAG:
                        wait_more(pool, v_ids_handed, v_ids_waited, 1)
                    if i >= GATHER_LAG:
                        gather_v(i - GATHER_LAG)
                for j in range(EXPERTS - GATHER_LAG, EXPERTS):
                    k = j - (EXPERTS - G_RING)
                    if more and k == 0:
                        wait_more(pool, ids_handed, ids_waited, 1)
                    if more and k >= 0:
                        gather_u(k)
                    gather_v(j)

            def bias_of(add, wait, dist, mask, dst, heads):
                for d, h in zip(dst, heads):
                    add(pool.tensor_scalar(d, dist, 0.0, table[:, h:h + 1], ALU.mult, ALU.add))
                wait()
                for j, start in enumerate(bucket_starts()):
                    for m, h in zip(mask, heads):
                        add(pool.tensor_scalar(m, dist, start, steps_t[:, j * DIFF_H + h:j * DIFF_H + h + 1], ALU.is_ge, ALU.mult))
                    wait()
                    for m, d in zip(mask, dst):
                        add(pool.tensor_tensor(d, d, m, ALU.add))
                    wait()

            pool.wait_ge(consts_made, 3)
            pool.tensor_copy(ahead, ahead.bitcast(I32)).then_inc(ahead_made, 1)
            pool.wait_ge(ahead_made, 1)
            pool.wait_ge(pre["steps"], 1)
            pool.wait_ge(pre["flag"], 1)
            jumps = pool.alloc_register("jumps_pool")
            pool.reg_load(jumps, flag[0:1, 0:1])
            with pool.If_eq(jumps, 0):
                band_steps = Steps(band_step)
                mask = [rows[:, 10, h * 256:(h + 1) * 256] for h in range(DIFF_H)]
                band_steps.run(pool, pool.tensor_scalar(gap, ahead[:, 0:256], -1.0, float(P), ALU.mult, ALU.add))
                band_steps.note(pool.tensor_scalar(hidden, gap, 0.0, NEG, ALU.is_lt, ALU.mult))
                for h in range(DIFF_H + 1):
                    band_steps.note(pool.memset(band[h][:, 0:SEQ], 0.0))
                    band_steps.note(pool.memset(band[h][:, SEQ:BAND], NEG))
                band_steps.run(pool, pool.tensor_scalar(dist, gap, 0.0, None, ALU.max))
                pool.tensor_tensor(band[DIFF_H][:, near:SEQ], band[DIFF_H][:, near:SEQ], hidden, ALU.add).then_inc(pre["band"], 1)
                pool.wait_ge(pre["band"], 1)
                pool.nop().then_inc(pre["gaps"], 1)
                for h in range(DIFF_H):
                    last = (BUCKETS - 1) * DIFF_H + h
                    band_steps.note(pool.tensor_scalar(band[h][:, 0:near], band[h][:, 0:near], 0.0, table[:, last:last + 1],
                                                       ALU.mult, ALU.add))
                own = range(VECTOR_HEADS, DIFF_H)
                bias_of(band_steps.note, lambda: band_steps.settle(pool), dist, mask, [band[h][:, near:SEQ] for h in own], own)
                for h in own:
                    pool.tensor_tensor(band[h][:, near:SEQ], band[h][:, near:SEQ], hidden, ALU.add).then_inc(pre["band"], 1)
                pool.wait_ge(pre["stored"], 16 * (DIFF_H + 1))
            with pool.Else():
                dist_any, hidden_any = rows[:, 5, :], rows[:, 11, :]
                mask = [rows[:, 6 + h, :] for h in range(DIFF_H)]
                tiles = [rows[:, h, :] for h in range(DIFF_H + 1)]
                first_ahead, own = lam_t[:, 6:7], lam_t[:, 7:8]
                any_waited, noted = counter(pool, "any_waited"), [0]

                def add(ins):
                    ins.then_inc(any_step, 1)
                    noted[0] += 1

                def wait():
                    wait_more(pool, any_step, any_waited, noted[0])
                    noted[0] = 0

                stored_waited = counter(pool, "stored_waited")
                pool.wait_ge(pre["rope_done"], 2)
                pool.memset(first_ahead, 0.0).then_inc(any_step, 1)
                wait_more(pool, any_step, any_waited, 1)
                with pool.Fori(0, NB) as b:
                    add(pool.tensor_copy(own, pos_q[:, bass.ds(b, 1)]))
                    wait()
                    add(pool.tensor_scalar(dist_any, rows[:, 12, :], own, -1.0, ALU.subtract, ALU.mult))
                    wait()
                    add(pool.tensor_scalar(dist_any, dist_any, 0.0, None, ALU.max))
                    add(pool.memset(tiles[DIFF_H], 0.0))
                    wait()
                    bias_of(add, wait, dist_any, mask, tiles[0:DIFF_H], range(DIFF_H))
                    add(pool.tensor_scalar(hidden_any, ahead, first_ahead, NEG, ALU.is_gt, ALU.mult))
                    wait()
                    add(pool.tensor_scalar(first_ahead, first_ahead, float(P), None, ALU.add))
                    wait()
                    for h in range(DIFF_H + 1):
                        pool.tensor_tensor(tiles[h], tiles[h], hidden_any, ALU.add).then_inc(pre["band"], 1)
                    wait_more(pool, pre["stored"], stored_waited, 16 * (DIFF_H + 1))
            pool.nop()
            pool.wait_ge(pre["rope_done"], 2)
            pool.wait_ge(pre["v_out"], 4)
            wait_more(pool, ids_handed, ids_waited, 1)
            for k in range(G_RING):
                gather_u(k)
            with pool.Fori(0, NB - 1):
                retrieve(True)
            retrieve(False)
            u_last, v_last = pool.snap(u_waited), pool.snap(v_waited)
            pool.wait_ge(u_used, u_last)
            pool.wait_ge(v_used, v_last)

        @block.tensor
        def _(pe):
            def slice_in(i, uses):
                pe.wait_ge(w_landed[i], 16 * uses)

            def mem_slice(i):
                slot = (i + W_SHIFT) % W_RING
                before = sum(1 for j in range(i) if (j + W_SHIFT) % W_RING == slot)
                pe.wait_ge(w_landed[slot], 16 * (before + 1))
                return w_ring[:, slot, :]

            uses0 = [sum(1 for j in range(MEM_SLICES) if (j + W_SHIFT) % W_RING == s) for s in range(W_RING)]

            def block_slice(b, i):
                slot = i % W_RING
                pe.wait_ge(w_landed[slot], 16 * (BLOCK_SLICES // W_RING) * b + 16 * (uses0[slot] + i // W_RING + 1))
                return w_ring[:, slot, :]

            pe.wait_ge(consts_made, 3)
            for t in range(MT):
                pe.wait_ge(pre["xs"], t + 1)
                for g in range(2):
                    if t:
                        pe.wait_ge(pre["memT"], 2 * (t - 1) + g + 1)
                    for k in range(4):
                        ins = pe.transpose(ps_t[g][:, k * P:(k + 1) * P], (e0, e1)[t][:, (4 * g + k) * P:(4 * g + k + 1) * P], ident[:, :])
                    ins.then_inc(pre["turned"], 1)
            pe.wait_ge(pre["memT"], 2 * MT)
            for f in range(KT):
                if f >= 4 and f % 2 == 0:
                    pe.wait_ge(pre["k_out"], f // 2 - 1)
                for half in range(2):
                    w = mem_slice(2 * f + half).rearrange("p (k c) -> p k c", k=4)
                    for k in range(4):
                        kt = 4 * half + k
                        ins = pe.matmul(ps_p[(f // 2) % 2][:, (f % 2) * MEM:(f % 2 + 1) * MEM], w[:, k, :], mem_t[:, kt, :],
                                        start=(kt == 0), stop=(kt == KT - 1))
                    ins.then_inc(w_used, 1)
            for n in range(2):
                if n:
                    pe.wait_ge(pre["v_out"], 2)
                for kt in range(KT):
                    w = mem_slice(2 * KT + n * KT + kt)
                    for t in range(MT):
                        ins = pe.matmul(ps_s[:, t * 512:(t + 1) * 512], mem_t[:, kt, t * P:(t + 1) * P], w,
                                        start=(kt == 0), stop=(kt == KT - 1), skip_group_check=True)
                    ins.then_inc(w_used, 1)

            def turn_x(b, n):
                pace.part(0.6)
                pe.wait_ge(scaled, 3 * b + n + 1)
                for g in range(2):
                    for k in range(4):
                        ins = pe.transpose(ps_t[g][:, k * P:(k + 1) * P], xs[:, (4 * g + k) * P:(4 * g + k + 1) * P], ident[:, :])
                    ins.then_inc(turned, 1)

            def col_tile(b, i, dst):
                for half in range(2):
                    w = block_slice(b, 2 * i + half).rearrange("p (k c) -> p k c", k=4)
                    for k in range(4):
                        kt = 4 * half + k
                        ins = pe.matmul(dst, w[:, k, :], hT[:, kt, :], start=(kt == 0), stop=(kt == KT - 1))
                    ins.then_inc(w_used, 1)

            def project(b, g, first, n):
                if g == 0:
                    pe.wait_ge(hT_made, 6 * b + 2)
                if g >= 2:
                    pe.wait_ge(proj_out[g - 2], b + 1)
                for i in range(n):
                    pace.part(i / n)
                    dst = ps_p[g % 2][:, i * P:(i + 1) * P]
                    if g < 4:
                        col_tile(b, first + i, dst)
                    else:
                        for half in range(2):
                            w = block_slice(b, 2 * (first + i) + half).rearrange("p (k c) -> p k c", k=4)
                            for k in range(4):
                                kt = 4 * half + k
                                ins = pe.matmul(dst, hT[:, kt, :], w[:, k, :], start=(kt == 0), stop=(kt == KT - 1))
                            ins.then_inc(w_used, 1)

            def latents(b):
                pe.wait_ge(lat_sq, b + 1)
                sq = pT
                pe.matmul(ps_t[0][:, 0:P], ones[:, :], sq[:, 0, :], start=True, stop=False)
                pe.matmul(ps_t[0][:, 0:P], ones[0:64, :], sq[0:64, 1, :], start=False, stop=True)
                pe.matmul(ps_t[0][:, P:2 * P], ones[:, :], sq[:, 2, :], start=True, stop=True).then_inc(lat_sum, 1)

            def mla_up(b):
                pe.wait_ge(lat_n, b + 1)
                pe.wait_ge(proj_out[3], b + 1)
                for h in range(MLA_H):
                    dst = ps_p[1][:, h * P:(h + 1) * P]
                    pe.matmul(dst, wuq[:, 0, h * P:(h + 1) * P], latent_n[:, 0, :], start=True, stop=False)
                    ins = pe.matmul(dst, wuq[0:64, 1, h * P:(h + 1) * P], latent_n[0:64, 1, :], start=False, stop=True)
                ins.then_inc(up_q, 1)
                pe.wait_ge(proj_out[4], b + 1)
                for h in range(MLA_H):
                    ins = pe.matmul(ps_p[0][0:NOPE, h * P:(h + 1) * P], wukv[:, 0, h * NOPE:(h + 1) * NOPE], latent_n[:, 2, :],
                                    start=True, stop=True)
                ins.then_inc(up_k, 1)
                pe.matmul(ps_t[1][:, 0:MLA_H * MLA_V], latent_n[:, 2, :], wukv[:, 1, :], start=True, stop=True).then_inc(up_v, 1)

            def gates(b):
                pace.part(0.1)
                pe.wait_ge(conv_done, b + 1)
                pe.wait_ge(kv_out, 2 * b + 2)
                for a in range(2):
                    for i in range(LT):
                        ins = pe.matmul(ps_t[a][:, i * P:(i + 1) * P], wgate[:, a, i, :], lru_x[:, i, :], start=True, stop=True)
                    ins.then_inc(gate_ps, 1)

            def recur(b):
                pace.part(0.5)
                pe.wait_ge(lru_sq, b + 1)
                for i in range(LT):
                    ins = pe.matmul(ps_t[0][:, 0:P], ones[:, :], lru_t[:, i, :], start=(i == 0), stop=(i == LT - 1))
                ins.then_inc(lru_sum, 1)

            def turn_p(b, src):
                n = key_tiles(b) // 2
                for g in range(2):
                    for k in range(n):
                        ins = pe.transpose(ps_t[g][:, k * P:(k + 1) * P], src[:, (n * g + k) * P:(n * g + k + 1) * P], ident[:, :])
                    ins.then_inc(p_turned, 1)

            def key_spans(b):
                n = key_tiles(b) * P
                return [(c, min(c + 512, n)) for c in range(0, n, 512)]

            def mla(b, h):
                if h == 0:
                    pe.wait_ge(q_nope, b + 1)
                    pe.wait_ge(q_rope, b + 1)
                    pe.wait_ge(k_rope, b + 1)
                    pe.wait_ge(kv_out, 2 * b + 2)
                if h == 1:
                    pe.wait_ge(lru_done, b + 1)
                n = 12 * b + h
                ge(pe, s_max, n)
                for c0, c1 in key_spans(b):
                    ins = pe.matmul(ps_s[:, c0:c1], q_mla[0:NOPE + ROPE, h, :], k_mla[:, h, c0:c1], start=True, stop=True)
                ins.then_inc(s_ps, 1)
                pace.part(0.4)
                pe.wait_ge(s_exp, n + 1)
                turn_p(b, (e0, e1)[h % 2])
                pace.part(0.8)
                m = 8 * b + h
                pe.wait_ge(pT_made, 2 * m + 2)
                for t in range(key_tiles(b)):
                    ins = pe.matmul(ps_p[0][:, h * MLA_V:(h + 1) * MLA_V], pT[:, t, :], v_mla[:, t, h * MLA_V:(h + 1) * MLA_V],
                                    start=(t == 0), stop=(t == key_tiles(b) - 1))
                ins.then_inc(pv_ps, 1)

            def diff(b, h):
                for c in range(2):
                    pace.part(0.2 * c)
                    n = 12 * b + 4 + 2 * h + c
                    ge(pe, s_max, n)
                    r = 32 * ((2 * h + c) % 4)
                    for c0, c1 in key_spans(b):
                        ins = pe.matmul(ps_s[:, c0:c1], q_diff[r:r + DK, (2 * h + c) // 4, :], k_diff[r:r + DK, (2 * h + c) // 4, c0:c1],
                                        start=True, stop=True)
                    ins.then_inc(s_ps, 1)
                pace.part(0.65)
                pe.wait_ge(w_done, 4 * b + h + 1)
                turn_p(b, e0)
                pace.part(0.85)
                m = 8 * b + 4 + h
                pe.wait_ge(pT_made, 2 * m + 2)
                for t in range(key_tiles(b)):
                    ins = pe.matmul(ps_p[1][:, h * DV:(h + 1) * DV], pT[:, t, :], v_diff[:, t, h * DV:(h + 1) * DV],
                                    start=(t == 0), stop=(t == key_tiles(b) - 1))
                ins.then_inc(pv_ps, 1)

            def join(b):
                pace.part(0.9)
                pe.wait_ge(y_made, b + 1)
                for k in range(2):
                    pe.transpose(ps_t[0][:, k * P:(k + 1) * P], xs[:, k * P:(k + 1) * P], ident[:, :])
                for k in range(2):
                    ins = pe.transpose(ps_t[0][:, (2 + k) * P:(3 + k) * P], xs[:, 512 + k * P:512 + (k + 1) * P], ident[:, :])
                ins.then_inc(y_turned, 1)

            def row_product(b, first, lhs):
                for n in range(2):
                    for kt in range(KT):
                        pace.part((n * KT + kt) / (2 * KT))
                        w = block_slice(b, first + n * KT + kt)
                        pe.matmul(ps_s[:, n * 512:(n + 1) * 512], lhs[:, kt, :], w, start=(kt == 0), stop=(kt == KT - 1)).then_inc(w_used, 1)

            def mix_out(b):
                pe.wait_ge(yT_made, b + 1)
                row_product(b, 34, hT)

            def queries(b, n, first):
                pe.wait_ge(hT_made, 6 * b + 4 + 2 * n)
                for f in range(KT):
                    pace.part(f / KT)
                    col_tile(b, first + f, ps_p[f // 4][:, (f % 4) * P:(f % 4 + 1) * P])

            def cross_scores(b):
                pe.wait_ge(q_out, 4 * b + 2)
                pe.wait_ge(out_added, 4 * b + 2)
                for h in range(CROSS_H):
                    for j in range(2):
                        ins = pe.matmul(ps_s[:, h * MEM:(h + 1) * MEM], feat_q[:, 2 * h + j, :], mem_k[:, 2 * h + j, :],
                                        start=(j == 0), stop=(j == 1))
                ins.then_inc(c_ps, 1)

            def cross_mix(b):
                pace.part(0.3)
                pe.wait_ge(c_norm, b + 1)
                for g in range(2):
                    for k in range(4):
                        ins = pe.transpose(ps_t[g][:, k * P:(k + 1) * P], e0[:, (4 * g + k) * P:(4 * g + k + 1) * P], ident[:, :])
                    ins.then_inc(c_turned, 1)
                pace.part(0.6)
                pe.wait_ge(c_pT, 2 * b + 2)
                for f in range(KT):
                    for m in range(MT):
                        ins = pe.matmul(ps_p[f // 4][:, (f % 4) * P:(f % 4 + 1) * P], mem_v[:, m, f * P:(f + 1) * P],
                                        pT[:, 2 * (f // 2) + m, :], start=(m == 0), stop=(m == MT - 1))
                    if f % 4 == 3:
                        ins.then_inc(co_ps, 1)

            def cross_out(b):
                pe.wait_ge(co_out, 2 * b + 2)
                row_product(b, 66, cross_oT)

            def peer_scores(b):
                pe.wait_ge(q_out, 4 * b + 4)
                for g in range(2):
                    pe.wait_ge(out_added, 4 * b + 4)
                    if g:
                        pe.wait_ge(k_out, 2 * b + 1)
                    for h in range(4):
                        ins = pe.matmul(ps_s[:, h * 2 * NKEYS:(h + 1) * 2 * NKEYS], feat_q[:, 4 * g + h, :], keys[:, :],
                                        start=True, stop=True)
                    ins.then_inc(k_ps, 1)

            front = {
                "norm_mix": lambda b: turn_x(b, 0), "latents": latents, "mla_up": mla_up, "gates": gates, "recur": recur,
                "join": join, "mix_out": mix_out, "norm_cross": lambda b: turn_x(b, 1),
                "cross_q": lambda b: queries(b, 0, 25), "cross_scores": cross_scores, "cross_mix": cross_mix,
                "cross_out": cross_out, "norm_ffn": lambda b: turn_x(b, 2), "peer_q": lambda b: queries(b, 1, 41),
                "peer_scores": peer_scores,
            }
            for g, (first, n) in enumerate([(0, 3), (3, 4), (7, 4), (11, 4), (15, 2)]):
                front[f"project_{g}"] = lambda b, g=g, first=first, n=n: project(b, g, first, n)
            for h in range(4):
                front[f"mla_{h}"] = lambda b, h=h: mla(b, h)
                front[f"diff_{h}"] = lambda b, h=h: diff(b, h)

            def add_row(bp, p):
                j = p - SUM_LAG
                if j >= 0:
                    pe.wait_ge(diag_made, bp * EXPERTS + j + 1)
                    pe.wait_ge(v_landed[j % G_RING], bp * (16 * EXPERTS // G_RING) + 16 * (j // G_RING + 1))
                    if j == 0:
                        ge(pe, fin_sum, bp)
                    for n in range(2):
                        ins = pe.matmul(ps_sum[:, n * 512:(n + 1) * 512], diag[:, j % 4, :], v_rows[:, j % G_RING, n * 512:(n + 1) * 512],
                                        start=(j == 0), stop=(j == EXPERTS - 1), skip_group_check=True)
                    ins.then_inc(v_used, 1)

            pace = Pace(add_row)
            pe.nop().then_inc(v_used, G_RING)
            pe.wait_ge(consts_in, 96)
            pe.wait_ge(ones_made, 1)
            pace.run(front, 0)
            with pe.Fori(1, NB) as b:
                pace.start(b - 1)
                pace.run(front, b)
                pace.to(END)
            pace.start(NB - 1)
            pace.to(END)

        @block.scalar
        def _(act):
            def copy(dst, src, scale=1.0):
                return act.activation(dst, src, ACT.Copy, scale=scale)

            for t in range(MT):
                act.wait_ge(mem_in, 16 * MT)
                act.activation(pT[:, :, :].rearrange("p a b -> p (a b)"), (e0, e1)[t][:, :], ACT.Square,
                               accum_out=small[:, t:t + 1]).then_inc(pre["square"], 1)
                act.wait_ge(pre["square"], t + 1)
            act.wait_ge(pre["abs"], 1)
            act.activation(small[:, 12:12 + LT], small[:, 8:8 + LT], ACT.Exp, scale=-1.0).then_inc(pre["exp"], 1)
            act.wait_ge(pre["lamsum"], 1)
            act.activation(lam_t[:, 2:4], lam_t[:, 0:2], ACT.Exp).then_inc(pre["lamexp"], 1)
            for c in range(2):
                act.wait_ge(pre["rope_arg"], c + 1)
                t = (x_cur, h_cur)[c][NOPE:NOPE + ROPE, :]
                act.activation(t, t, ACT.Sin).then_inc(act_step, 1)
                act.wait_ge(act_step, c + 1)
                if c == 0:
                    act.nop().then_inc(pre["rope_done"], 1)
                else:
                    act.activation(t, t, ACT.Copy, scale=cols[NOPE:NOPE + ROPE, COL["sign"]:COL["sign"] + 1]).then_inc(pre["rope_done"], 1)
            for f in range(4):
                act.wait_ge(w_used, 4 * (f + 1))
                copy(mem_k[:, 2 * f:2 * f + 2, :].rearrange("p a b -> p (a b)"), ps_p[f % 2][:, :]).then_inc(pre["k_out"], 1)
            for n in range(2):
                act.wait_ge(w_used, 2 * KT + KT * (n + 1))
                for t in range(MT):
                    copy(mem_v[:, t, n * 512:(n + 1) * 512], ps_s[:, t * 512:(t + 1) * 512]).then_inc(pre["v_out"], 1)

            def square_x(b, n):
                if n == 0:
                    act.wait_ge(x_landed, 16 * b + 16)
                    ge(act, handed, b)
                else:
                    act.wait_ge(out_added, 4 * b + 2 * n)
                act.activation(xs[:, :], x_next[:, :], ACT.Square, accum_out=small[:, n:n + 1]).then_inc(squared, 1)

            def project_0(b):
                pace.part(1)
                act.wait_ge(w_used, products(b, 6))
                copy(latent.rearrange("p a t -> p (a t)"), ps_p[0][:, 0:3 * P])
                copy(k_swap[NOPE:NOPE + ROPE, :], ps_p[0][96:128, P:2 * P]).then_inc(proj_out[0], 1)

            def project_1(b):
                pace.part(1)
                act.wait_ge(w_used, products(b, 14))
                copy(q_diff.rearrange("p a t -> p (a t)"), ps_p[1][:, 0:2 * P], DIFF_SCALE)
                copy(k_diff[:, :, bass.ds(b * P, P)], ps_p[1][:, 2 * P:4 * P].rearrange("p (a t) -> p a t", a=2)).then_inc(proj_out[1], 1)

            def project_2(b):
                pace.part(1)
                act.wait_ge(w_used, products(b, 22))
                copy(conv_in[:, :, CONV_W - 1:], ps_p[0][:, :].rearrange("p (a t) -> p a t", a=LT)).then_inc(proj_out[2], 1)

            def project_3(b):
                pace.part(1)
                act.wait_ge(w_used, products(b, 30))
                act.activation(gelu_g.rearrange("p a t -> p (a t)"), ps_p[1][:, :], ACT.Gelu).then_inc(proj_out[3], 1)

            def project_4(b):
                pace.part(1)
                act.wait_ge(w_used, products(b, 34))
                copy(v_diff[:, bass.ds(b, 1), :].rearrange("p a c -> p (a c)"), ps_p[0][:, 0:2 * P]).then_inc(proj_out[4], 1)

            def mla_up(b):
                act.wait_ge(up_q, b + 1)
                copy(e1[NOPE:NOPE + ROPE, 0:512], ps_p[1][96:128, :]).then_inc(q_swap, 1)
                copy(q_mla[0:NOPE, :, :].rearrange("p a t -> p (a t)"), ps_p[1][0:NOPE, :], MLA_SCALE).then_inc(q_nope, 1)
                act.wait_ge(up_k, b + 1)
                copy(k_mla[0:NOPE, :, bass.ds(b * P, P)], ps_p[0][0:NOPE, :].rearrange("p (a t) -> p a t", a=MLA_H)).then_inc(kv_out, 1)
                act.wait_ge(up_v, b + 1)
                copy(v_mla[:, bass.ds(b, 1), :].rearrange("p a c -> p (a c)"), ps_t[1][:, 0:MLA_H * MLA_V]).then_inc(kv_out, 1)

            def gates(b):
                act.wait_ge(q_rope, b + 1)
                for a, dst in ((0, lru_t), (1, lru_i)):
                    act.wait_ge(gate_ps, 2 * b + a + 1)
                    for i in range(LT):
                        ins = act.activation(dst[:, i, :], ps_t[a][:, i * P:(i + 1) * P], ACT.Tanh,
                                             bias=gates_c[:, a * LT + i:a * LT + i + 1], scale=0.5)
                    ins.then_inc(gate_out, 1)
                act.wait_ge(gate_out, 2 * b + 2)
                for i in range(LT):
                    act.activation(lru_a[:, i, :], lru_t[:, i, :], ACT.Exp, bias=lru_c[:, i:i + 1], scale=lru_c[:, i:i + 1])
                for i in range(LT):
                    ins = act.activation(lru_t[:, i, :], lru_t[:, i, :], ACT.Tanh, bias=lru_c[:, LT + i:LT + i + 1],
                                         scale=lru_c[:, LT + i:LT + i + 1])
                ins.then_inc(decay_out, 1)
                pace.part(0.5)
                act.wait_ge(root_in, b + 1)
                act.activation(lru_t.rearrange("p a t -> p (a t)"), lru_t.rearrange("p a t -> p (a t)"), ACT.Sqrt).then_inc(root_out, 1)

            def exp_scores(b, n, buf):
                act.wait_ge(s_max, 12 * b + n + 1)
                keys_n = key_tiles(b) * P
                act.activation(buf[:, 0:keys_n], buf[:, 0:keys_n], ACT.Exp, bias=small[:, 32 + n:33 + n],
                               accum_out=small[:, 48 + n:49 + n]).then_inc(s_exp, 1)

            def out_pT(b, m):
                n = key_tiles(b) // 2
                for g in range(2):
                    act.wait_ge(p_turned, 16 * b + (2 * m + g + 1))
                    copy(pT[:, n * g:n * g + n, :].rearrange("p a t -> p (a t)"), ps_t[g][:, 0:n * P]).then_inc(pT_made, 1)

            def mla(b, h):
                exp_scores(b, h, (e0, e1)[h % 2])
                pace.part(0.4)
                out_pT(b, h)

            def diff(b, h):
                exp_scores(b, 4 + 2 * h, e0)
                pace.part(0.2)
                exp_scores(b, 5 + 2 * h, e1)
                pace.part(0.65)
                out_pT(b, 4 + h)

            def queries(b, n):
                for g in range(2):
                    pace.part((g + 1) / 2)
                    act.wait_ge(w_used, products(b, (50, 82)[n] + 8 * (g + 1)))
                    copy(feat_a[:, g * 512:(g + 1) * 512], ps_p[g][:, :], CROSS_SCALE if n == 0 else 1.0).then_inc(q_out, 1)

            def cross_scores(b):
                act.wait_ge(c_max, b + 1)
                for h in range(CROSS_H):
                    ins = act.activation(e0[:, h * MEM:(h + 1) * MEM], ps_s[:, h * MEM:(h + 1) * MEM], ACT.Exp,
                                         bias=small[:, 64 + h:65 + h], accum_out=small[:, 68 + h:69 + h])
                ins.then_inc(c_exp, 1)

            def cross_mix(b):
                pace.part(0.6)
                for g in range(2):
                    act.wait_ge(c_turned, 2 * b + g + 1)
                    copy(pT[:, 4 * g:4 * g + 4, :].rearrange("p a t -> p (a t)"), ps_t[g][:, :]).then_inc(c_pT, 1)
                pace.part(1)
                for g in range(2):
                    act.wait_ge(co_ps, 2 * b + g + 1)
                    copy(feat_b[:, g * 512:(g + 1) * 512], ps_p[g][:, :]).then_inc(co_out, 1)

            def peer_scores(b):
                for g in range(2):
                    act.wait_ge(k_ps, 2 * b + g + 1)
                    copy((e0, e1)[g][:, :], ps_s[:, :]).then_inc(k_out, 1)

            def choose(b):
                pace.part(0.5)
                act.wait_ge(g_arg, b + 1)
                act.activation(g_next[:, :], g_next[:, :], ACT.Exp).then_inc(g_exp, 1)

            front = {
                "norm_mix": lambda b: square_x(b, 0), "project_0": project_0, "project_1": project_1, "project_2": project_2,
                "project_3": project_3, "project_4": project_4, "mla_up": mla_up, "gates": gates,
                "norm_cross": lambda b: square_x(b, 1), "cross_q": lambda b: queries(b, 0), "cross_scores": cross_scores,
                "cross_mix": cross_mix, "norm_ffn": lambda b: square_x(b, 2), "peer_q": lambda b: queries(b, 1),
                "peer_scores": peer_scores, "choose": choose,
            }
            for h in range(4):
                front[f"mla_{h}"] = lambda b, h=h: mla(b, h)
                front[f"diff_{h}"] = lambda b, h=h: diff(b, h)

            def position(bp, p):
                if p % STEP == STEP - 1 and p < EXPERTS:
                    s = p // STEP
                    act.wait_ge(u_used, bp * EXPERTS + (G_RING + (s + 1) * STEP))
                    act.activation(acts[:, s * STEP:(s + 1) * STEP], dots[:, s * STEP:(s + 1) * STEP], ACT.Gelu).then_inc(acts_made, 1)
                j = p - DIAG_LAG
                if 0 <= j < EXPERTS:
                    if j % STEP == 0:
                        act.wait_ge(coef_made, bp * STEPS + (j // STEP + 1))
                    act.wait_ge(v_used, bp * EXPERTS + (j + G_RING - 3))
                    act.activation(diag[:, j % 4, :], ident[:, :], ACT.Copy, scale=coef[:, j:j + 1]).then_inc(diag_made, 1)

            def finish(bp):
                act.wait_ge(fin_sum, bp + 1)
                act.activation(e0[:, :], x_cur[:, :], ACT.Square, accum_out=out_stat[:, 0:1]).then_inc(fin_sq, 1)

            pace = Pace(position)
            pace.run(front, 0)
            with act.Fori(1, NB) as b:
                pace.start(b - 1)
                pace.run(front, b)
                pace.to(END)
                finish(b - 1)
            pace.start(NB - 1)
            pace.to(END)
            finish(NB - 1)

        @block.vector
        def _(dve):
            steps = Steps(dve_step)
            scores_waited, keys_waited, top_waited = (counter(dve, n) for n in ("scores_waited", "keys_waited", "top_waited"))

            def run(ins):
                steps.run(dve, ins)

            def rsqrt(y, v, t):
                run(dve.tensor_scalar(t.bitcast(I32), v.bitcast(I32), 1, None, ALU.logical_shift_right))
                run(dve.tensor_scalar(y.bitcast(I32), t.bitcast(I32), -1.0, float(0x5F3759DF), ALU.mult, ALU.add))
                for _ in range(3):
                    run(dve.scalar_tensor_tensor(t, y, -0.5, y, ALU.mult, ALU.mult))
                    run(dve.tensor_tensor(t, t, v, ALU.mult))
                    run(dve.scalar_tensor_tensor(y, t, 1.5, y, ALU.add, ALU.mult))

            dve.memset(ones[:, :], 1.0).then_inc(ones_made, 1)
            dve.wait_ge(cols_in, 16)
            for t in range(MT):
                dve.wait_ge(pre["square"], t + 1)
                run(dve.tensor_scalar(small[:, 2:3], small[:, t:t + 1], 1.0 / D, EPS, ALU.mult, ALU.add))
                rsqrt(small[:, 3:4], small[:, 2:3], small[:, 4:5])
                dve.tensor_scalar((e0, e1)[t][:, :], (e0, e1)[t][:, :], small[:, 3:4], None, ALU.mult).then_inc(pre["xs"], 1)
                for g in range(2):
                    dve.wait_ge(pre["turned"], 2 * t + g + 1)
                    dve.tensor_tensor(mem_t[:, 4 * g:4 * g + 4, t * P:(t + 1) * P], ps_t[g][:, :].rearrange("p (a t) -> p a t", a=4),
                                      bc(col("mem", 4 * g, 4).unsqueeze(2), [P, 4, P]), ALU.mult).then_inc(pre["memT"], 1)
            run(dve.tensor_scalar(gates_c[:, 0:2 * LT], col("gate_b", 0, 2 * LT), 0.5, None, ALU.mult))
            lam4, neg4, e4, s4, q4, r4 = (small[:, 8 + LT * i:8 + LT * (i + 1)] for i in (0, 2, 1, 3, 4, 5))
            run(dve.tensor_scalar(neg4, col("lam", 0, LT), -1.0, None, ALU.mult))
            dve.tensor_tensor(lam4, col("lam", 0, LT), neg4, ALU.max).then_inc(pre["abs"], 1)
            dve.wait_ge(pre["exp"], 1)
            run(dve.tensor_scalar(s4, e4, 2.0, None, ALU.add))
            run(dve.reciprocal(q4, s4))
            run(dve.tensor_tensor(s4, e4, q4, ALU.mult))
            run(dve.tensor_tensor(q4, s4, s4, ALU.mult))
            run(dve.tensor_scalar(r4, q4, 1.0 / 17, 1.0 / 15, ALU.mult, ALU.add))
            for n in (13, 11, 9, 7, 5, 3, 1):
                run(dve.tensor_tensor(r4, r4, q4, ALU.mult))
                run(dve.tensor_scalar(r4, r4, 1.0 / n, None, ALU.add))
            run(dve.scalar_tensor_tensor(r4, r4, 2.0, s4, ALU.mult, ALU.mult))
            run(dve.scalar_tensor_tensor(r4, neg4, 0.0, r4, ALU.max, ALU.add))
            run(dve.tensor_scalar(lru_c[:, 0:LT], r4, -4.0, None, ALU.mult))
            run(dve.tensor_scalar(lru_c[:, LT:2 * LT], r4, 4.0, None, ALU.mult))
            dve.wait_ge(rows_in, 32)
            dl, out_scratch = g_cur[:, 0:4 * DK], e1
            for i in range(2):
                ins = dve.tensor_tensor_reduce(out_scratch[:, 32 * i:32 * i + 32], dl[:, 2 * i * DK:(2 * i + 1) * DK],
                                               dl[:, (2 * i + 1) * DK:(2 * i + 2) * DK], 1.0, 0.0, ALU.mult, ALU.add, lam_t[:, i:i + 1])
            ins.then_inc(pre["lamsum"], 1)
            dve.wait_ge(pre["lamexp"], 1)
            run(dve.tensor_tensor(lam_t[:, 4:5], lam_t[:, 3:4], lam_t[:, 2:3], ALU.subtract))
            run(dve.tensor_scalar(lam_t[:, 5:6], lam_t[:, 4:5], LAM_INIT, None, ALU.subtract))
            dve.tensor_tensor(steps_t[:, :], table[:, DIFF_H:], table[:, 0:(BUCKETS - 1) * DIFF_H], ALU.subtract).then_inc(pre["steps"], 1)
            dve.wait_ge(pos_in, 32)
            pos_k = rows[:, 11, :]
            run(dve.tensor_copy(pos_q[:, :], pos_i[:, :]))
            run(dve.tensor_copy(rows[:, 12, :], pos_k.bitcast(I32)))
            pos_k = rows[:, 12, :]
            run(dve.tensor_tensor(rows[:, 11, 0:SEQ - 1], pos_k[:, 1:], pos_k[:, 0:SEQ - 1], ALU.subtract))
            run(dve.tensor_scalar(rows[:, 11, 0:SEQ - 1], rows[:, 11, 0:SEQ - 1], 1.0, None, ALU.not_equal))
            run(dve.tensor_reduce(small[:, 5:6], rows[:, 11, 0:SEQ - 1], AX_X, ALU.max))
            run(dve.tensor_copy(flag[:, :], small[:, 5:6]))
            dve.nop().then_inc(pre["flag"], 1)
            r = slice(NOPE, NOPE + ROPE)
            angle, turns = rows[r, 11, :], e0[r, :]
            run(dve.tensor_scalar(angle, pos_k[r, :], cols[r, COL["freq"]:COL["freq"] + 1], None, ALU.mult))
            for c, t in enumerate((x_cur[r, :], h_cur[r, :])):
                run(dve.tensor_scalar(turns, angle, 1.0 / (2 * math.pi), 0.25 if c == 0 else 0.0, ALU.mult, ALU.add))
                run(dve.tensor_scalar(turns, turns, ROUND, None, ALU.add))
                run(dve.tensor_scalar(turns, turns, ROUND, None, ALU.subtract))
                run(dve.scalar_tensor_tensor(t, turns, -TWO_PI_A, angle, ALU.mult, ALU.add))
                run(dve.scalar_tensor_tensor(t, turns, -TWO_PI_B, t, ALU.mult, ALU.add))
                run(dve.scalar_tensor_tensor(t, turns, -TWO_PI_C, t, ALU.mult, ALU.add))
                if c == 0:
                    run(dve.tensor_scalar(t, t, math.pi / 2, None, ALU.add))
                pi = float(np.nextafter(np.float32(math.pi), np.float32(0)))
                run(dve.tensor_scalar(t, t, pi, -pi, ALU.min, ALU.max))
                dve.nop().then_inc(pre["rope_arg"], 1)

            dve.wait_ge(consts_made, 3)
            run(dve.tensor_copy(iota_f[:, :], iota_i[:, :]))
            jumps = dve.alloc_register("jumps_dve")
            dve.reg_load(jumps, flag[0:1, 0:1])
            with dve.If_eq(jumps, 0):
                near_steps = Steps(near_step)
                reached = hT[:, 0:2, :].rearrange("p a t -> p (a t)")
                dst = [band[h][:, near:SEQ] for h in range(VECTOR_HEADS)]
                dve.wait_ge(pre["gaps"], 1)
                for h in range(VECTOR_HEADS):
                    near_steps.note(dve.tensor_scalar(dst[h], dist, 0.0, table[:, h:h + 1], ALU.mult, ALU.add))
                near_steps.settle(dve)
                for j, start in enumerate(bucket_starts()):
                    near_steps.run(dve, dve.tensor_scalar(reached, dist, start, None, ALU.is_ge))
                    for h in range(VECTOR_HEADS):
                        near_steps.note(dve.scalar_tensor_tensor(dst[h], reached, steps_t[:, j * DIFF_H + h:j * DIFF_H + h + 1], dst[h],
                                                                 ALU.mult, ALU.add))
                    near_steps.settle(dve)
                for h in range(VECTOR_HEADS):
                    dve.tensor_tensor(dst[h], dst[h], hidden, ALU.add).then_inc(pre["near"], 1)
            with dve.Else():
                dve.nop()
            dve.nop()

            def norm(b, n, gain):
                pace.part(0.3)
                dve.wait_ge(squared, 3 * b + n + 1)
                run(dve.tensor_scalar(small[:, 4:5], small[:, n:n + 1], 1.0 / D, EPS, ALU.mult, ALU.add))
                rsqrt(small[:, 5:6], small[:, 4:5], small[:, 6:7])
                dve.tensor_scalar(xs[:, :], x_next[:, :], small[:, 5:6], None, ALU.mult).then_inc(scaled, 1)
                pace.part(0.7)
                for g in range(2):
                    dve.wait_ge(turned, 6 * b + 2 * n + g + 1)
                    dve.tensor_tensor(hT[:, 4 * g:4 * g + 4, :], ps_t[g][:, :].rearrange("p (a t) -> p a t", a=4),
                                      bc(col(gain, 4 * g, 4).unsqueeze(2), [P, 4, P]), ALU.mult).then_inc(hT_made, 1)

            def latents(b):
                dve.wait_ge(proj_out[0], b + 1)
                dve.tensor_tensor(pT[:, 0:3, :], latent, latent, ALU.mult).then_inc(lat_sq, 1)
                pace.part(0.7)
                dve.wait_ge(lat_sum, b + 1)
                steps.note(dve.tensor_scalar(pT[:, 3, :], ps_t[0][:, 0:P], 1.0 / Q_RANK, EPS, ALU.mult, ALU.add))
                run(dve.tensor_scalar(pT[:, 4, :], ps_t[0][:, P:2 * P], 1.0 / KV_RANK, EPS, ALU.mult, ALU.add))
                flat = pT[:, :, :].rearrange("p a t -> p (a t)")
                rsqrt(flat[:, 5 * P:7 * P], flat[:, 3 * P:5 * P], flat[:, 0:2 * P])
                dve.scalar_tensor_tensor(latent_n[:, 0, :], latent[:, 0, :], col("qn", 0), pT[:, 5, :], ALU.mult, ALU.mult)
                dve.scalar_tensor_tensor(latent_n[0:64, 1, :], latent[0:64, 1, :], col("qn", 1)[0:64, :], pT[0:64, 5, :],
                                         ALU.mult, ALU.mult)
                dve.scalar_tensor_tensor(latent_n[:, 2, :], latent[:, 2, :], col("kvn"), pT[:, 6, :], ALU.mult, ALU.mult)\
                   .then_inc(lat_n, 1)

            def mla_up(b):
                rr = slice(NOPE, NOPE + ROPE)
                dve.wait_ge(rope_landed, 16 * b + 16)
                steps.note(dve.tensor_tensor(pT[rr, 3, :], latent[rr, 1, :], rope_t[rr, 0, :], ALU.mult))
                run(dve.tensor_tensor(pT[rr, 4, :], k_swap[rr, :], rope_t[rr, 1, :], ALU.mult))
                dve.tensor_tensor(k_mla[rr, :, bass.ds(b * P, P)], bc(pT[rr, 3:4, :], [ROPE, MLA_H, P]),
                                  bc(pT[rr, 4:5, :], [ROPE, MLA_H, P]), ALU.add).then_inc(k_rope, 1)
                cos, sin = (bc(rope_t[rr, c:c + 1, :], [ROPE, MLA_H, P]) for c in range(2))
                straight = e1[rr, 512:1024].rearrange("p (a t) -> p a t", a=MLA_H)
                swapped = e1[rr, 0:512].rearrange("p (a t) -> p a t", a=MLA_H)
                dve.wait_ge(up_q, b + 1)
                steps.note(dve.scalar_tensor_tensor(straight, ps_p[1][rr, :].rearrange("p (a t) -> p a t", a=MLA_H), MLA_SCALE, cos,
                                                    ALU.mult, ALU.mult))
                dve.wait_ge(q_swap, b + 1)
                run(dve.scalar_tensor_tensor(swapped, swapped, MLA_SCALE, sin, ALU.mult, ALU.mult))
                dve.tensor_tensor(q_mla[rr, :, :], straight, swapped, ALU.add).then_inc(q_rope, 1)

            def conv(b):
                dve.wait_ge(proj_out[2], b + 1)
                for i in range(LT):
                    steps.note(dve.tensor_scalar(lru_x[:, i, :], conv_in[:, i, 0:P], col("conv_w", i), col("conv_b", i),
                                                 ALU.mult, ALU.add))
                for k in range(1, CONV_W):
                    steps.settle(dve)
                    for i in range(LT):
                        steps.note(dve.scalar_tensor_tensor(lru_x[:, i, :], conv_in[:, i, k:k + P], col("conv_w", k * LT + i),
                                                            lru_x[:, i, :], ALU.mult, ALU.add))
                dve.tensor_copy(conv_in[:, :, 0:CONV_W - 1], conv_in[:, :, P:P + CONV_W - 1]).then_inc(conv_done, 1)

            def gates(b):
                dve.wait_ge(gate_out, 2 * b + 2)
                run(dve.scalar_tensor_tensor(lru_i, lru_i, 1.0, lru_x, ALU.add, ALU.mult))
                pace.part(0.3)
                dve.wait_ge(decay_out, b + 1)
                run(dve.tensor_tensor(lru_x, lru_a, lru_a, ALU.mult))
                dve.scalar_tensor_tensor(lru_t, lru_x, 1.0, lru_t, ALU.add, ALU.mult).then_inc(root_in, 1)
                pace.part(0.7)
                dve.wait_ge(root_out, b + 1)
                run(dve.scalar_tensor_tensor(lru_i, lru_i, 0.5, lru_t, ALU.mult, ALU.mult))
                for i in range(LT):
                    steps.note(dve.tensor_tensor_scan(lru_x[:, i, :], lru_a[:, i, :], lru_i[:, i, :], h_last[:, i:i + 1],
                                                      ALU.mult, ALU.add))
                steps.settle(dve)
                steps.note(dve.tensor_copy(h_last[:, :], lru_x[:, :, P - 1]))
                dve.wait_ge(proj_out[3], b + 1)
                run(dve.tensor_tensor(lru_i, lru_x, gelu_g, ALU.mult))
                dve.tensor_tensor(lru_t, lru_i, lru_i, ALU.mult).then_inc(lru_sq, 1)

            def recur(b):
                pace.part(0.8)
                dve.wait_ge(lru_sum, b + 1)
                run(dve.tensor_scalar(lru_a[:, 0, :], ps_t[0][:, 0:P], 1.0 / LRU_W, EPS, ALU.mult, ALU.add))
                rsqrt(lru_a[:, 1, :], lru_a[:, 0, :], lru_a[:, 2, :])
                for i in range(LT):
                    ins = dve.scalar_tensor_tensor(hT[:, 2 + i, :], lru_i[:, i, :], col("yn", 2 + i), lru_a[:, 1, :], ALU.mult, ALU.mult)
                ins.then_inc(lru_done, 1)
                dve.wait_ge(lru_done, b + 1)

            def masked_max(b, n, buf):
                wait_more(dve, s_ps, scores_waited, 1)
                keys_n = key_tiles(b) * P
                run(dve.tensor_tensor_reduce(buf[:, 0:keys_n], ps_s[:, 0:keys_n], bias_t[:, 0:keys_n], 1.0, -3.0e38, ALU.add, ALU.max,
                                             small[:, 16 + n:17 + n]))
                dve.tensor_scalar(small[:, 32 + n:33 + n], small[:, 16 + n:17 + n], -1.0, None, ALU.mult).then_inc(s_max, 1)

            def mla(b, h):
                if h == 0:
                    dve.wait_ge(bias_landed, 80 * b + 16)
                if h >= 2:
                    dve.wait_ge(p_turned, 16 * b + 2 * (h - 1))
                masked_max(b, h, (e0, e1)[h % 2])
                if h == MLA_H - 1:
                    dve.nop().then_inc(bias_used, 1)

            def diff(b, h):
                dve.wait_ge(bias_landed, 80 * b + 16 * (h + 2))
                dve.wait_ge(p_turned, 16 * b + 2 * (4 + h))
                masked_max(b, 4 + 2 * h, e0)
                pace.part(0.2)
                masked_max(b, 5 + 2 * h, e1)
                dve.nop().then_inc(bias_used, 1)
                pace.part(0.45)
                dve.wait_ge(s_exp, 12 * b + 6 + 2 * h)
                run(dve.reciprocal(small[:, 72:74], small[:, 52 + 2 * h:54 + 2 * h]))
                run(dve.tensor_scalar(small[:, 74:75], small[:, 73:74], lam_t[:, 5:6], None, ALU.mult))
                keys_n = key_tiles(b) * P
                run(dve.tensor_scalar(e1[:, 0:keys_n], e1[:, 0:keys_n], small[:, 74:75], None, ALU.mult))
                dve.scalar_tensor_tensor(e0[:, 0:keys_n], e0[:, 0:keys_n], small[:, 72:73], e1[:, 0:keys_n], ALU.mult, ALU.add)\
                   .then_inc(w_done, 1)

            def join(b):
                dve.wait_ge(pv_ps, 8 * b + 8)
                run(dve.reciprocal(small[:, 76:80], small[:, 48:52]))
                for h in range(MLA_H):
                    steps.note(dve.tensor_scalar(xs[:, h * MLA_V:(h + 1) * MLA_V], ps_p[0][:, h * MLA_V:(h + 1) * MLA_V],
                                                 small[:, 76 + h:77 + h], None, ALU.mult))
                run(dve.tensor_copy(xs[:, 512:768], ps_p[1][:, 0:256]))
                steps.note(dve.tensor_tensor_reduce(xs[:, 256:512], xs[:, 0:256], xs[:, 0:256], 1.0, 0.0, ALU.mult, ALU.add,
                                                    small[:, 84:85]))
                run(dve.tensor_tensor(xs[:, 768:1024], xs[:, 512:768], xs[:, 512:768], ALU.mult))
                run(dve.tensor_reduce(small[:, 85:89], xs[:, 768:1024].rearrange("p (h c) -> p h c", h=DIFF_H), AX_X, ALU.add))
                steps.note(dve.tensor_scalar(small[:, 90:91], small[:, 84:85], 1.0 / (MLA_H * MLA_V), EPS, ALU.mult, ALU.add))
                run(dve.tensor_scalar(small[:, 91:95], small[:, 85:89], 1.0 / DV, EPS, ALU.mult, ALU.add))
                rsqrt(small[:, 95:100], small[:, 90:95], small[:, 100:105])
                dve.tensor_scalar(xs[:, 0:256], xs[:, 0:256], small[:, 95:96], None, ALU.mult)
                o = xs[:, 512:768].rearrange("p (h c) -> p h c", h=DIFF_H)
                dve.tensor_tensor(o, o, bc(small[:, 96:100].unsqueeze(2), [P, DIFF_H, DV]), ALU.mult).then_inc(y_made, 1)
                dve.wait_ge(y_turned, b + 1)
                t = ps_t[0][:, :].rearrange("p (a t) -> p a t", a=4)
                dve.tensor_tensor(hT[:, 0:2, :], t[:, 0:2, :], bc(col("yn", 0, 2).unsqueeze(2), [P, 2, P]), ALU.mult)
                dve.scalar_tensor_tensor(hT[:, 6:8, :], t[:, 2:4, :], 1.0 - LAM_INIT, bc(col("yn", 6, 2).unsqueeze(2), [P, 2, P]),
                                         ALU.mult, ALU.mult).then_inc(yT_made, 1)

            def add_out(b, first):
                for n in range(2):
                    pace.part((n + 1) / 2)
                    dve.wait_ge(w_used, products(b, first + KT * (n + 1)))
                    dve.tensor_tensor(x_next[:, n * 512:(n + 1) * 512], x_next[:, n * 512:(n + 1) * 512],
                                      ps_s[:, n * 512:(n + 1) * 512], ALU.add).then_inc(out_added, 1)

            def cross_scores(b):
                dve.wait_ge(c_ps, b + 1)
                run(dve.tensor_reduce(small[:, 60:64], ps_s[:, :].rearrange("p (h m) -> p h m", h=CROSS_H), AX_X, ALU.max))
                dve.tensor_scalar(small[:, 64:68], small[:, 60:64], -1.0, None, ALU.mult).then_inc(c_max, 1)

            def cross_mix(b):
                pace.part(0.1)
                dve.wait_ge(c_exp, b + 1)
                run(dve.reciprocal(small[:, 80:84], small[:, 68:72]))
                for h in range(CROSS_H):
                    ins = dve.tensor_scalar(e0[:, h * MEM:(h + 1) * MEM], e0[:, h * MEM:(h + 1) * MEM], small[:, 80 + h:81 + h], None,
                                            ALU.mult)
                ins.then_inc(c_norm, 1)

            def top16(values, indices, sources, share0, share1):
                n = len(sources)
                for first in (0, 8):
                    pace.part(share0 + (share1 - share0) * first / 16)
                    for v, s in zip(values, sources):
                        dve.max(v[:, first:first + 8], s).then_inc(top_step, 1)
                    pace.part(share0 + (share1 - share0) * (first + 4) / 16)
                    wait_more(dve, top_step, top_waited, n)
                    for v, i, s in zip(values, indices, sources):
                        dve.max_index(i[:, first:first + 8], v[:, first:first + 8], s).then_inc(top_step, 1)
                        if first == 0:
                            dve.match_replace(s, v[:, 0:8], s, -3.0e38).then_inc(top_step, 1)
                    wait_more(dve, top_step, top_waited, 2 * n if first == 0 else n)

            def top(b, g):
                pace.part(0.2)
                wait_more(dve, k_out, keys_waited, 1)
                at = range(8 * g, 8 * g + 8)
                top16([top_v[:, a, :] for a in at], [top_i[:, a, :] for a in at],
                      [(e0, e1)[g][:, k * NKEYS:(k + 1) * NKEYS] for k in range(8)], 0.2, 1.0)

            def choose(b):
                halves = [e[:, :].rearrange("p (h i j) -> p h i j", h=4, i=TOPK) for e in (e0, e1)]
                wide = [P, 4, TOPK, TOPK]
                tv = top_v[:, :, :].rearrange("p (h c) k -> p h c k", c=2)
                run(dve.tensor_copy(top_f[:, :, :], top_i[:, :, :]))
                tf = top_f[:, :, :].rearrange("p (h c) k -> p h c k", c=2)
                for g in range(2):
                    hs = slice(4 * g, 4 * g + 4)
                    dve.tensor_tensor(halves[g], bc(tv[:, hs, 0, :].unsqueeze(3), wide), bc(tv[:, hs, 1, :].unsqueeze(2), wide),
                                      ALU.add).then_inc(top_step, 1)
                wait_more(dve, top_step, top_waited, 2)
                top16([best_v[:, h, :] for h in range(HEADS)], [best_i[:, h, :] for h in range(HEADS)],
                      [(e0, e1)[h // 4][:, (h % 4) * 256:(h % 4 + 1) * 256] for h in range(HEADS)], 0.05, 0.5)
                g3 = g_next[:, :].rearrange("p (h k) -> p h k", h=HEADS)
                dve.tensor_tensor(g3, best_v[:, :, :], bc(best_v[:, :, 0:1], [P, HEADS, TOPK]), ALU.subtract).then_inc(g_arg, 1)
                flat_i = best_i[:, :, :].rearrange("p h k -> p (h k)")
                steps.note(dve.tensor_scalar(pick_i[:, 0, :], flat_i, 4, None, ALU.logical_shift_right))
                run(dve.tensor_scalar(pick_i[:, 1, :], flat_i, TOPK - 1, None, ALU.bitwise_and))
                run(dve.tensor_copy(pick[:, 0:2, :], pick_i[:, :, :]))
                for c in range(2):
                    pace.part(0.5 + 0.25 * c)
                    place = pick[:, c, :].rearrange("p (h k) -> p h k", h=HEADS)
                    found = pick[:, 2 + c, :].rearrange("p (h k) -> p h k", h=HEADS)
                    for g in range(2):
                        hs = slice(4 * g, 4 * g + 4)
                        steps.note(dve.tensor_tensor(halves[g], bc(place[:, hs, :].unsqueeze(3), wide),
                                                     bc(iota_f[:, :].unsqueeze(1).unsqueeze(1), wide), ALU.is_equal))
                    pace.part(0.58 + 0.25 * c)
                    steps.settle(dve)
                    for g in range(2):
                        hs = slice(4 * g, 4 * g + 4)
                        steps.note(dve.tensor_tensor(halves[g], halves[g], bc(tf[:, hs, c, :].unsqueeze(2), wide), ALU.mult))
                    pace.part(0.66 + 0.25 * c)
                    steps.settle(dve)
                    for g in range(2):
                        hs = slice(4 * g, 4 * g + 4)
                        steps.note(dve.tensor_reduce(found[:, hs, :], halves[g], AX_X, ALU.add))
                    steps.settle(dve)
                run(dve.scalar_tensor_tensor(ids_next[:, :], pick[:, 2, :], float(NKEYS), pick[:, 3, :], ALU.mult, ALU.add))
                dve.wait_ge(g_exp, b + 1)
                run(dve.tensor_reduce(small[:, 106:106 + HEADS], g3, AX_X, ALU.add))
                run(dve.reciprocal(small[:, 114:114 + HEADS], small[:, 106:106 + HEADS]))
                run(dve.tensor_tensor(g3, g3, bc(small[:, 114:114 + HEADS].unsqueeze(2), [P, HEADS, TOPK]), ALU.mult))

            def hand_ids(b):
                if isinstance(b, int):
                    dve.wait_ge(pre["rope_stored"], 32)
                dve.wait_ge(u_used, b * EXPERTS + G_RING)
                dve.tensor_copy(ids_u[:, :], ids_next[:, :]).then_inc(ids_handed, 1)
                dve.tensor_tensor(h_cur[:, :], xs[:, :], ffn_row[:, :], ALU.mult).then_inc(handed, 1)
                dve.wait_ge(handed, b + 1)

            def hand_over(b):
                dve.wait_ge(v_used, b * EXPERTS + G_RING)
                dve.tensor_copy(ids_v[:, :], ids_next[:, :]).then_inc(v_ids_handed, 1)
                ge(dve, coef_made, b * STEPS)
                steps.note(dve.tensor_copy(g_cur[:, :], g_next[:, :]))
                ge(dve, fin_stored, 16 * b)
                dve.tensor_copy(x_cur[:, :], x_next[:, :]).then_inc(x_handed, 1)
                dve.wait_ge(x_handed, b + 1)
                dve.wait_ge(v_ids_handed, b + 1)
                steps.settle(dve)

            front = {
                "norm_mix": lambda b: norm(b, 0, "mix"), "latents": latents, "mla_up": mla_up, "conv": conv, "gates": gates,
                "recur": recur, "join": join, "mix_out": lambda b: add_out(b, 34), "norm_cross": lambda b: norm(b, 1, "cross"),
                "cross_scores": cross_scores, "cross_mix": cross_mix, "cross_out": lambda b: add_out(b, 66),
                "norm_ffn": lambda b: norm(b, 2, "ffn"), "top_0": lambda b: top(b, 0), "top_1": lambda b: top(b, 1),
                "choose": choose,
            }
            for h in range(4):
                front[f"mla_{h}"] = lambda b, h=h: mla(b, h)
                front[f"diff_{h}"] = lambda b, h=h: diff(b, h)

            def multiply_row(bp, p):
                dve.wait_ge(u_landed[p % G_RING], bp * (16 * EXPERTS // G_RING) + 16 * (p // G_RING + 1))
                row = u_rows[:, p % G_RING, :]
                dve.tensor_tensor_reduce(row, row, h_cur[:, :], 1.0, 0.0, ALU.mult, ALU.add, dots[:, p:p + 1]).then_inc(u_used, 1)

            def position(bp, p):
                if EARLY <= p < EXPERTS:
                    multiply_row(bp, p)
                if EXPERTS <= p < EXPERTS + EARLY and not isinstance(bp, int):
                    multiply_row(bp + 1, p - EXPERTS)
                done = p - GATE_LAG
                if done >= STEP and done % STEP == 0 and done <= EXPERTS:
                    s = done // STEP - 1
                    dve.wait_ge(acts_made, bp * STEPS + s + 1)
                    a = slice(s * STEP, (s + 1) * STEP)
                    dve.tensor_tensor(coef[:, a], g_cur[:, a], acts[:, a], ALU.mult).then_inc(coef_made, 1)

            def finish(bp):
                dve.wait_ge(v_used, bp * EXPERTS + (EXPERTS + G_RING))
                dve.tensor_tensor(x_cur[:, :], x_cur[:, :], ps_sum[:, :], ALU.add).then_inc(fin_sum, 1)
                dve.wait_ge(fin_sq, bp + 1)
                run(dve.tensor_scalar(out_stat[:, 1:2], out_stat[:, 0:1], 1.0 / D, EPS, ALU.mult, ALU.add))
                rsqrt(out_stat[:, 2:3], out_stat[:, 1:2], out_stat[:, 3:4])
                dve.scalar_tensor_tensor(x_cur[:, :], x_cur[:, :], out_stat[:, 2:3], final_row[:, :], ALU.mult, ALU.mult)\
                   .then_inc(fin_made, 1)

            dve.wait_ge(consts_in, 96)
            dve.wait_ge(consts_made, 9)
            dve.nop().then_inc(u_used, G_RING)
            pace = Pace(position)
            prologue_steps = steps.n
            pace.run(front, 0)
            hand_ids(0)
            for p in range(EARLY):
                multiply_row(0, p)
            hand_over(0)
            first_steps = steps.n - prologue_steps
            finish_steps = 12
            with dve.Fori(1, NB) as b:
                steps.start(b * (first_steps + finish_steps) + (prologue_steps - finish_steps))
                pace.start(b - 1)
                pace.run(front, b)
                hand_ids(b)
                pace.to(END)
                finish(b - 1)
                hand_over(b)
                assert steps.n == first_steps + finish_steps, (steps.n, first_steps)
            pace.start(NB - 1)
            steps.start(prologue_steps + NB * first_steps + (NB - 1) * finish_steps)
            pace.to(END)
            finish(NB - 1)


def kernel(x, mem, positions, rel_bias, norm_mix, w_in, mla_q_norm, mla_w_uq, mla_kv_norm, mla_w_ukv, lru_conv_w, lru_conv_b,
           lru_w_a, lru_b_a, lru_w_x, lru_b_x, lru_lambda, diff_lambda, diff_norm, out_norm_mla, out_norm_lru, w_out,
           norm_cross, norm_mem, w_cq, w_ckv, w_co, norm_ffn, peer_w_q, peer_keys, peer_u, peer_v, norm_final):
    import concourse.bacc as bacc
    from concourse.bass_utils import run_bass_kernel_spmd

    A = np.asarray

    def column_slices(w):
        n = w.shape[1] // P
        return w.reshape(2, 4, P, n, P).transpose(3, 0, 2, 1, 4).reshape(2 * n, P, HALF)

    def row_slices(w):
        return w.reshape(KT, P, 2, HALF).transpose(2, 0, 1, 3).reshape(2 * KT, P, HALF)

    def swapped(w):
        return np.concatenate([w[..., ROPE // 2:], w[..., :ROPE // 2]], axis=-1)

    w = A(w_in)[0]
    at = np.cumsum([0, Q_RANK, KV_RANK, ROPE, LRU_W, LRU_W, 256, 256, 256])
    c_q, c_kv, k_r, x_l, g_l, q_d, k_d, v_d = (w[:, at[i]:at[i + 1]] for i in range(8))
    w_in_own = np.concatenate([c_q, k_r, swapped(k_r), c_kv, q_d, k_d, x_l, g_l, v_d], axis=1)
    ckv = A(w_ckv)[0]
    wstream = np.concatenate([column_slices(ckv[:, :D]), row_slices(ckv[:, D:]), column_slices(w_in_own), row_slices(A(w_out)[0]),
                              column_slices(A(w_cq)[0]), row_slices(A(w_co)[0]), column_slices(A(peer_w_q)[0])])

    columns = np.zeros((P, N_COLS), np.float32)

    def put(name, a, rows=P):
        a = A(a).reshape(-1, rows).T
        columns[0:rows, COL[name]:COL[name] + a.shape[1]] = a

    for name, a in (("mix", norm_mix), ("cross", norm_cross), ("mem", norm_mem), ("ffn", norm_ffn), ("kvn", mla_kv_norm),
                    ("conv_w", lru_conv_w), ("conv_b", lru_conv_b), ("lam", lru_lambda)):
        put(name, a)
    columns[:, COL["qn"]] = A(mla_q_norm)[0, 0:P]
    columns[0:Q_RANK - P, COL["qn"] + 1] = A(mla_q_norm)[0, P:]
    dn = A(diff_norm)[0]
    put("yn", np.concatenate([A(out_norm_mla)[0], A(out_norm_lru)[0], dn, dn, dn, dn]))
    put("gate_b", np.concatenate([A(lru_b_a).reshape(-1), A(lru_b_x).reshape(-1)]))
    freq = np.float32(ROPE_THETA) ** (-np.arange(0, ROPE, 2, dtype=np.float32) / np.float32(ROPE))
    columns[NOPE:NOPE + ROPE, COL["freq"]] = np.concatenate([freq, freq])
    columns[NOPE:NOPE + ROPE, COL["sign"]] = np.repeat(np.float32([-1, 1]), ROPE // 2)

    uq = A(mla_w_uq)[0].reshape(Q_RANK, MLA_H, NOPE + ROPE)
    uq = np.concatenate([uq, swapped(uq[:, :, NOPE:])], axis=2).reshape(Q_RANK, MLA_H * P)
    w_uq = np.zeros((P, 2, MLA_H * P), np.float32)
    w_uq[:, 0] = uq[0:P]
    w_uq[0:Q_RANK - P, 1] = uq[P:]
    ukv = A(mla_w_ukv)[0].reshape(KV_RANK, MLA_H, 2, NOPE)
    w_ukv = ukv.transpose(0, 2, 1, 3).reshape(KV_RANK, 2, MLA_H * NOPE)
    w_gates = np.zeros((P, 2, LT, P), np.float32)
    for a, g in enumerate((A(lru_w_a)[0], A(lru_w_x)[0])):
        for i in range(LRU_W // LRU_G):
            r = (i % 2) * LRU_G
            w_gates[r:r + LRU_G, a, i // 2, r:r + LRU_G] = g[i]
    pk = A(peer_keys)[0]
    keys_t = np.zeros((P, 2 * NKEYS), np.float32)
    keys_t[0:64, 0:NKEYS] = pk[0].T
    keys_t[64:128, NKEYS:] = pk[1].T

    ins = {
        "x": A(x)[0], "wstream": wstream, "columns": columns, "w_uq": w_uq, "w_ukv": w_ukv, "w_gates": w_gates, "keys_t": keys_t,
        "ffn_gain": A(norm_ffn)[0], "final_gain": A(norm_final), "mem": A(mem)[0], "positions": A(positions)[0],
        "pos_cols": A(positions)[0].reshape(NB, P).T,
        "rel_bias": A(rel_bias).reshape(-1), "diff_lambda": A(diff_lambda)[0].reshape(-1), "peer_u": A(peer_u)[0],
        "peer_v": A(peer_v)[0],
    }
    ins = {k: np.ascontiguousarray(v) for k, v in ins.items()}
    nc = bacc.Bacc("TRN2", target_bir_lowering=False, num_devices=1)
    aps = {k: nc.dram_tensor("in_" + k, v.shape, mybir.dt.from_np(v.dtype), kind="ExternalInput").ap() for k, v in ins.items()}
    out = nc.dram_tensor("out", (SEQ, D), F32, kind="ExternalOutput").ap()
    program(nc, *aps.values(), out)
    r = run_bass_kernel_spmd(nc, [{"in_" + k: v for k, v in ins.items()}], core_ids=[0])
    return r.results[0]["out"].reshape(1, SEQ, D)
```

```python
import math
from contextlib import ExitStack

import concourse.bass as bass
import numpy as np
from concourse import mybir

F32 = mybir.dt.float32
I32 = mybir.dt.int32
U32 = mybir.dt.uint32
ALU = mybir.AluOpType
ACT = mybir.ActivationFunctionType
AX_X = mybir.AxisListType.X

P = 128
D = 1024
KT = D // P
SEQ = 1024
NB = SEQ // P
MEM = 256
MT = MEM // P
EPS = 1e-6
NEG = -1e30

MLA_H, NOPE, ROPE, MLA_V = 4, 64, 32, 64
Q_RANK, KV_RANK = 192, 128
MLA_SCALE = 1.0 / math.sqrt(NOPE + ROPE)
ROPE_THETA = 10000.0
LRU_W, LRU_G, CONV_W = 512, 64, 4
LT = LRU_W // P
DIFF_H, DK, DV = 4, 32, 64
DIFF_SCALE = 1.0 / math.sqrt(DK)
LAM_INIT = 0.8 - 0.6 * math.exp(-0.3 * 0)
CROSS_H = 4
CROSS_SCALE = 1.0 / math.sqrt(D // CROSS_H)
BUCKETS, MAX_DIST = 32, 128
HEADS, NKEYS, TOPK = 8, 128, 16
EXPERTS = HEADS * TOPK

HALF = 512
VECTOR_HEADS = 3
W_RING = 7
G_RING = 8
STEP = 8
STEPS = EXPERTS // STEP
IN_TILES = 17
MEM_SLICES = 4 * KT
BLOCK_SLICES = 2 * (IN_TILES + 4 * KT)
W_SHIFT = (-MEM_SLICES) % W_RING
BAND = 2 * SEQ - P

_COLS = [("mix", KT), ("cross", KT), ("mem", KT), ("ffn", KT), ("qn", 2), ("kvn", 1), ("yn", KT), ("conv_w", CONV_W * LT),
         ("conv_b", LT), ("gate_b", 2 * LT), ("lam", LT), ("freq", 1), ("sign", 1)]
COL, N_COLS = {}, 0
for _name, _n in _COLS:
    COL[_name] = N_COLS
    N_COLS += _n


def bucket_starts():
    exact = BUCKETS // 2
    out = [float(j) for j in range(1, exact + 1)]
    for j in range(1, BUCKETS - exact):
        out.append(float(math.ceil(exact * (MAX_DIST / exact) ** (j / (BUCKETS - exact)))))
    return out


TWO_PI_A = 6.28125
TWO_PI_B = float(np.float32(np.round((2 * math.pi - TWO_PI_A) * 2 ** 21) / 2 ** 21))
TWO_PI_C = 2 * math.pi - TWO_PI_A - TWO_PI_B
ROUND = 1.5 * 2.0 ** 23

PIECES = [("norm_mix", 1.5), ("project_0", 3.9), ("project_1", 5.9), ("project_2", 4.2), ("latents", 0.9),
          ("project_3", 4.2), ("project_4", 2.4), ("mla_up", 1.5), ("conv", 0.8), ("gates", 2.8), ("recur", 2.1),
          ("mla_0", 3.8), ("mla_1", 3.4), ("mla_2", 2.6), ("mla_3", 2.4), ("diff_0", 3.9), ("diff_1", 4.4),
          ("diff_2", 4.5), ("diff_3", 4.4), ("join", 1.4), ("mix_out", 8.9), ("norm_cross", 1.5), ("cross_q", 8.5),
          ("cross_scores", 0.8), ("cross_mix", 1.5), ("cross_out", 8.9), ("norm_ffn", 1.5), ("peer_q", 8.5),
          ("peer_scores", 1.5), ("top_0", 3.9), ("choose_0", 7.5), ("top_1", 5.0), ("choose_1", 9.0)]
FRONT_END = EXPERTS


def on_vector(j):
    return j % SHARE == SHARE - 1


def sum_index(j):
    return j - j // SHARE


def spans():
    total, done, out = sum(n for _, n in PIECES), 0, []
    for name, n in PIECES:
        out.append((name, FRONT_END * done / total, FRONT_END * (done + n) / total))
        done += n
    return out


LOOPS = [(1, 4, 4), (4, 6, 6), (6, NB, NB)]

GATE_LAG = 1
DIAG_LAG = STEP + 2
SUM_LAG = STEP + 3
GATHER_LAG = STEP + 4
SHARE = 8
SUM_ROWS = EXPERTS - EXPERTS // SHARE
SUM_SLOTS = G_RING - G_RING // SHARE
FIRST = EXPERTS // 2
EARLY = G_RING
END = EXPERTS + SUM_LAG


def program(nc, x, wstream, columns, w_uq, w_ukv, w_gates, keys_t, ffn_gain, final_gain, mem, positions, pos_cols,
            rel_bias, diff_lambda, peer_u, peer_v, out):
    with ExitStack() as ctx:
        def sb(name, shape, dt=F32):
            return ctx.enter_context(nc.sbuf_tensor(name, shape, dt))

        def pb(name, cols):
            return ctx.enter_context(nc.psum_tensor(name, [P, cols], F32))

        def sem(name):
            return ctx.enter_context(nc.semaphore(name))

        rows = sb("rows", [P, 2 * G_RING, D])
        u_rows, v_rows = rows[:, 0:G_RING, :], rows[:, G_RING:2 * G_RING, :]
        w_ring = sb("w_ring", [P, W_RING, HALF])
        ident = sb("ident", [P, P])
        ones = sb("ones", [P, P])
        cols = sb("cols", [P, N_COLS])
        ffn_row = sb("ffn_row", [P, D])
        wuq = sb("wuq", [P, 2, MLA_H * P])
        wukv = sb("wukv", [P, 2, MLA_H * NOPE])
        wgate = sb("wgate", [P, 2, LT, P])
        keys = sb("keys", [P, 2 * NKEYS])
        mem_k = sb("mem_k", [P, KT, MEM])
        mem_v = sb("mem_v", [P, MT, D])
        k_mla = sb("k_mla", [NOPE + ROPE, MLA_H, SEQ])
        v_mla = sb("v_mla", [P, NB, MLA_H * MLA_V])
        k_diff = sb("k_diff", [P, 2, SEQ])
        v_diff = sb("v_diff", [P, NB, DIFF_H * DV])
        x_next = sb("x_next", [P, D])
        x_cur = sb("x_cur", [P, D])
        h_cur = sb("h_cur", [P, D])
        xs = sb("xs", [P, D])
        hT = sb("hT", [P, KT, P])
        e0 = sb("e0", [P, D])
        e1 = sb("e1", [P, D])
        pT = sb("pT", [P, KT, P])
        bias_t = sb("bias_t", [P, 2, SEQ])
        x_in = bias_t[:, 1, :]
        feat_a = sb("feat_a", [P, KT * P])
        feat_b = sb("feat_b", [P, KT * P])
        conv_in = sb("conv_in", [P, LT, P + CONV_W - 1])
        rope_t = sb("rope_t", [NOPE + ROPE, 2, P])
        k_swap = sb("k_swap", [NOPE + ROPE, P])
        h_last = sb("h_last", [P, LT])
        small = sb("small", [P, 128])
        gates_c = sb("gates_c", [P, 2 * LT])
        lru_c = sb("lru_c", [P, 2 * LT])
        lam_t = sb("lam_t", [P, 8])
        pos_i = sb("pos_i", [P, NB], I32)
        pos_q = sb("pos_q", [P, NB])
        flag = sb("flag", [P, 1], I32)
        iota_i = sb("iota_i", [P, TOPK], I32)
        iota_f = sb("iota_f", [P, TOPK])
        ids_u = sb("ids_u", [P, EXPERTS], U32)
        ids_v = sb("ids_v", [P, EXPERTS], U32)
        g_cur = sb("g_cur", [P, EXPERTS])
        dots = sb("dots", [P, EXPERTS])
        acts = sb("acts", [P, EXPERTS])
        coef = acts
        diag = sb("diag", [P, 4, P])
        out_stat = sb("out_stat", [P, 8])

        latent = feat_a[:, 0:3 * P].rearrange("p (a t) -> p a t", a=3)
        latent_n = feat_a[:, 3 * P:6 * P].rearrange("p (a t) -> p a t", a=3)
        q_diff = feat_a[:, 6 * P:8 * P].rearrange("p (a t) -> p a t", a=2)
        q_mla = feat_b[:, 0:4 * P].rearrange("p (a t) -> p a t", a=4)
        gelu_g = feat_b[:, 4 * P:8 * P].rearrange("p (a t) -> p a t", a=4)
        feat_q = feat_a[:, :].rearrange("p (a t) -> p a t", a=KT)
        cross_oT = feat_b[:, :].rearrange("p (a t) -> p a t", a=KT)
        lru_x = e0[:, 0:512].rearrange("p (a t) -> p a t", a=LT)
        lru_a = e0[:, 512:1024].rearrange("p (a t) -> p a t", a=LT)
        lru_t = e1[:, 0:512].rearrange("p (a t) -> p a t", a=LT)
        lru_i = e1[:, 512:1024].rearrange("p (a t) -> p a t", a=LT)
        table = dots[:, 0:BUCKETS * DIFF_H]
        steps_t = acts[:, 0:(BUCKETS - 1) * DIFF_H]
        top_v = feat_b[:, 0:256].rearrange("p (a k) -> p a k", k=TOPK)
        top_i = feat_b[:, 256:512].bitcast(U32).rearrange("p (a k) -> p a k", k=TOPK)
        top_f = feat_b[:, 512:768].rearrange("p (a k) -> p a k", k=TOPK)
        best_v = feat_b[:, 768:896].rearrange("p (a k) -> p a k", k=TOPK)
        best_i = feat_b[:, 896:1024].bitcast(U32).rearrange("p (a k) -> p a k", k=TOPK)
        pick = pT[:, 0:4, :]
        pick_i = pT[:, 4:6, :].bitcast(U32)
        ids_next, g_next = pT[:, 6, :].bitcast(U32), pT[:, 7, :]
        mem_t = rows[:, 14:16, :].rearrange("p a (k m) -> p (a k) m", m=MEM)

        near = SEQ - 2 * P
        band = [rows[:, 2 * h:2 * h + 2, :].rearrange("p a c -> p (a c)") for h in range(DIFF_H + 1)]
        ahead = rows[:, 13, :]
        gap, dist, hidden = ahead[:, 0:256], ahead[:, 256:512], ahead[:, 512:768]

        ps_sum = pb("ps_sum", D)
        ps_p = [pb("ps_p0", 512), pb("ps_p1", 512)]
        ps_s = pb("ps_s", D)
        ps_t = [pb("ps_t0", 512), pb("ps_t1", 512)]

        bias_d = nc.dram_tensor("bias_rows", (DIFF_H + 1, SEQ, BAND), F32, kind="Internal").ap()
        rope_d = nc.dram_tensor("rope_rows", (2, ROPE, SEQ), F32, kind="Internal").ap()

        cols_in, rows_in, pos_in, mem_in = sem("cols_in"), sem("rows_in"), sem("pos_in"), sem("mem_in")
        consts_in = sem("consts_in")
        w_landed = [sem(f"w_landed{i}") for i in range(W_RING)]
        w_used = sem("w_used")
        consts_made = sem("consts_made")
        ones_made = sem("ones_made")
        ahead_made = sem("ahead_made")
        dve_step, act_step, pool_step = sem("dve_step"), sem("act_step"), sem("pool_step")
        band_step, near_step, any_step, top_step = (sem(n) for n in ("band_step", "near_step", "any_step", "top_step"))
        pre = {n: sem("pre_" + n) for n in
               ("square", "xs", "turned", "memT", "k_out", "v_out", "abs", "exp", "lamsum",
                "lamexp", "rope_arg", "rope_done", "rope_stored", "band", "stored", "flag", "steps", "gaps", "near")}
        x_landed, rope_landed = sem("x_landed"), sem("rope_landed")
        bias_landed, bias_used = [sem("bias_landed0"), sem("bias_landed1")], sem("bias_used")
        handed = sem("handed")
        squared, scaled, turned, hT_made = sem("squared"), sem("scaled"), sem("turned"), sem("hT_made")
        proj_out = [sem(f"proj_out{g}") for g in range(5)]
        lat_sq, lat_sum, lat_n = sem("lat_sq"), sem("lat_sum"), sem("lat_n")
        up_q, up_k, up_v, q_swap, q_nope, q_rope, k_rope, kv_out = (sem(n) for n in (
            "up_q", "up_k", "up_v", "q_swap", "q_nope", "q_rope", "k_rope", "kv_out"))
        conv_done, gate_ps, gate_out, decay_out, root_in, root_out = (sem(n) for n in (
            "conv_done", "gate_ps", "gate_out", "decay_out", "root_in", "root_out"))
        lru_sq, lru_sum, lru_done = sem("lru_sq"), sem("lru_sum"), sem("lru_done")
        s_ps, s_max, s_exp, w_done = sem("s_ps"), sem("s_max"), sem("s_exp"), sem("w_done")
        p_turned, pT_made, pv_ps = sem("p_turned"), sem("pT_made"), sem("pv_ps")
        y_made, y_turned, yT_made = sem("y_made"), sem("y_turned"), sem("yT_made")
        out_added = sem("out_added")
        q_out = sem("q_out")
        c_ps, c_max, c_exp, c_norm, c_turned, c_pT, co_ps, co_out = (sem(n) for n in (
            "c_ps", "c_max", "c_exp", "c_norm", "c_turned", "c_pT", "co_ps", "co_out"))
        k_ps, k_out = sem("key_ps"), sem("key_out")
        g_arg, g_exp = sem("g_arg"), sem("g_exp")
        x_copied, gain_landed = sem("x_copied"), sem("gain_landed")
        x_handed, ids_handed, v_ids_handed = sem("x_handed"), sem("ids_handed"), sem("v_ids_handed")
        u_landed = [sem(f"u_landed{i}") for i in range(G_RING)]
        v_landed = [sem(f"v_landed{i}") for i in range(G_RING)]
        u_used, v_used = sem("u_used"), sem("v_used")
        v_added = sem("v_added")
        acts_made, coef_made, diag_made = sem("acts_made"), sem("coef_made"), sem("diag_made")
        fin_sum, fin_sq, fin_made, fin_stored = sem("fin_sum"), sem("fin_sq"), sem("fin_made"), sem("fin_stored")

        class Steps:

            def __init__(self, semaphore):
                self.sem, self.origin, self.n = semaphore, 0, 0

            def start(self, origin):
                self.origin, self.n = origin, 0

            def note(self, ins):
                ins.then_inc(self.sem, 1)
                self.n += 1

            def settle(self, eng):
                eng.wait_ge(self.sem, self.origin + self.n)

            def run(self, eng, ins):
                self.note(ins)
                self.settle(eng)

        def ge(eng, semaphore, value):
            if isinstance(value, int) and value <= 0:
                return
            eng.wait_ge(semaphore, value)

        def bc(ap, shape):
            return ap.broadcast_to(shape)

        def col(name, i=0, n=1):
            return cols[:, COL[name] + i:COL[name] + i + n]

        def products(b, i):
            return b * BLOCK_SLICES + (MEM_SLICES + i)

        class Pace:

            def __init__(self, position):
                self.position, self.at, self.bp = position, 0, None
                self.first = self.last = 0

            def start(self, bp):
                self.at, self.bp = 0, bp

            def to(self, r):
                if self.bp is not None:
                    for p in range(self.at, r):
                        self.position(self.bp, p)
                    self.at = max(self.at, r)

            def part(self, share):
                self.to(int(self.first + share * (self.last - self.first)))

            def run(self, front, b):
                for name, self.first, self.last in spans():
                    if name in front:
                        self.part(0)
                        front[name](b)
                self.to(FRONT_END)

        def counter(eng, name):
            reg = eng.alloc_register(name)
            eng.reg_mov(reg, 0)
            return reg

        wide = [NB]

        def key_tiles(b):
            return 2 if isinstance(b, int) else wide[0]

        def wait_more(eng, semaphore, waited, n):
            eng.wait_ge(semaphore, eng.snap(waited) + n)
            eng.reg_add(waited, waited, n)

        block = ctx.enter_context(nc.Block())

        @block.sync
        def _(sp):
            def load_w(i, n):
                slot = (i + W_SHIFT) % W_RING if isinstance(n, int) and n < MEM_SLICES else (i - MEM_SLICES) % W_RING
                ge(sp, w_used, n - W_RING + 1)
                sp.dma_start(w_ring[:, slot, :], wstream[i]).then_inc(w_landed[slot], 16)

            sp.dma_start(cols[:, :], columns).then_inc(cols_in, 16)
            for t in range(MT):
                sp.dma_start((e0, e1)[t][:, :], mem[t * P:(t + 1) * P, :]).then_inc(mem_in, 16)
            for i in range(W_RING):
                load_w(i, i)
            sp.dma_start(rows[:, 11, :].bitcast(I32), positions.partition_broadcast(P)).then_inc(pos_in, 16)
            sp.dma_start(pos_i[:, :], pos_cols).then_inc(pos_in, 16)
            sp.dma_start(table[:, :], rel_bias.partition_broadcast(P)).then_inc(rows_in, 16)
            sp.dma_start(g_cur[:, 0:4 * DK], diff_lambda.partition_broadcast(P)).then_inc(rows_in, 16)
            sp.dma_start(wuq[:, :, :], w_uq).then_inc(consts_in, 16)
            sp.dma_start(wukv[:, :, :], w_ukv).then_inc(consts_in, 16)
            sp.dma_start(wgate[:, :, :, :], w_gates).then_inc(consts_in, 16)
            sp.dma_start(keys[:, :], keys_t).then_inc(consts_in, 16)
            sp.dma_start(ffn_row[:, :], ffn_gain.partition_broadcast(P)).then_inc(consts_in, 16)
            sp.dma_start(x_in[:, :], x[0:P, :]).then_inc(x_landed, 16)
            for i in range(W_RING, MEM_SLICES):
                load_w(i, i)
            jumps = sp.alloc_register("jumps_sp")
            row_at, col_at, row_step, col_step = (sp.alloc_register(n) for n in ("row_at", "col_at", "row_step", "col_step"))

            def store_rope():
                for c in range(2):
                    sp.wait_ge(pre["rope_done"], c + 1)
                    sp.dma_start(rope_d[c], (x_cur, h_cur)[c][NOPE:NOPE + ROPE, :]).then_inc(pre["rope_stored"], 16)
                sp.wait_ge(pre["rope_stored"], 32)

            def store_mask():
                sp.wait_ge(pre["flag"], 1)
                sp.reg_load(jumps, flag[0:1, 0:1])
                with sp.If_eq(jumps, 0):
                    for reg, value in ((row_at, 0), (col_at, SEQ - P), (row_step, 0), (col_step, P)):
                        sp.reg_mov(reg, value)
                    sp.wait_ge(pre["band"], 1)
                    store_band(DIFF_H, 1)
                with sp.Else():
                    for reg, value in ((row_at, 0), (col_at, 0), (row_step, P), (col_step, 0)):
                        sp.reg_mov(reg, value)
                    with sp.Fori(0, NB) as b:
                        for h in range(DIFF_H + 1):
                            sp.wait_ge(ones_made, 1)
                            sp.wait_ge(pre["band"], b * (DIFF_H + 1) + (h + 1))
                            sp.dma_start(bias_d[h, bass.ds(b * P, P), 0:SEQ], rows[:, h, :]).then_inc(pre["stored"], 16)
                    sp.wait_ge(pre["stored"], 16 * NB * (DIFF_H + 1))
                sp.nop()

            def store_band(h, n):
                sp.dma_start(bias_d[h, 0:P, :], rows[:, 2 * h:2 * h + 2, :].rearrange("p a c -> p (a c)")[:, 0:BAND])\
                  .then_inc(pre["stored"], 16)
                sp.wait_ge(pre["stored"], 16 * n)

            def store_biases():
                with sp.If_eq(jumps, 0):
                    sp.wait_ge(pre["near"], VECTOR_HEADS)
                    sp.wait_ge(pre["band"], 1 + (DIFF_H - VECTOR_HEADS))
                    for h in range(DIFF_H):
                        store_band(h, 2 + h)
                with sp.Else():
                    sp.nop()
                sp.nop()

            def front_loads(b, c0, c1):
                for i in range(c0, c1):
                    load_w(MEM_SLICES + i, MEM_SLICES + b * BLOCK_SLICES + i)

            def load_bias(b, h):
                turn = (h + 1) % (DIFF_H + 1)
                at, left = sp.snap(row_at, min_val=0, max_val=SEQ - P), sp.snap(col_at, min_val=0, max_val=SEQ - P)
                sp.wait_ge(ones_made, 1)
                if turn == 1:
                    sp.wait_ge(x_copied, b + 1)
                else:
                    ge(sp, bias_used, b * (DIFF_H + 1) + max(turn - 1, 0))
                sp.dma_start(bias_t[:, turn % 2, :], bias_d[h, bass.ds(at, P), bass.ds(left, SEQ)]).then_inc(bias_landed[turn % 2], 16)
                if h == DIFF_H - 1:
                    sp.reg_add(row_at, row_at, row_step)
                    sp.reg_sub(col_at, col_at, col_step)

            def load_x(b):
                if isinstance(b, int):
                    return
                sp.wait_ge(ones_made, 1)
                ge(sp, bias_used, b * (DIFF_H + 1) - 1)
                sp.dma_start(x_in[:, :], x[bass.ds(b * P, P), :]).then_inc(x_landed, 16)

            def load_rope(b):
                sp.wait_ge(ones_made, 1)
                ge(sp, q_rope, b)
                ge(sp, k_rope, b)
                sp.dma_start(rope_t[NOPE:NOPE + ROPE, :, :],
                             rope_d[:, :, bass.ds(b * P, P)].rearrange("c r t -> r c t")).then_inc(rope_landed, 16)

            per_tile = 2
            w_at = {"project_0": (0, 3), "project_1": (3, 7), "project_2": (7, 11), "project_3": (11, 15),
                    "project_4": (15, 17), "mix_out": (17, 25), "cross_q": (25, 33), "cross_out": (33, 41),
                    "peer_q": (41, 49)}
            ahead_slices = W_RING
            front = {n: (lambda b, r=r: front_loads(b, per_tile * r[0], per_tile * r[1])) for n, r in w_at.items()}
            front["norm_mix"] = load_x

            def project_3(b):
                front_loads(b, per_tile * 11, per_tile * 15)
                if isinstance(b, int):
                    store_rope()
                load_rope(b)

            def project_4(b):
                front_loads(b, per_tile * 15, per_tile * 17)
                if isinstance(b, int):
                    store_mask()
                load_bias(b, DIFF_H)
                front_loads(b, per_tile * 17, per_tile * 17 + ahead_slices)
                if not isinstance(b, int):
                    load_bias(b, 0)

            def mix_out(b):
                front_loads(b, per_tile * 17 + ahead_slices, per_tile * 25)

            def diff_0(b):
                if isinstance(b, int):
                    store_biases()
                    load_bias(b, 0)
                load_bias(b, 1)

            front["project_3"], front["project_4"], front["diff_0"], front["mix_out"] = project_3, project_4, diff_0, mix_out
            for h in range(2, DIFF_H):
                front[f"diff_{h - 1}"] = lambda b, h=h: load_bias(b, h)

            def load_gain(b):
                sp.wait_ge(ones_made, 1)
                sp.wait_ge(ids_handed, 2 * b + 2)
                sp.dma_start(e1[:, :], final_gain.partition_broadcast(P)).then_inc(gain_landed, 16)

            pace = Pace(None)
            pace.run(front, 0)
            with sp.Fori(1, NB) as b:
                pace.run(front, b)
                load_gain(b)
            sp.wait_ge(fin_stored, 16 * NB)

        @block.gpsimd
        def _(pool):
            pool.memset(ident[:, :], 0.0).then_inc(pool_step, 1)
            pool.iota(iota_i[:, :], [[1, TOPK]], base=0, channel_multiplier=0).then_inc(consts_made, 1)
            pool.iota(rows[:, 13, :].bitcast(I32), [[1, SEQ]], base=0, channel_multiplier=-1).then_inc(consts_made, 1)
            pool.wait_ge(pool_step, 1)
            pool.affine_select(out=ident[:, :], in_=ident[:, :], compare_op=ALU.not_equal, fill=1.0, base=0,
                               pattern=[[-1, P]], channel_multiplier=1).then_inc(consts_made, 1)
            for t in (k_mla, v_mla, k_diff, v_diff, conv_in, h_last):
                pool.memset(t[tuple(slice(None) for _ in t.shape)], 0.0).then_inc(consts_made, 1)

            u_waited, v_waited, v_added_waited, ids_waited, v_ids_waited = (counter(pool, n) for n in (
                "u_waited", "v_waited", "v_added_waited", "ids_waited", "v_ids_waited"))

            def gather_u(j):
                wait_more(pool, u_used, u_waited, 1)
                pool.indirect_dma_start(u_rows[:, j % G_RING, :], None, peer_u,
                                        bass.IndirectOffsetOnAxis(ap=ids_u[:, j:j + 1], axis=0)).then_inc(u_landed[j % G_RING], 16)

            def gather_v(j):
                if on_vector(j):
                    wait_more(pool, v_added, v_added_waited, 1)
                else:
                    wait_more(pool, v_used, v_waited, 1)
                pool.indirect_dma_start(v_rows[:, j % G_RING, :], None, peer_v,
                                        bass.IndirectOffsetOnAxis(ap=ids_v[:, j:j + 1], axis=0)).then_inc(v_landed[j % G_RING], 16)

            def retrieve(more):
                wait_more(pool, ids_handed, ids_waited, 1)
                for i in range(G_RING, EXPERTS):
                    gather_u(i)
                    if i == GATHER_LAG:
                        wait_more(pool, v_ids_handed, v_ids_waited, 1)
                    if i >= GATHER_LAG:
                        gather_v(i - GATHER_LAG)
                for j in range(EXPERTS - GATHER_LAG, EXPERTS):
                    k = j - (EXPERTS - GATHER_LAG)
                    if more and k == 0:
                        wait_more(pool, ids_handed, ids_waited, 1)
                    if more and k < G_RING:
                        gather_u(k)
                    gather_v(j)

            def bias_of(add, wait, dist, mask, dst, heads):
                for d, h in zip(dst, heads):
                    add(pool.tensor_scalar(d, dist, 0.0, table[:, h:h + 1], ALU.mult, ALU.add))
                wait()
                for j, start in enumerate(bucket_starts()):
                    for m, h in zip(mask, heads):
                        add(pool.tensor_scalar(m, dist, start, steps_t[:, j * DIFF_H + h:j * DIFF_H + h + 1], ALU.is_ge, ALU.mult))
                    wait()
                    for m, d in zip(mask, dst):
                        add(pool.tensor_tensor(d, d, m, ALU.add))
                    wait()

            pool.wait_ge(consts_made, 3)
            pool.tensor_copy(ahead, ahead.bitcast(I32)).then_inc(ahead_made, 1)
            pool.wait_ge(ahead_made, 1)
            pool.wait_ge(pre["steps"], 1)
            pool.wait_ge(pre["flag"], 1)
            jumps = pool.alloc_register("jumps_pool")
            pool.reg_load(jumps, flag[0:1, 0:1])
            with pool.If_eq(jumps, 0):
                band_steps = Steps(band_step)
                mask = [rows[:, 10, h * 256:(h + 1) * 256] for h in range(DIFF_H)]
                band_steps.run(pool, pool.tensor_scalar(gap, ahead[:, 0:256], -1.0, float(P), ALU.mult, ALU.add))
                band_steps.note(pool.tensor_scalar(hidden, gap, 0.0, NEG, ALU.is_lt, ALU.mult))
                for h in range(DIFF_H + 1):
                    band_steps.note(pool.memset(band[h][:, 0:SEQ], 0.0))
                    band_steps.note(pool.memset(band[h][:, SEQ:BAND], NEG))
                band_steps.run(pool, pool.tensor_scalar(dist, gap, 0.0, None, ALU.max))
                pool.tensor_tensor(band[DIFF_H][:, near:SEQ], band[DIFF_H][:, near:SEQ], hidden, ALU.add).then_inc(pre["band"], 1)
                pool.wait_ge(pre["band"], 1)
                pool.nop().then_inc(pre["gaps"], 1)
                for h in range(DIFF_H):
                    last = (BUCKETS - 1) * DIFF_H + h
                    band_steps.note(pool.tensor_scalar(band[h][:, 0:near], band[h][:, 0:near], 0.0, table[:, last:last + 1],
                                                       ALU.mult, ALU.add))
                own = range(VECTOR_HEADS, DIFF_H)
                bias_of(band_steps.note, lambda: band_steps.settle(pool), dist, mask, [band[h][:, near:SEQ] for h in own], own)
                for h in own:
                    pool.tensor_tensor(band[h][:, near:SEQ], band[h][:, near:SEQ], hidden, ALU.add).then_inc(pre["band"], 1)
                pool.wait_ge(pre["stored"], 16 * (DIFF_H + 1))
            with pool.Else():
                dist_any, hidden_any = rows[:, 5, :], rows[:, 11, :]
                mask = [rows[:, 6 + h, :] for h in range(DIFF_H)]
                tiles = [rows[:, h, :] for h in range(DIFF_H + 1)]
                first_ahead, own = lam_t[:, 6:7], lam_t[:, 7:8]
                any_waited, noted = counter(pool, "any_waited"), [0]

                def add(ins):
                    ins.then_inc(any_step, 1)
                    noted[0] += 1

                def wait():
                    wait_more(pool, any_step, any_waited, noted[0])
                    noted[0] = 0

                stored_waited = counter(pool, "stored_waited")
                pool.wait_ge(pre["rope_done"], 2)
                pool.memset(first_ahead, 0.0).then_inc(any_step, 1)
                wait_more(pool, any_step, any_waited, 1)
                with pool.Fori(0, NB) as b:
                    add(pool.tensor_copy(own, pos_q[:, bass.ds(b, 1)]))
                    wait()
                    add(pool.tensor_scalar(dist_any, rows[:, 12, :], own, -1.0, ALU.subtract, ALU.mult))
                    wait()
                    add(pool.tensor_scalar(dist_any, dist_any, 0.0, None, ALU.max))
                    add(pool.memset(tiles[DIFF_H], 0.0))
                    wait()
                    bias_of(add, wait, dist_any, mask, tiles[0:DIFF_H], range(DIFF_H))
                    add(pool.tensor_scalar(hidden_any, ahead, first_ahead, NEG, ALU.is_gt, ALU.mult))
                    wait()
                    add(pool.tensor_scalar(first_ahead, first_ahead, float(P), None, ALU.add))
                    wait()
                    for h in range(DIFF_H + 1):
                        pool.tensor_tensor(tiles[h], tiles[h], hidden_any, ALU.add).then_inc(pre["band"], 1)
                    wait_more(pool, pre["stored"], stored_waited, 16 * (DIFF_H + 1))
            pool.nop()
            pool.wait_ge(pre["rope_done"], 2)
            pool.wait_ge(pre["v_out"], 4)
            wait_more(pool, ids_handed, ids_waited, 1)
            for k in range(G_RING):
                gather_u(k)
            with pool.Fori(0, NB - 1):
                retrieve(True)
            retrieve(False)
            u_last, v_last, v_added_last = pool.snap(u_waited), pool.snap(v_waited), pool.snap(v_added_waited)
            pool.wait_ge(u_used, u_last)
            pool.wait_ge(v_used, v_last)
            pool.wait_ge(v_added, v_added_last)

        @block.tensor
        def _(pe):
            def mem_slice(i):
                slot = (i + W_SHIFT) % W_RING
                before = sum(1 for j in range(i) if (j + W_SHIFT) % W_RING == slot)
                pe.wait_ge(w_landed[slot], 16 * (before + 1))
                return w_ring[:, slot, :]

            uses0 = [sum(1 for j in range(MEM_SLICES) if (j + W_SHIFT) % W_RING == s) for s in range(W_RING)]

            def block_slice(b, i):
                slot = i % W_RING
                pe.wait_ge(w_landed[slot], 16 * (BLOCK_SLICES // W_RING) * b + 16 * (uses0[slot] + i // W_RING + 1))
                return w_ring[:, slot, :]

            pe.wait_ge(consts_made, 3)
            for t in range(MT):
                pe.wait_ge(pre["xs"], t + 1)
                for g in range(2):
                    if t:
                        pe.wait_ge(pre["memT"], 2 * (t - 1) + g + 1)
                    for k in range(4):
                        ins = pe.transpose(ps_t[g][:, k * P:(k + 1) * P], (e0, e1)[t][:, (4 * g + k) * P:(4 * g + k + 1) * P], ident[:, :])
                    ins.then_inc(pre["turned"], 1)
            pe.wait_ge(pre["memT"], 2 * MT)
            for f in range(KT):
                if f >= 4 and f % 2 == 0:
                    pe.wait_ge(pre["k_out"], f // 2 - 1)
                for half in range(2):
                    w = mem_slice(2 * f + half).rearrange("p (k c) -> p k c", k=4)
                    for k in range(4):
                        kt = 4 * half + k
                        ins = pe.matmul(ps_p[(f // 2) % 2][:, (f % 2) * MEM:(f % 2 + 1) * MEM], w[:, k, :], mem_t[:, kt, :],
                                        start=(kt == 0), stop=(kt == KT - 1))
                    ins.then_inc(w_used, 1)
            for n in range(2):
                if n:
                    pe.wait_ge(pre["v_out"], 2)
                for kt in range(KT):
                    w = mem_slice(2 * KT + n * KT + kt)
                    for t in range(MT):
                        ins = pe.matmul(ps_s[:, t * 512:(t + 1) * 512], mem_t[:, kt, t * P:(t + 1) * P], w,
                                        start=(kt == 0), stop=(kt == KT - 1), skip_group_check=True)
                    ins.then_inc(w_used, 1)

            def turn_x(b, n):
                pace.part(0.6)
                pe.wait_ge(scaled, 3 * b + n + 1)
                for g in range(2):
                    for k in range(4):
                        ins = pe.transpose(ps_t[g][:, k * P:(k + 1) * P], xs[:, (4 * g + k) * P:(4 * g + k + 1) * P], ident[:, :])
                    ins.then_inc(turned, 1)

            def col_tile(b, i, dst):
                for half in range(2):
                    w = block_slice(b, 2 * i + half).rearrange("p (k c) -> p k c", k=4)
                    for k in range(4):
                        kt = 4 * half + k
                        ins = pe.matmul(dst, w[:, k, :], hT[:, kt, :], start=(kt == 0), stop=(kt == KT - 1))
                    ins.then_inc(w_used, 1)

            def project(b, g, first, n):
                if g == 0:
                    pe.wait_ge(hT_made, 6 * b + 2)
                if g >= 2:
                    pe.wait_ge(proj_out[g - 2], b + 1)
                for i in range(n):
                    pace.part(i / n)
                    dst = ps_p[g % 2][:, i * P:(i + 1) * P]
                    if g < 4:
                        col_tile(b, first + i, dst)
                    else:
                        for half in range(2):
                            w = block_slice(b, 2 * (first + i) + half).rearrange("p (k c) -> p k c", k=4)
                            for k in range(4):
                                kt = 4 * half + k
                                ins = pe.matmul(dst, hT[:, kt, :], w[:, k, :], start=(kt == 0), stop=(kt == KT - 1))
                            ins.then_inc(w_used, 1)

            def latents(b):
                pe.wait_ge(lat_sq, b + 1)
                sq = pT
                pe.matmul(ps_t[0][:, 0:P], ones[:, :], sq[:, 0, :], start=True, stop=False)
                pe.matmul(ps_t[0][:, 0:P], ones[0:64, :], sq[0:64, 1, :], start=False, stop=True)
                pe.matmul(ps_t[0][:, P:2 * P], ones[:, :], sq[:, 2, :], start=True, stop=True).then_inc(lat_sum, 1)

            def mla_up(b):
                pe.wait_ge(lat_n, b + 1)
                pe.wait_ge(proj_out[3], b + 1)
                for h in range(MLA_H):
                    dst = ps_p[1][:, h * P:(h + 1) * P]
                    pe.matmul(dst, wuq[:, 0, h * P:(h + 1) * P], latent_n[:, 0, :], start=True, stop=False)
                    ins = pe.matmul(dst, wuq[0:64, 1, h * P:(h + 1) * P], latent_n[0:64, 1, :], start=False, stop=True)
                ins.then_inc(up_q, 1)
                pe.wait_ge(proj_out[4], b + 1)
                for h in range(MLA_H):
                    ins = pe.matmul(ps_p[0][0:NOPE, h * P:(h + 1) * P], wukv[:, 0, h * NOPE:(h + 1) * NOPE], latent_n[:, 2, :],
                                    start=True, stop=True)
                ins.then_inc(up_k, 1)
                pe.matmul(ps_t[1][:, 0:MLA_H * MLA_V], latent_n[:, 2, :], wukv[:, 1, :], start=True, stop=True).then_inc(up_v, 1)

            def gates(b):
                pace.part(0.1)
                pe.wait_ge(conv_done, b + 1)
                pe.wait_ge(kv_out, 2 * b + 2)
                for a in range(2):
                    for i in range(LT):
                        ins = pe.matmul(ps_t[a][:, i * P:(i + 1) * P], wgate[:, a, i, :], lru_x[:, i, :], start=True, stop=True)
                    ins.then_inc(gate_ps, 1)

            def recur(b):
                pace.part(0.5)
                pe.wait_ge(lru_sq, b + 1)
                for i in range(LT):
                    ins = pe.matmul(ps_t[0][:, 0:P], ones[:, :], lru_t[:, i, :], start=(i == 0), stop=(i == LT - 1))
                ins.then_inc(lru_sum, 1)

            def turn_p(b, src):
                n = key_tiles(b) // 2
                for g in range(2):
                    for k in range(n):
                        ins = pe.transpose(ps_t[g][:, k * P:(k + 1) * P], src[:, (n * g + k) * P:(n * g + k + 1) * P], ident[:, :])
                    ins.then_inc(p_turned, 1)

            def key_spans(b):
                n = key_tiles(b) * P
                return [(c, min(c + 512, n)) for c in range(0, n, 512)]

            def scores(b, n):
                ge(pe, s_max, 12 * b + n)
                for c0, c1 in key_spans(b):
                    if n < MLA_H:
                        ins = pe.matmul(ps_s[:, c0:c1], q_mla[0:NOPE + ROPE, n, :], k_mla[:, n, c0:c1], start=True, stop=True)
                    else:
                        half = n - MLA_H
                        r = DK * (half % 4)
                        ins = pe.matmul(ps_s[:, c0:c1], q_diff[r:r + DK, half // 4, :], k_diff[r:r + DK, half // 4, c0:c1],
                                        start=True, stop=True)
                ins.then_inc(s_ps, 1)

            def values(b, m, bank, v, h):
                pe.wait_ge(pT_made, 16 * b + (2 * m + 2))
                for t in range(key_tiles(b)):
                    ins = pe.matmul(bank[:, h * DV:(h + 1) * DV], pT[:, t, :], v[:, t, h * DV:(h + 1) * DV],
                                    start=(t == 0), stop=(t == key_tiles(b) - 1))
                ins.then_inc(pv_ps, 1)

            def mla(b, h):
                if h == 0:
                    pe.wait_ge(q_nope, b + 1)
                    pe.wait_ge(q_rope, b + 1)
                    pe.wait_ge(k_rope, b + 1)
                    pe.wait_ge(kv_out, 2 * b + 2)
                    scores(b, 0)
                scores(b, h + 1)
                pace.part(0.4)
                if h == 0:
                    pe.wait_ge(lru_done, b + 1)
                pe.wait_ge(s_exp, 12 * b + h + 1)
                turn_p(b, (e0, e1)[h % 2])
                pace.part(0.8)
                values(b, h, ps_p[0], v_mla, h)

            def diff(b, h):
                scores(b, 5 + 2 * h)
                pace.part(0.3)
                if h < DIFF_H - 1:
                    scores(b, 6 + 2 * h)
                pace.part(0.6)
                pe.wait_ge(w_done, 4 * b + h + 1)
                turn_p(b, e0)
                pace.part(0.85)
                values(b, MLA_H + h, ps_p[1], v_diff, h)

            def join(b):
                pace.part(0.9)
                pe.wait_ge(y_made, b + 1)
                for k in range(2):
                    pe.transpose(ps_t[0][:, k * P:(k + 1) * P], xs[:, k * P:(k + 1) * P], ident[:, :])
                for k in range(2):
                    ins = pe.transpose(ps_t[0][:, (2 + k) * P:(3 + k) * P], xs[:, 512 + k * P:512 + (k + 1) * P], ident[:, :])
                ins.then_inc(y_turned, 1)

            def row_product(b, first, lhs):
                for n in range(2):
                    for kt in range(KT):
                        pace.part((n * KT + kt) / (2 * KT))
                        w = block_slice(b, first + n * KT + kt)
                        pe.matmul(ps_s[:, n * 512:(n + 1) * 512], lhs[:, kt, :], w, start=(kt == 0), stop=(kt == KT - 1)).then_inc(w_used, 1)

            def mix_out(b):
                pe.wait_ge(yT_made, b + 1)
                row_product(b, 34, hT)

            def queries(b, n, first):
                pe.wait_ge(hT_made, 6 * b + 4 + 2 * n)
                for f in range(KT):
                    pace.part(f / KT)
                    col_tile(b, first + f, ps_p[f // 4][:, (f % 4) * P:(f % 4 + 1) * P])

            def cross_scores(b):
                pe.wait_ge(q_out, 4 * b + 2)
                pe.wait_ge(out_added, 4 * b + 2)
                for h in range(CROSS_H):
                    for j in range(2):
                        ins = pe.matmul(ps_s[:, h * MEM:(h + 1) * MEM], feat_q[:, 2 * h + j, :], mem_k[:, 2 * h + j, :],
                                        start=(j == 0), stop=(j == 1))
                ins.then_inc(c_ps, 1)

            def cross_mix(b):
                pace.part(0.3)
                pe.wait_ge(c_norm, b + 1)
                for g in range(2):
                    for k in range(4):
                        ins = pe.transpose(ps_t[g][:, k * P:(k + 1) * P], e0[:, (4 * g + k) * P:(4 * g + k + 1) * P], ident[:, :])
                    ins.then_inc(c_turned, 1)
                pace.part(0.6)
                pe.wait_ge(c_pT, 2 * b + 2)
                for f in range(KT):
                    for m in range(MT):
                        ins = pe.matmul(ps_p[f // 4][:, (f % 4) * P:(f % 4 + 1) * P], mem_v[:, m, f * P:(f + 1) * P],
                                        pT[:, 2 * (f // 2) + m, :], start=(m == 0), stop=(m == MT - 1))
                    if f % 4 == 3:
                        ins.then_inc(co_ps, 1)

            def cross_out(b):
                pe.wait_ge(co_out, 2 * b + 2)
                row_product(b, 66, cross_oT)

            def peer_scores(b):
                pe.wait_ge(q_out, 4 * b + 4)
                for g in range(2):
                    pe.wait_ge(out_added, 4 * b + 4)
                    if g:
                        pe.wait_ge(k_out, 2 * b + 1)
                    for h in range(4):
                        ins = pe.matmul(ps_s[:, h * 2 * NKEYS:(h + 1) * 2 * NKEYS], feat_q[:, 4 * g + h, :], keys[:, :],
                                        start=True, stop=True)
                    ins.then_inc(k_ps, 1)

            front = {
                "norm_mix": lambda b: turn_x(b, 0), "latents": latents, "mla_up": mla_up, "gates": gates, "recur": recur,
                "join": join, "mix_out": mix_out, "norm_cross": lambda b: turn_x(b, 1),
                "cross_q": lambda b: queries(b, 0, 25), "cross_scores": cross_scores, "cross_mix": cross_mix,
                "cross_out": cross_out, "norm_ffn": lambda b: turn_x(b, 2), "peer_q": lambda b: queries(b, 1, 41),
                "peer_scores": peer_scores,
            }
            for g, (first, n) in enumerate([(0, 3), (3, 4), (7, 4), (11, 4), (15, 2)]):
                front[f"project_{g}"] = lambda b, g=g, first=first, n=n: project(b, g, first, n)
            for h in range(4):
                front[f"mla_{h}"] = lambda b, h=h: mla(b, h)
                front[f"diff_{h}"] = lambda b, h=h: diff(b, h)

            def add_row(bp, p):
                j = p - SUM_LAG
                if j >= 0 and not on_vector(j):
                    n = sum_index(j)
                    pe.wait_ge(diag_made, bp * SUM_ROWS + n + 1)
                    pe.wait_ge(v_landed[j % G_RING], bp * (16 * EXPERTS // G_RING) + 16 * (j // G_RING + 1))
                    if j == 0:
                        ge(pe, fin_sum, bp)
                    for c in range(2):
                        ins = pe.matmul(ps_sum[:, c * 512:(c + 1) * 512], diag[:, n % 4, :], v_rows[:, j % G_RING, c * 512:(c + 1) * 512],
                                        start=(n == 0), stop=(n == SUM_ROWS - 1), skip_group_check=True)
                    ins.then_inc(v_used, 1)

            pace = Pace(add_row)
            pe.nop().then_inc(v_used, SUM_SLOTS)
            pe.wait_ge(consts_in, 80)
            pe.wait_ge(ones_made, 1)
            pace.run(front, 0)
            for first, last, wide[0] in LOOPS:
                with pe.Fori(first, last) as b:
                    pace.start(b - 1)
                    pace.run(front, b)
                    pace.to(END)
            pace.start(NB - 1)
            pace.to(END)

        @block.scalar
        def _(act):
            def copy(dst, src, scale=1.0):
                return act.activation(dst, src, ACT.Copy, scale=scale)

            def square_x(b, n):
                if n == 0:
                    act.wait_ge(x_landed, 16 * b + 16)
                    ge(act, handed, b)
                else:
                    act.wait_ge(out_added, 4 * b + 2 * n)
                act.activation(xs[:, :], (x_in if n == 0 else x_next)[:, :], ACT.Square, accum_out=small[:, n:n + 1]).then_inc(squared, 1)

            for t in range(MT):
                act.wait_ge(mem_in, 16 * MT)
                act.activation(pT[:, :, :].rearrange("p a b -> p (a b)"), (e0, e1)[t][:, :], ACT.Square,
                               accum_out=small[:, t:t + 1]).then_inc(pre["square"], 1)
                act.wait_ge(pre["square"], t + 1)
            def keys_out(f):
                act.wait_ge(w_used, 4 * (f + 1))
                copy(mem_k[:, 2 * f:2 * f + 2, :].rearrange("p a b -> p (a b)"), ps_p[f % 2][:, :]).then_inc(pre["k_out"], 1)

            keys_out(0)
            keys_out(1)
            act.wait_ge(pre["abs"], 1)
            act.activation(small[:, 12:12 + LT], small[:, 8:8 + LT], ACT.Exp, scale=-1.0).then_inc(pre["exp"], 1)
            act.wait_ge(pre["lamsum"], 1)
            act.activation(lam_t[:, 2:4], lam_t[:, 0:2], ACT.Exp).then_inc(pre["lamexp"], 1)
            for c in range(2):
                act.wait_ge(pre["rope_arg"], c + 1)
                t = (x_cur, h_cur)[c][NOPE:NOPE + ROPE, :]
                act.activation(t, t, ACT.Sin).then_inc(act_step, 1)
                act.wait_ge(act_step, c + 1)
                if c == 0:
                    act.nop().then_inc(pre["rope_done"], 1)
                else:
                    act.activation(t, t, ACT.Copy, scale=cols[NOPE:NOPE + ROPE, COL["sign"]:COL["sign"] + 1]).then_inc(pre["rope_done"], 1)
            square_x(0, 0)
            keys_out(2)
            keys_out(3)
            for n in range(2):
                act.wait_ge(w_used, 2 * KT + KT * (n + 1))
                for t in range(MT):
                    copy(mem_v[:, t, n * 512:(n + 1) * 512], ps_s[:, t * 512:(t + 1) * 512]).then_inc(pre["v_out"], 1)

            def project_0(b):
                pace.part(1)
                act.wait_ge(w_used, products(b, 6))
                copy(latent.rearrange("p a t -> p (a t)"), ps_p[0][:, 0:3 * P])
                copy(k_swap[NOPE:NOPE + ROPE, :], ps_p[0][96:128, P:2 * P]).then_inc(proj_out[0], 1)

            def project_1(b):
                pace.part(1)
                act.wait_ge(w_used, products(b, 14))
                copy(q_diff.rearrange("p a t -> p (a t)"), ps_p[1][:, 0:2 * P], DIFF_SCALE)
                copy(k_diff[:, :, bass.ds(b * P, P)], ps_p[1][:, 2 * P:4 * P].rearrange("p (a t) -> p a t", a=2)).then_inc(proj_out[1], 1)

            def project_2(b):
                pace.part(1)
                act.wait_ge(w_used, products(b, 22))
                copy(conv_in[:, :, CONV_W - 1:], ps_p[0][:, :].rearrange("p (a t) -> p a t", a=LT)).then_inc(proj_out[2], 1)

            def project_3(b):
                pace.part(1)
                act.wait_ge(w_used, products(b, 30))
                act.activation(gelu_g.rearrange("p a t -> p (a t)"), ps_p[1][:, :], ACT.Gelu).then_inc(proj_out[3], 1)

            def project_4(b):
                pace.part(1)
                act.wait_ge(w_used, products(b, 34))
                copy(v_diff[:, bass.ds(b, 1), :].rearrange("p a c -> p (a c)"), ps_p[0][:, 0:2 * P]).then_inc(proj_out[4], 1)

            def mla_up(b):
                act.wait_ge(up_q, b + 1)
                copy(e1[NOPE:NOPE + ROPE, 0:512], ps_p[1][96:128, :]).then_inc(q_swap, 1)
                copy(q_mla[0:NOPE, :, :].rearrange("p a t -> p (a t)"), ps_p[1][0:NOPE, :], MLA_SCALE).then_inc(q_nope, 1)
                act.wait_ge(up_k, b + 1)
                copy(k_mla[0:NOPE, :, bass.ds(b * P, P)], ps_p[0][0:NOPE, :].rearrange("p (a t) -> p a t", a=MLA_H)).then_inc(kv_out, 1)
                act.wait_ge(up_v, b + 1)
                copy(v_mla[:, bass.ds(b, 1), :].rearrange("p a c -> p (a c)"), ps_t[1][:, 0:MLA_H * MLA_V]).then_inc(kv_out, 1)

            def gates(b):
                pace.part(0.1)
                act.wait_ge(q_rope, b + 1)
                for a, dst in ((0, lru_t), (1, lru_i)):
                    act.wait_ge(gate_ps, 2 * b + a + 1)
                    for i in range(LT):
                        ins = act.activation(dst[:, i, :], ps_t[a][:, i * P:(i + 1) * P], ACT.Tanh,
                                             bias=gates_c[:, a * LT + i:a * LT + i + 1], scale=0.5)
                    ins.then_inc(gate_out, 1)
                act.wait_ge(gate_out, 2 * b + 2)
                for i in range(LT):
                    act.activation(lru_a[:, i, :], lru_t[:, i, :], ACT.Exp, bias=lru_c[:, i:i + 1], scale=lru_c[:, i:i + 1])
                for i in range(LT):
                    ins = act.activation(lru_t[:, i, :], lru_t[:, i, :], ACT.Tanh, bias=lru_c[:, LT + i:LT + i + 1],
                                         scale=lru_c[:, LT + i:LT + i + 1])
                ins.then_inc(decay_out, 1)
                pace.part(0.5)
                act.wait_ge(root_in, b + 1)
                act.activation(lru_t.rearrange("p a t -> p (a t)"), lru_t.rearrange("p a t -> p (a t)"), ACT.Sqrt).then_inc(root_out, 1)

            def exp_scores(b, n, buf):
                act.wait_ge(s_max, 12 * b + n + 1)
                keys_n = key_tiles(b) * P
                act.activation(buf[:, 0:keys_n], buf[:, 0:keys_n], ACT.Exp, bias=small[:, 32 + n:33 + n],
                               accum_out=small[:, 48 + n:49 + n]).then_inc(s_exp, 1)

            def out_pT(b, m):
                n = key_tiles(b) // 2
                for g in range(2):
                    act.wait_ge(p_turned, 16 * b + (2 * m + g + 1))
                    copy(pT[:, n * g:n * g + n, :].rearrange("p a t -> p (a t)"), ps_t[g][:, 0:n * P]).then_inc(pT_made, 1)

            def mla(b, h):
                for n in ((0, 1), (2,), (3,), ())[h]:
                    exp_scores(b, n, (e0, e1)[n % 2])
                pace.part(0.4)
                out_pT(b, h)

            def diff(b, h):
                exp_scores(b, 4 + 2 * h, e0)
                pace.part(0.2)
                exp_scores(b, 5 + 2 * h, e1)
                pace.part(0.65)
                out_pT(b, 4 + h)

            def queries(b, n):
                for g in range(2):
                    pace.part((g + 1) / 2)
                    act.wait_ge(w_used, products(b, (50, 82)[n] + 8 * (g + 1)))
                    copy(feat_a[:, g * 512:(g + 1) * 512], ps_p[g][:, :], CROSS_SCALE if n == 0 else 1.0).then_inc(q_out, 1)

            def cross_scores(b):
                act.wait_ge(c_max, b + 1)
                for h in range(CROSS_H):
                    ins = act.activation(e0[:, h * MEM:(h + 1) * MEM], ps_s[:, h * MEM:(h + 1) * MEM], ACT.Exp,
                                         bias=small[:, 64 + h:65 + h], accum_out=small[:, 68 + h:69 + h])
                ins.then_inc(c_exp, 1)

            def cross_mix(b):
                pace.part(0.6)
                for g in range(2):
                    act.wait_ge(c_turned, 2 * b + g + 1)
                    copy(pT[:, 4 * g:4 * g + 4, :].rearrange("p a t -> p (a t)"), ps_t[g][:, :]).then_inc(c_pT, 1)
                pace.part(1)
                for g in range(2):
                    act.wait_ge(co_ps, 2 * b + g + 1)
                    copy(feat_b[:, g * 512:(g + 1) * 512], ps_p[g][:, :]).then_inc(co_out, 1)

            def peer_scores(b):
                for g in range(2):
                    act.wait_ge(k_ps, 2 * b + g + 1)
                    copy((e0, e1)[g][:, :], ps_s[:, :]).then_inc(k_out, 1)

            def choose(b):
                pace.part(0.5)
                act.wait_ge(g_arg, b + 1)
                act.activation(g_next[:, :], g_next[:, :], ACT.Exp).then_inc(g_exp, 1)

            front = {
                "norm_mix": lambda b: None if isinstance(b, int) else square_x(b, 0), "project_0": project_0, "project_1": project_1, "project_2": project_2,
                "project_3": project_3, "project_4": project_4, "mla_up": mla_up, "gates": gates,
                "norm_cross": lambda b: square_x(b, 1), "cross_q": lambda b: queries(b, 0), "cross_scores": cross_scores,
                "cross_mix": cross_mix, "norm_ffn": lambda b: square_x(b, 2), "peer_q": lambda b: queries(b, 1),
                "peer_scores": peer_scores, "choose_1": choose,
            }
            for h in range(4):
                front[f"mla_{h}"] = lambda b, h=h: mla(b, h)
                front[f"diff_{h}"] = lambda b, h=h: diff(b, h)

            def position(bp, p):
                if p % STEP == STEP - 1 and p < EXPERTS:
                    s = p // STEP
                    act.wait_ge(u_used, bp * EXPERTS + (G_RING + (s + 1) * STEP))
                    act.activation(acts[:, s * STEP:(s + 1) * STEP], dots[:, s * STEP:(s + 1) * STEP], ACT.Gelu).then_inc(acts_made, 1)
                j = p - DIAG_LAG
                if 0 <= j < EXPERTS and not on_vector(j):
                    n = sum_index(j)
                    if j % STEP == 0:
                        act.wait_ge(coef_made, bp * STEPS + (j // STEP + 1))
                    act.wait_ge(v_used, bp * SUM_ROWS + (n + SUM_SLOTS - 3))
                    act.activation(diag[:, n % 4, :], ident[:, :], ACT.Copy, scale=coef[:, j:j + 1]).then_inc(diag_made, 1)

            def finish(bp):
                act.wait_ge(fin_sum, bp + 1)
                act.activation(e0[:, :], x_cur[:, :], ACT.Square, accum_out=out_stat[:, 0:1]).then_inc(fin_sq, 1)
                act.wait_ge(ones_made, 1)
                act.wait_ge(fin_made, bp + 1)
                act.dma_start(out[bass.ds(bp * P, P), :], x_cur[:, :]).then_inc(fin_stored, 16)

            pace = Pace(position)
            pace.run(front, 0)
            for first, last, wide[0] in LOOPS:
                with act.Fori(first, last) as b:
                    pace.start(b - 1)
                    pace.run(front, b)
                    pace.to(END)
                    finish(b - 1)
            pace.start(NB - 1)
            pace.to(END)
            finish(NB - 1)

        @block.vector
        def _(dve):
            steps = Steps(dve_step)
            scores_waited, keys_waited, top_waited = (counter(dve, n) for n in ("scores_waited", "keys_waited", "top_waited"))

            def run(ins):
                steps.run(dve, ins)

            def rsqrt(y, v, t):
                run(dve.tensor_scalar(t.bitcast(I32), v.bitcast(I32), 1, None, ALU.logical_shift_right))
                run(dve.tensor_scalar(y.bitcast(I32), t.bitcast(I32), -1.0, float(0x5F3759DF), ALU.mult, ALU.add))
                for _ in range(3):
                    run(dve.scalar_tensor_tensor(t, y, -0.5, y, ALU.mult, ALU.mult))
                    run(dve.tensor_tensor(t, t, v, ALU.mult))
                    run(dve.scalar_tensor_tensor(y, t, 1.5, y, ALU.add, ALU.mult))

            dve.memset(ones[:, :], 1.0).then_inc(ones_made, 1)
            dve.wait_ge(cols_in, 16)
            for t in range(MT):
                dve.wait_ge(pre["square"], t + 1)
                run(dve.tensor_scalar(small[:, 2:3], small[:, t:t + 1], 1.0 / D, EPS, ALU.mult, ALU.add))
                rsqrt(small[:, 3:4], small[:, 2:3], small[:, 4:5])
                dve.tensor_scalar((e0, e1)[t][:, :], (e0, e1)[t][:, :], small[:, 3:4], None, ALU.mult).then_inc(pre["xs"], 1)
                for g in range(2):
                    dve.wait_ge(pre["turned"], 2 * t + g + 1)
                    dve.tensor_tensor(mem_t[:, 4 * g:4 * g + 4, t * P:(t + 1) * P], ps_t[g][:, :].rearrange("p (a t) -> p a t", a=4),
                                      bc(col("mem", 4 * g, 4).unsqueeze(2), [P, 4, P]), ALU.mult).then_inc(pre["memT"], 1)
            run(dve.tensor_scalar(gates_c[:, 0:2 * LT], col("gate_b", 0, 2 * LT), 0.5, None, ALU.mult))
            lam4, neg4, e4, s4, q4, r4 = (small[:, 8 + LT * i:8 + LT * (i + 1)] for i in (0, 2, 1, 3, 4, 5))
            run(dve.tensor_scalar(neg4, col("lam", 0, LT), -1.0, None, ALU.mult))
            dve.tensor_tensor(lam4, col("lam", 0, LT), neg4, ALU.max).then_inc(pre["abs"], 1)
            dve.wait_ge(rows_in, 32)
            dl, out_scratch = g_cur[:, 0:4 * DK], e1
            for i in range(2):
                ins = dve.tensor_tensor_reduce(out_scratch[:, 32 * i:32 * i + 32], dl[:, 2 * i * DK:(2 * i + 1) * DK],
                                               dl[:, (2 * i + 1) * DK:(2 * i + 2) * DK], 1.0, 0.0, ALU.mult, ALU.add, lam_t[:, i:i + 1])
            ins.then_inc(pre["lamsum"], 1)
            dve.tensor_tensor(steps_t[:, :], table[:, DIFF_H:], table[:, 0:(BUCKETS - 1) * DIFF_H], ALU.subtract).then_inc(pre["steps"], 1)
            dve.wait_ge(pos_in, 32)
            pos_k = rows[:, 11, :]
            run(dve.tensor_copy(pos_q[:, :], pos_i[:, :]))
            run(dve.tensor_copy(rows[:, 12, :], pos_k.bitcast(I32)))
            pos_k = rows[:, 12, :]
            run(dve.tensor_tensor(rows[:, 11, 0:SEQ - 1], pos_k[:, 1:], pos_k[:, 0:SEQ - 1], ALU.subtract))
            run(dve.tensor_scalar(rows[:, 11, 0:SEQ - 1], rows[:, 11, 0:SEQ - 1], 1.0, None, ALU.not_equal))
            run(dve.tensor_reduce(small[:, 5:6], rows[:, 11, 0:SEQ - 1], AX_X, ALU.max))
            run(dve.tensor_copy(flag[:, :], small[:, 5:6]))
            dve.nop().then_inc(pre["flag"], 1)
            r = slice(NOPE, NOPE + ROPE)
            angle, turns = rows[r, 11, :], e0[r, :]
            run(dve.tensor_scalar(angle, pos_k[r, :], cols[r, COL["freq"]:COL["freq"] + 1], None, ALU.mult))
            for c, t in enumerate((x_cur[r, :], h_cur[r, :])):
                run(dve.tensor_scalar(turns, angle, 1.0 / (2 * math.pi), 0.25 if c == 0 else 0.0, ALU.mult, ALU.add))
                run(dve.tensor_scalar(turns, turns, ROUND, None, ALU.add))
                run(dve.tensor_scalar(turns, turns, ROUND, None, ALU.subtract))
                run(dve.scalar_tensor_tensor(t, turns, -TWO_PI_A, angle, ALU.mult, ALU.add))
                run(dve.scalar_tensor_tensor(t, turns, -TWO_PI_B, t, ALU.mult, ALU.add))
                run(dve.scalar_tensor_tensor(t, turns, -TWO_PI_C, t, ALU.mult, ALU.add))
                if c == 0:
                    run(dve.tensor_scalar(t, t, math.pi / 2, None, ALU.add))
                pi = float(np.nextafter(np.float32(math.pi), np.float32(0)))
                run(dve.tensor_scalar(t, t, pi, -pi, ALU.min, ALU.max))
                dve.nop().then_inc(pre["rope_arg"], 1)

            dve.wait_ge(pre["exp"], 1)
            run(dve.tensor_scalar(s4, e4, 2.0, None, ALU.add))
            run(dve.reciprocal(q4, s4))
            run(dve.tensor_tensor(s4, e4, q4, ALU.mult))
            run(dve.tensor_tensor(q4, s4, s4, ALU.mult))
            run(dve.tensor_scalar(r4, q4, 1.0 / 17, 1.0 / 15, ALU.mult, ALU.add))
            for n in (13, 11, 9, 7, 5, 3, 1):
                run(dve.tensor_tensor(r4, r4, q4, ALU.mult))
                run(dve.tensor_scalar(r4, r4, 1.0 / n, None, ALU.add))
            run(dve.scalar_tensor_tensor(r4, r4, 2.0, s4, ALU.mult, ALU.mult))
            run(dve.scalar_tensor_tensor(r4, neg4, 0.0, r4, ALU.max, ALU.add))
            run(dve.tensor_scalar(lru_c[:, 0:LT], r4, -4.0, None, ALU.mult))
            run(dve.tensor_scalar(lru_c[:, LT:2 * LT], r4, 4.0, None, ALU.mult))
            dve.wait_ge(pre["lamexp"], 1)
            run(dve.tensor_tensor(lam_t[:, 4:5], lam_t[:, 3:4], lam_t[:, 2:3], ALU.subtract))
            run(dve.tensor_scalar(lam_t[:, 5:6], lam_t[:, 4:5], LAM_INIT, None, ALU.subtract))
            dve.wait_ge(consts_made, 3)
            run(dve.tensor_copy(iota_f[:, :], iota_i[:, :]))
            jumps = dve.alloc_register("jumps_dve")
            dve.reg_load(jumps, flag[0:1, 0:1])
            near_steps = Steps(near_step)

            def near_biases(heads):
                with dve.If_eq(jumps, 0):
                    reached = e0[:, 0:2 * P]
                    dst = {h: band[h][:, near:SEQ] for h in heads}
                    dve.wait_ge(pre["gaps"], 1)
                    for h in heads:
                        near_steps.note(dve.tensor_scalar(dst[h], dist, 0.0, table[:, h:h + 1], ALU.mult, ALU.add))
                    near_steps.settle(dve)
                    for j, start in enumerate(bucket_starts()):
                        near_steps.run(dve, dve.tensor_scalar(reached, dist, start, None, ALU.is_ge))
                        for h in heads:
                            near_steps.note(dve.scalar_tensor_tensor(dst[h], reached, steps_t[:, j * DIFF_H + h:j * DIFF_H + h + 1], dst[h],
                                                                     ALU.mult, ALU.add))
                        near_steps.settle(dve)
                    for h in heads:
                        dve.tensor_tensor(dst[h], dst[h], hidden, ALU.add).then_inc(pre["near"], 1)
                with dve.Else():
                    dve.nop()
                dve.nop()

            def scale_x(b, n):
                pace.part(0.3)
                dve.wait_ge(squared, 3 * b + n + 1)
                run(dve.tensor_scalar(small[:, 4:5], small[:, n:n + 1], 1.0 / D, EPS, ALU.mult, ALU.add))
                rsqrt(small[:, 5:6], small[:, 4:5], small[:, 6:7])
                if n == 0:
                    dve.tensor_scalar(xs[:, :], x_in[:, :], small[:, 5:6], None, ALU.mult).then_inc(scaled, 1)
                    dve.tensor_copy(x_next[:, :], x_in[:, :]).then_inc(x_copied, 1)
                else:
                    dve.tensor_scalar(xs[:, :], x_next[:, :], small[:, 5:6], None, ALU.mult).then_inc(scaled, 1)

            def norm(b, n, gain):
                if n or not isinstance(b, int):
                    scale_x(b, n)
                pace.part(0.7)
                for g in range(2):
                    dve.wait_ge(turned, 6 * b + 2 * n + g + 1)
                    dve.tensor_tensor(hT[:, 4 * g:4 * g + 4, :], ps_t[g][:, :].rearrange("p (a t) -> p a t", a=4),
                                      bc(col(gain, 4 * g, 4).unsqueeze(2), [P, 4, P]), ALU.mult).then_inc(hT_made, 1)
                if isinstance(b, int) and n == 0:
                    near_biases(range(VECTOR_HEADS - 1, VECTOR_HEADS))

            def latents(b):
                dve.wait_ge(proj_out[0], b + 1)
                dve.tensor_tensor(pT[:, 0:3, :], latent, latent, ALU.mult).then_inc(lat_sq, 1)
                pace.part(0.7)
                dve.wait_ge(lat_sum, b + 1)
                steps.note(dve.tensor_scalar(pT[:, 3, :], ps_t[0][:, 0:P], 1.0 / Q_RANK, EPS, ALU.mult, ALU.add))
                run(dve.tensor_scalar(pT[:, 4, :], ps_t[0][:, P:2 * P], 1.0 / KV_RANK, EPS, ALU.mult, ALU.add))
                flat = pT[:, :, :].rearrange("p a t -> p (a t)")
                rsqrt(flat[:, 5 * P:7 * P], flat[:, 3 * P:5 * P], flat[:, 0:2 * P])
                dve.scalar_tensor_tensor(latent_n[:, 0, :], latent[:, 0, :], col("qn", 0), pT[:, 5, :], ALU.mult, ALU.mult)
                dve.scalar_tensor_tensor(latent_n[0:64, 1, :], latent[0:64, 1, :], col("qn", 1)[0:64, :], pT[0:64, 5, :],
                                         ALU.mult, ALU.mult)
                dve.scalar_tensor_tensor(latent_n[:, 2, :], latent[:, 2, :], col("kvn"), pT[:, 6, :], ALU.mult, ALU.mult)\
                   .then_inc(lat_n, 1)

            def mla_up(b):
                rr = slice(NOPE, NOPE + ROPE)
                dve.wait_ge(rope_landed, 16 * b + 16)
                steps.note(dve.tensor_tensor(pT[rr, 3, :], latent[rr, 1, :], rope_t[rr, 0, :], ALU.mult))
                run(dve.tensor_tensor(pT[rr, 4, :], k_swap[rr, :], rope_t[rr, 1, :], ALU.mult))
                dve.tensor_tensor(k_mla[rr, :, bass.ds(b * P, P)], bc(pT[rr, 3:4, :], [ROPE, MLA_H, P]),
                                  bc(pT[rr, 4:5, :], [ROPE, MLA_H, P]), ALU.add).then_inc(k_rope, 1)
                cos, sin = (bc(rope_t[rr, c:c + 1, :], [ROPE, MLA_H, P]) for c in range(2))
                straight = e1[rr, 512:1024].rearrange("p (a t) -> p a t", a=MLA_H)
                swapped = e1[rr, 0:512].rearrange("p (a t) -> p a t", a=MLA_H)
                dve.wait_ge(up_q, b + 1)
                steps.note(dve.scalar_tensor_tensor(straight, ps_p[1][rr, :].rearrange("p (a t) -> p a t", a=MLA_H), MLA_SCALE, cos,
                                                    ALU.mult, ALU.mult))
                dve.wait_ge(q_swap, b + 1)
                run(dve.scalar_tensor_tensor(swapped, swapped, MLA_SCALE, sin, ALU.mult, ALU.mult))
                dve.tensor_tensor(q_mla[rr, :, :], straight, swapped, ALU.add).then_inc(q_rope, 1)

            def conv(b):
                dve.wait_ge(proj_out[2], b + 1)
                for i in range(LT):
                    steps.note(dve.tensor_scalar(lru_x[:, i, :], conv_in[:, i, 0:P], col("conv_w", i), col("conv_b", i),
                                                 ALU.mult, ALU.add))
                for k in range(1, CONV_W):
                    steps.settle(dve)
                    for i in range(LT):
                        steps.note(dve.scalar_tensor_tensor(lru_x[:, i, :], conv_in[:, i, k:k + P], col("conv_w", k * LT + i),
                                                            lru_x[:, i, :], ALU.mult, ALU.add))
                dve.tensor_copy(conv_in[:, :, 0:CONV_W - 1], conv_in[:, :, P:P + CONV_W - 1]).then_inc(conv_done, 1)

            def gates(b):
                pace.part(0.1)
                dve.wait_ge(gate_out, 2 * b + 2)
                run(dve.scalar_tensor_tensor(lru_i, lru_i, 1.0, lru_x, ALU.add, ALU.mult))
                pace.part(0.3)
                dve.wait_ge(decay_out, b + 1)
                run(dve.tensor_tensor(lru_x, lru_a, lru_a, ALU.mult))
                dve.scalar_tensor_tensor(lru_t, lru_x, 1.0, lru_t, ALU.add, ALU.mult).then_inc(root_in, 1)
                pace.part(0.7)
                dve.wait_ge(root_out, b + 1)
                run(dve.scalar_tensor_tensor(lru_i, lru_i, 0.5, lru_t, ALU.mult, ALU.mult))
                for i in range(LT):
                    steps.note(dve.tensor_tensor_scan(lru_x[:, i, :], lru_a[:, i, :], lru_i[:, i, :], h_last[:, i:i + 1],
                                                      ALU.mult, ALU.add))
                steps.settle(dve)
                steps.note(dve.tensor_copy(h_last[:, :], lru_x[:, :, P - 1]))
                dve.wait_ge(proj_out[3], b + 1)
                run(dve.tensor_tensor(lru_i, lru_x, gelu_g, ALU.mult))
                dve.tensor_tensor(lru_t, lru_i, lru_i, ALU.mult).then_inc(lru_sq, 1)

            def recur(b):
                pace.part(0.8)
                dve.wait_ge(lru_sum, b + 1)
                run(dve.tensor_scalar(lru_a[:, 0, :], ps_t[0][:, 0:P], 1.0 / LRU_W, EPS, ALU.mult, ALU.add))
                rsqrt(lru_a[:, 1, :], lru_a[:, 0, :], lru_a[:, 2, :])
                for i in range(LT):
                    ins = dve.scalar_tensor_tensor(hT[:, 2 + i, :], lru_i[:, i, :], col("yn", 2 + i), lru_a[:, 1, :], ALU.mult, ALU.mult)
                ins.then_inc(lru_done, 1)
                dve.wait_ge(lru_done, b + 1)

            def masked_max(b, n, buf, bias):
                wait_more(dve, s_ps, scores_waited, 1)
                keys_n = key_tiles(b) * P
                run(dve.tensor_tensor_reduce(buf[:, 0:keys_n], ps_s[:, 0:keys_n], bias[:, 0:keys_n], 1.0, -3.0e38, ALU.add, ALU.max,
                                             small[:, 16 + n:17 + n]))
                dve.tensor_scalar(small[:, 32 + n:33 + n], small[:, 16 + n:17 + n], -1.0, None, ALU.mult).then_inc(s_max, 1)

            def mla(b, h):
                if h == 0:
                    dve.wait_ge(bias_landed[0], 48 * b + 16)
                for n in ((0, 1), (2,), (3,), ())[h]:
                    if n >= 2:
                        dve.wait_ge(p_turned, 16 * b + 2 * (n - 1))
                    masked_max(b, n, (e0, e1)[n % 2], bias_t[:, 0, :])
                if h == MLA_H - 2:
                    dve.nop().then_inc(bias_used, 1)

            def diff(b, h):
                dve.wait_ge(bias_landed[(h + 1) % 2], (32, 48)[h % 2] * b + 16 * ((h + 1) // 2 + 1))
                bias = bias_t[:, (h + 1) % 2, :]
                dve.wait_ge(p_turned, 16 * b + (2 * (4 + h) if h else 2 * 3))
                masked_max(b, 4 + 2 * h, e0, bias)
                pace.part(0.2)
                if h == 0:
                    dve.wait_ge(p_turned, 16 * b + 2 * 4)
                masked_max(b, 5 + 2 * h, e1, bias)
                dve.nop().then_inc(bias_used, 1)
                pace.part(0.45)
                dve.wait_ge(s_exp, 12 * b + 6 + 2 * h)
                run(dve.reciprocal(small[:, 72:74], small[:, 52 + 2 * h:54 + 2 * h]))
                run(dve.tensor_scalar(small[:, 74:75], small[:, 73:74], lam_t[:, 5:6], None, ALU.mult))
                keys_n = key_tiles(b) * P
                run(dve.tensor_scalar(e1[:, 0:keys_n], e1[:, 0:keys_n], small[:, 74:75], None, ALU.mult))
                dve.scalar_tensor_tensor(e0[:, 0:keys_n], e0[:, 0:keys_n], small[:, 72:73], e1[:, 0:keys_n], ALU.mult, ALU.add)\
                   .then_inc(w_done, 1)

            def join(b):
                dve.wait_ge(pv_ps, 8 * b + 8)
                run(dve.reciprocal(small[:, 76:80], small[:, 48:52]))
                for h in range(MLA_H):
                    steps.note(dve.tensor_scalar(xs[:, h * MLA_V:(h + 1) * MLA_V], ps_p[0][:, h * MLA_V:(h + 1) * MLA_V],
                                                 small[:, 76 + h:77 + h], None, ALU.mult))
                run(dve.tensor_copy(xs[:, 512:768], ps_p[1][:, 0:256]))
                steps.note(dve.tensor_tensor_reduce(xs[:, 256:512], xs[:, 0:256], xs[:, 0:256], 1.0, 0.0, ALU.mult, ALU.add,
                                                    small[:, 84:85]))
                run(dve.tensor_tensor(xs[:, 768:1024], xs[:, 512:768], xs[:, 512:768], ALU.mult))
                run(dve.tensor_reduce(small[:, 85:89], xs[:, 768:1024].rearrange("p (h c) -> p h c", h=DIFF_H), AX_X, ALU.add))
                steps.note(dve.tensor_scalar(small[:, 90:91], small[:, 84:85], 1.0 / (MLA_H * MLA_V), EPS, ALU.mult, ALU.add))
                run(dve.tensor_scalar(small[:, 91:95], small[:, 85:89], 1.0 / DV, EPS, ALU.mult, ALU.add))
                rsqrt(small[:, 95:100], small[:, 90:95], small[:, 100:105])
                dve.tensor_scalar(xs[:, 0:256], xs[:, 0:256], small[:, 95:96], None, ALU.mult)
                o = xs[:, 512:768].rearrange("p (h c) -> p h c", h=DIFF_H)
                dve.tensor_tensor(o, o, bc(small[:, 96:100].unsqueeze(2), [P, DIFF_H, DV]), ALU.mult).then_inc(y_made, 1)
                pace.part(0.9)
                dve.wait_ge(y_turned, b + 1)
                t = ps_t[0][:, :].rearrange("p (a t) -> p a t", a=4)
                dve.tensor_tensor(hT[:, 0:2, :], t[:, 0:2, :], bc(col("yn", 0, 2).unsqueeze(2), [P, 2, P]), ALU.mult)
                dve.scalar_tensor_tensor(hT[:, 6:8, :], t[:, 2:4, :], 1.0 - LAM_INIT, bc(col("yn", 6, 2).unsqueeze(2), [P, 2, P]),
                                         ALU.mult, ALU.mult).then_inc(yT_made, 1)

            def add_out(b, first):
                for n in range(2):
                    pace.part((n + 1) / 2)
                    dve.wait_ge(w_used, products(b, first + KT * (n + 1)))
                    dve.tensor_tensor(x_next[:, n * 512:(n + 1) * 512], x_next[:, n * 512:(n + 1) * 512],
                                      ps_s[:, n * 512:(n + 1) * 512], ALU.add).then_inc(out_added, 1)

            def cross_scores(b):
                dve.wait_ge(c_ps, b + 1)
                run(dve.tensor_reduce(small[:, 60:64], ps_s[:, :].rearrange("p (h m) -> p h m", h=CROSS_H), AX_X, ALU.max))
                dve.tensor_scalar(small[:, 64:68], small[:, 60:64], -1.0, None, ALU.mult).then_inc(c_max, 1)

            def cross_mix(b):
                pace.part(0.1)
                dve.wait_ge(c_exp, b + 1)
                run(dve.reciprocal(small[:, 80:84], small[:, 68:72]))
                for h in range(CROSS_H):
                    ins = dve.tensor_scalar(e0[:, h * MEM:(h + 1) * MEM], e0[:, h * MEM:(h + 1) * MEM], small[:, 80 + h:81 + h], None,
                                            ALU.mult)
                ins.then_inc(c_norm, 1)

            def top16(values, indices, sources, share0, share1):
                n = len(sources)
                for first in (0, 8):
                    def part(stage, k):
                        pace.part(share0 + (share1 - share0) * ((first / 8) + (stage + k / n) / 2) / 2)

                    for k, (v, s) in enumerate(zip(values, sources)):
                        part(0, k)
                        dve.max(v[:, first:first + 8], s).then_inc(top_step, 1)
                    part(1, 0)
                    wait_more(dve, top_step, top_waited, n)
                    for k, (v, i, s) in enumerate(zip(values, indices, sources)):
                        part(1, k)
                        dve.max_index(i[:, first:first + 8], v[:, first:first + 8], s).then_inc(top_step, 1)
                        if first == 0:
                            dve.match_replace(s, v[:, 0:8], s, -3.0e38).then_inc(top_step, 1)
                    wait_more(dve, top_step, top_waited, 2 * n if first == 0 else n)

            def top(b, g):
                pace.part(0.2)
                wait_more(dve, k_out, keys_waited, 1)
                at = range(8 * g, 8 * g + 8)
                top16([top_v[:, a, :] for a in at], [top_i[:, a, :] for a in at],
                      [(e0, e1)[g][:, k * NKEYS:(k + 1) * NKEYS] for k in range(8)], 0.2, 1.0)

            def choose(b, g):
                hs = slice(4 * g, 4 * g + 4)
                e = (e0, e1)[g]
                pairs = e[:, :].rearrange("p (h i j) -> p h i j", h=4, i=TOPK)
                wide_shape = [P, 4, TOPK, TOPK]
                tv = top_v[:, :, :].rearrange("p (h c) k -> p h c k", c=2)
                tf = top_f[:, :, :].rearrange("p (h c) k -> p h c k", c=2)
                steps.note(dve.tensor_copy(top_f[:, 8 * g:8 * g + 8, :], top_i[:, 8 * g:8 * g + 8, :]))
                dve.tensor_tensor(pairs, bc(tv[:, hs, 0, :].unsqueeze(3), wide_shape), bc(tv[:, hs, 1, :].unsqueeze(2), wide_shape),
                                  ALU.add).then_inc(top_step, 1)
                wait_more(dve, top_step, top_waited, 1)
                top16([best_v[:, h, :] for h in range(4 * g, 4 * g + 4)], [best_i[:, h, :] for h in range(4 * g, 4 * g + 4)],
                      [e[:, h * 256:(h + 1) * 256] for h in range(4)], 0.05, 0.5)
                g3 = g_next[:, :].rearrange("p (h k) -> p h k", h=HEADS)
                if g:
                    dve.tensor_tensor(g3, best_v[:, :, :], bc(best_v[:, :, 0:1], [P, HEADS, TOPK]), ALU.subtract).then_inc(g_arg, 1)
                c4 = slice(4 * TOPK * g, 4 * TOPK * (g + 1))
                flat_i = best_i[:, :, :].rearrange("p h k -> p (h k)")[:, c4]
                steps.note(dve.tensor_scalar(pick_i[:, 0, c4], flat_i, 4, None, ALU.logical_shift_right))
                run(dve.tensor_scalar(pick_i[:, 1, c4], flat_i, TOPK - 1, None, ALU.bitwise_and))
                run(dve.tensor_copy(pick[:, 0:2, c4], pick_i[:, :, c4]))
                for c in range(2):
                    pace.part(0.5 + 0.25 * c)
                    place = pick[:, c, c4].rearrange("p (h k) -> p h k", h=4)
                    found = pick[:, 2 + c, c4].rearrange("p (h k) -> p h k", h=4)
                    run(dve.tensor_tensor(pairs, bc(place.unsqueeze(3), wide_shape),
                                          bc(iota_f[:, :].unsqueeze(1).unsqueeze(1), wide_shape), ALU.is_equal))
                    pace.part(0.58 + 0.25 * c)
                    run(dve.tensor_tensor(pairs, pairs, bc(tf[:, hs, c, :].unsqueeze(2), wide_shape), ALU.mult))
                    pace.part(0.66 + 0.25 * c)
                    run(dve.tensor_reduce(found, pairs, AX_X, ALU.add))
                run(dve.scalar_tensor_tensor(ids_next[:, c4], pick[:, 2, c4], float(NKEYS), pick[:, 3, c4], ALU.mult, ALU.add))
                if g == 0:
                    hand_first_ids(b)
                    return
                dve.wait_ge(g_exp, b + 1)
                run(dve.tensor_reduce(small[:, 106:106 + HEADS], g3, AX_X, ALU.add))
                run(dve.reciprocal(small[:, 114:114 + HEADS], small[:, 106:106 + HEADS]))
                run(dve.tensor_tensor(g3, g3, bc(small[:, 114:114 + HEADS].unsqueeze(2), [P, HEADS, TOPK]), ALU.mult))

            def hand_first_ids(b):
                dve.tensor_copy(ids_u[:, 0:FIRST], ids_next[:, 0:FIRST]).then_inc(ids_handed, 1)

            def hand_ids(b):
                if isinstance(b, int):
                    dve.wait_ge(pre["rope_stored"], 32)
                dve.wait_ge(u_used, b * EXPERTS + G_RING)
                dve.tensor_copy(ids_u[:, FIRST:], ids_next[:, FIRST:]).then_inc(ids_handed, 1)
                dve.tensor_tensor(h_cur[:, :], xs[:, :], ffn_row[:, :], ALU.mult).then_inc(handed, 1)
                dve.wait_ge(handed, b + 1)

            def hand_over(b):
                dve.wait_ge(v_used, b * SUM_ROWS + SUM_SLOTS)
                dve.tensor_copy(ids_v[:, :], ids_next[:, :]).then_inc(v_ids_handed, 1)
                ge(dve, coef_made, b * STEPS)
                steps.note(dve.tensor_copy(g_cur[:, :], g_next[:, :]))
                ge(dve, fin_stored, 16 * b)
                dve.tensor_copy(x_cur[:, :], x_next[:, :]).then_inc(x_handed, 1)
                dve.wait_ge(x_handed, b + 1)
                dve.wait_ge(v_ids_handed, b + 1)
                steps.settle(dve)

            front = {
                "norm_mix": lambda b: norm(b, 0, "mix"), "latents": latents, "mla_up": mla_up, "conv": conv, "gates": gates,
                "recur": recur, "join": join, "mix_out": lambda b: add_out(b, 34), "norm_cross": lambda b: norm(b, 1, "cross"),
                "cross_scores": cross_scores, "cross_mix": cross_mix, "cross_out": lambda b: add_out(b, 66),
                "norm_ffn": lambda b: norm(b, 2, "ffn"), "top_0": lambda b: top(b, 0), "top_1": lambda b: top(b, 1),
                "choose_0": lambda b: choose(b, 0), "choose_1": lambda b: choose(b, 1),
            }
            for h in range(4):
                front[f"mla_{h}"] = lambda b, h=h: mla(b, h)
                front[f"diff_{h}"] = lambda b, h=h: diff(b, h)

            def multiply_row(bp, p):
                dve.wait_ge(u_landed[p % G_RING], bp * (16 * EXPERTS // G_RING) + 16 * (p // G_RING + 1))
                row = u_rows[:, p % G_RING, :]
                dve.tensor_tensor_reduce(row, row, h_cur[:, :], 1.0, 0.0, ALU.mult, ALU.add, dots[:, p:p + 1]).then_inc(u_used, 1)

            def position(bp, p):
                if EARLY <= p < EXPERTS:
                    multiply_row(bp, p)
                if EXPERTS <= p < EXPERTS + EARLY and not isinstance(bp, int):
                    multiply_row(bp + 1, p - EXPERTS)
                j = p - SUM_LAG
                if j >= 0 and on_vector(j):
                    dve.wait_ge(v_landed[j % G_RING], bp * (16 * EXPERTS // G_RING) + 16 * (j // G_RING + 1))
                    dve.wait_ge(v_added, bp * (EXPERTS // SHARE) + (j + G_RING) // SHARE)
                    dve.wait_ge(coef_made, bp * STEPS + (j // STEP + 1))
                    dve.scalar_tensor_tensor(x_cur[:, :], v_rows[:, j % G_RING, :], coef[:, j:j + 1], x_cur[:, :], ALU.mult, ALU.add)\
                       .then_inc(v_added, 1)
                done = p - GATE_LAG
                if done >= STEP and done % STEP == 0 and done <= EXPERTS:
                    s = done // STEP - 1
                    dve.wait_ge(acts_made, bp * STEPS + s + 1)
                    a = slice(s * STEP, (s + 1) * STEP)
                    dve.tensor_tensor(coef[:, a], g_cur[:, a], acts[:, a], ALU.mult).then_inc(coef_made, 1)

            def finish(bp):
                dve.wait_ge(v_used, bp * SUM_ROWS + (SUM_ROWS + SUM_SLOTS))
                dve.wait_ge(v_added, bp * (EXPERTS // SHARE) + (EXPERTS + G_RING) // SHARE)
                dve.tensor_tensor(x_cur[:, :], x_cur[:, :], ps_sum[:, :], ALU.add).then_inc(fin_sum, 1)
                dve.wait_ge(fin_sq, bp + 1)
                run(dve.tensor_scalar(out_stat[:, 1:2], out_stat[:, 0:1], 1.0 / D, EPS, ALU.mult, ALU.add))
                rsqrt(out_stat[:, 2:3], out_stat[:, 1:2], out_stat[:, 3:4])
                dve.wait_ge(gain_landed, 16 * bp + (0 if isinstance(bp, int) else 16))
                dve.scalar_tensor_tensor(x_cur[:, :], x_cur[:, :], out_stat[:, 2:3], e1[:, :], ALU.mult, ALU.mult)\
                   .then_inc(fin_made, 1)

            dve.wait_ge(consts_in, 80)
            dve.wait_ge(consts_made, 9)
            dve.nop().then_inc(u_used, G_RING)
            dve.nop().then_inc(v_added, G_RING // SHARE)
            pace = Pace(position)
            scale_steps = -steps.n
            scale_x(0, 0)
            scale_steps += steps.n
            near_biases(range(VECTOR_HEADS - 1))
            prologue_steps = steps.n - scale_steps
            pace.run(front, 0)
            hand_ids(0)
            for p in range(EARLY):
                multiply_row(0, p)
            hand_over(0)
            first_steps = steps.n - prologue_steps
            finish_steps = 12
            for first, last, wide[0] in LOOPS:
                with dve.Fori(first, last) as b:
                    steps.start(b * (first_steps + finish_steps) + (prologue_steps - finish_steps))
                    pace.start(b - 1)
                    pace.run(front, b)
                    hand_ids(b)
                    pace.to(END)
                    finish(b - 1)
                    hand_over(b)
                    assert steps.n == first_steps + finish_steps, (steps.n, first_steps)
            pace.start(NB - 1)
            steps.start(prologue_steps + NB * first_steps + (NB - 1) * finish_steps)
            pace.to(END)
            finish(NB - 1)


def kernel(x, mem, positions, rel_bias, norm_mix, w_in, mla_q_norm, mla_w_uq, mla_kv_norm, mla_w_ukv, lru_conv_w, lru_conv_b,
           lru_w_a, lru_b_a, lru_w_x, lru_b_x, lru_lambda, diff_lambda, diff_norm, out_norm_mla, out_norm_lru, w_out,
           norm_cross, norm_mem, w_cq, w_ckv, w_co, norm_ffn, peer_w_q, peer_keys, peer_u, peer_v, norm_final):
    import concourse.bacc as bacc
    from concourse.bass_utils import run_bass_kernel_spmd

    A = np.asarray

    def column_slices(w):
        n = w.shape[1] // P
        return w.reshape(2, 4, P, n, P).transpose(3, 0, 2, 1, 4).reshape(2 * n, P, HALF)

    def row_slices(w):
        return w.reshape(KT, P, 2, HALF).transpose(2, 0, 1, 3).reshape(2 * KT, P, HALF)

    def swapped(w):
        return np.concatenate([w[..., ROPE // 2:], w[..., :ROPE // 2]], axis=-1)

    w = A(w_in)[0]
    at = np.cumsum([0, Q_RANK, KV_RANK, ROPE, LRU_W, LRU_W, 256, 256, 256])
    c_q, c_kv, k_r, x_l, g_l, q_d, k_d, v_d = (w[:, at[i]:at[i + 1]] for i in range(8))
    w_in_own = np.concatenate([c_q, k_r, swapped(k_r), c_kv, q_d, k_d, x_l, g_l, v_d], axis=1)
    ckv = A(w_ckv)[0]
    wstream = np.concatenate([column_slices(ckv[:, :D]), row_slices(ckv[:, D:]), column_slices(w_in_own), row_slices(A(w_out)[0]),
                              column_slices(A(w_cq)[0]), row_slices(A(w_co)[0]), column_slices(A(peer_w_q)[0])])

    columns = np.zeros((P, N_COLS), np.float32)

    def put(name, a, rows=P):
        a = A(a).reshape(-1, rows).T
        columns[0:rows, COL[name]:COL[name] + a.shape[1]] = a

    for name, a in (("mix", norm_mix), ("cross", norm_cross), ("mem", norm_mem), ("ffn", norm_ffn), ("kvn", mla_kv_norm),
                    ("conv_w", lru_conv_w), ("conv_b", lru_conv_b), ("lam", lru_lambda)):
        put(name, a)
    columns[:, COL["qn"]] = A(mla_q_norm)[0, 0:P]
    columns[0:Q_RANK - P, COL["qn"] + 1] = A(mla_q_norm)[0, P:]
    dn = A(diff_norm)[0]
    put("yn", np.concatenate([A(out_norm_mla)[0], A(out_norm_lru)[0], dn, dn, dn, dn]))
    put("gate_b", np.concatenate([A(lru_b_a).reshape(-1), A(lru_b_x).reshape(-1)]))
    freq = np.float32(ROPE_THETA) ** (-np.arange(0, ROPE, 2, dtype=np.float32) / np.float32(ROPE))
    columns[NOPE:NOPE + ROPE, COL["freq"]] = np.concatenate([freq, freq])
    columns[NOPE:NOPE + ROPE, COL["sign"]] = np.repeat(np.float32([-1, 1]), ROPE // 2)

    uq = A(mla_w_uq)[0].reshape(Q_RANK, MLA_H, NOPE + ROPE)
    uq = np.concatenate([uq, swapped(uq[:, :, NOPE:])], axis=2).reshape(Q_RANK, MLA_H * P)
    w_uq = np.zeros((P, 2, MLA_H * P), np.float32)
    w_uq[:, 0] = uq[0:P]
    w_uq[0:Q_RANK - P, 1] = uq[P:]
    ukv = A(mla_w_ukv)[0].reshape(KV_RANK, MLA_H, 2, NOPE)
    w_ukv = ukv.transpose(0, 2, 1, 3).reshape(KV_RANK, 2, MLA_H * NOPE)
    w_gates = np.zeros((P, 2, LT, P), np.float32)
    for a, g in enumerate((A(lru_w_a)[0], A(lru_w_x)[0])):
        for i in range(LRU_W // LRU_G):
            r = (i % 2) * LRU_G
            w_gates[r:r + LRU_G, a, i // 2, r:r + LRU_G] = g[i]
    pk = A(peer_keys)[0]
    keys_t = np.zeros((P, 2 * NKEYS), np.float32)
    keys_t[0:64, 0:NKEYS] = pk[0].T
    keys_t[64:128, NKEYS:] = pk[1].T

    ins = {
        "x": A(x)[0], "wstream": wstream, "columns": columns, "w_uq": w_uq, "w_ukv": w_ukv, "w_gates": w_gates, "keys_t": keys_t,
        "ffn_gain": A(norm_ffn)[0], "final_gain": A(norm_final), "mem": A(mem)[0], "positions": A(positions)[0],
        "pos_cols": A(positions)[0].reshape(NB, P).T,
        "rel_bias": A(rel_bias).reshape(-1), "diff_lambda": A(diff_lambda)[0].reshape(-1), "peer_u": A(peer_u)[0],
        "peer_v": A(peer_v)[0],
    }
    ins = {k: np.ascontiguousarray(v) for k, v in ins.items()}
    nc = bacc.Bacc("TRN2", target_bir_lowering=False, num_devices=1)
    aps = {k: nc.dram_tensor("in_" + k, v.shape, mybir.dt.from_np(v.dtype), kind="ExternalInput").ap() for k, v in ins.items()}
    out = nc.dram_tensor("out", (SEQ, D), F32, kind="ExternalOutput").ap()
    program(nc, *aps.values(), out)
    r = run_bass_kernel_spmd(nc, [{"in_" + k: v for k, v in ins.items()}], core_ids=[0])
    return r.results[0]["out"].reshape(1, SEQ, D)
```
